# Optimizing a Trainium2 kernel written in Bass

```python
import math, functools
import jax, jax.numpy as jnp
from jax import lax
import numpy as np

D_MODEL = 1024
BATCH = 1
SEQ = 256
DEPTH = 2

HEAD_DIM = 64
ROPE_THETA = 500000.0
ROPE_DIM = HEAD_DIM // 4
Q_BLOCK = 128
NORM_EPS = 1e-5
D_FF = -(-8 * D_MODEL // (3 * 256)) * 256

MOBA_HEADS = 8
MOBA_BLOCK = 256
MOBA_TOPK = 3
MOBA_Q = 64
DIFF_HEADS = 4
DIFF_V = 2 * HEAD_DIM
NSA_HEADS = 8
NSA_GROUPS = 2
NSA_CMP_LEN = 32
NSA_CMP_STRIDE = 16
NSA_CMP_HIDDEN = 256
NSA_SEL_BLOCK = 64
NSA_SEL_TOPK = 16
NSA_WINDOW = 512
NSA_FORCE_BONUS = 1e3
MLA_HEADS = 8
MLA_Q_RANK = 256
MLA_KV_RANK = 128
MLA_NOPE = 64
MLA_ROPE = 32
MLA_V = 64

EV_SIZES = [MOBA_HEADS * HEAD_DIM] * 3 + [DIFF_HEADS * 2 * HEAD_DIM] * 2 + [DIFF_HEADS * DIFF_V]
EV_IN = sum(EV_SIZES)
EV_OUT = MOBA_HEADS * HEAD_DIM + DIFF_HEADS * DIFF_V
OD_SIZES = ([NSA_HEADS * HEAD_DIM] + [NSA_GROUPS * HEAD_DIM] * 6 + [NSA_HEADS * 3]
            + [MLA_Q_RANK, MLA_KV_RANK, MLA_ROPE])
OD_IN = sum(OD_SIZES)
OD_OUT = NSA_HEADS * HEAD_DIM + MLA_HEADS * MLA_V

kernel_name = "hybrid_moba_diff_nsa_mla_trunk"

def rmsnorm(x, g):
    xf = x.astype(jnp.float32)
    y = xf * lax.rsqrt(jnp.mean(xf * xf, axis=-1, keepdims=True) + NORM_EPS)
    return (y * g.astype(jnp.float32)).astype(x.dtype)

def rope_tables(positions, dim):
    inv = 1.0 / (ROPE_THETA ** (jnp.arange(0, dim, 2, dtype=jnp.float32) / dim))
    ang = positions.astype(jnp.float32)[..., None] * inv
    return jnp.cos(ang), jnp.sin(ang)

def apply_rope(x, cos, sin):
    r = cos.shape[-1]
    cos, sin = cos.astype(x.dtype), sin.astype(x.dtype)
    x1, x2, xp = x[..., :r], x[..., r:2 * r], x[..., 2 * r:]
    return jnp.concatenate([x1 * cos - x2 * sin, x2 * cos + x1 * sin, xp], axis=-1)

def masked_softmax(s, mask):
    s = jnp.where(mask, s.astype(jnp.float32), -1e30)
    m = jnp.max(s, axis=-1, keepdims=True)
    e = jnp.where(mask, jnp.exp(s - m), 0.0)
    return e / jnp.maximum(jnp.sum(e, axis=-1, keepdims=True), 1e-30)

def split_cols(x, sizes):
    return jnp.split(x, [int(i) for i in np.cumsum(sizes)[:-1]], axis=-1)

def heads(x, n):
    B, S, _ = x.shape
    return x.reshape(B, S, n, -1).transpose(0, 2, 1, 3)

def merge_heads(o):
    B, n, S, d = o.shape
    return o.transpose(0, 2, 1, 3).reshape(B, S, n * d)

def causal_attention(q, k, v, scale):
    B, H, S, _ = q.shape
    kpos = jnp.arange(S)

    def chunk(c):
        q0 = c * Q_BLOCK
        qc = lax.dynamic_slice_in_dim(q, q0, Q_BLOCK, axis=2)
        tq = q0 + jnp.arange(Q_BLOCK)
        p = masked_softmax(jnp.einsum('bhqd,bhkd->bhqk', qc, k) * scale, kpos[None, :] <= tq[:, None])
        return jnp.einsum('bhqk,bhkd->bhqd', p.astype(v.dtype), v)

    o = lax.map(chunk, jnp.arange(S // Q_BLOCK))
    return o.transpose(1, 2, 0, 3, 4).reshape(B, H, S, v.shape[-1])

def moba_attention(q, k, v):
    B, H, S, d = q.shape
    Sp = -(-S // MOBA_BLOCK) * MOBA_BLOCK
    pad = ((0, 0), (0, 0), (0, Sp - S), (0, 0))
    q, k, v = jnp.pad(q, pad), jnp.pad(k, pad), jnp.pad(v, pad)
    nb = Sp // MOBA_BLOCK
    topk = min(MOBA_TOPK, nb)
    kb = k.reshape(B, H, nb, MOBA_BLOCK, d)
    vb = v.reshape(B, H, nb, MOBA_BLOCK, d)
    kmean = jnp.mean(kb.astype(jnp.float32), axis=3).astype(k.dtype)
    scale = d ** -0.5
    bi = jnp.arange(B)[:, None, None, None]
    hi = jnp.arange(H)[None, :, None, None]
    blk = jnp.arange(nb)

    def chunk(c):
        q0 = c * MOBA_Q
        qc = lax.dynamic_slice_in_dim(q, q0, MOBA_Q, axis=2)
        tq = q0 + jnp.arange(MOBA_Q)
        own = q0 // MOBA_BLOCK
        gate = jnp.einsum('bhqd,bhnd->bhqn', qc, kmean).astype(jnp.float32)
        gate = jnp.where(blk < own, gate, -jnp.inf)
        gval, sel = lax.top_k(gate, topk)
        ok = jnp.isfinite(gval)
        ks = kb[bi, hi, sel]
        vs = vb[bi, hi, sel]
        s_sel = (jnp.einsum('bhqd,bhqkjd->bhqkj', qc, ks) * scale).reshape(B, H, MOBA_Q, topk * MOBA_BLOCK)
        m_sel = jnp.broadcast_to(ok[..., None], (B, H, MOBA_Q, topk, MOBA_BLOCK)).reshape(B, H, MOBA_Q, topk * MOBA_BLOCK)
        ko = lax.dynamic_slice_in_dim(k, own * MOBA_BLOCK, MOBA_BLOCK, axis=2)
        vo = lax.dynamic_slice_in_dim(v, own * MOBA_BLOCK, MOBA_BLOCK, axis=2)
        s_own = jnp.einsum('bhqd,bhjd->bhqj', qc, ko) * scale
        m_own = (own * MOBA_BLOCK + jnp.arange(MOBA_BLOCK))[None, :] <= tq[:, None]
        m_own = jnp.broadcast_to(m_own, (B, H, MOBA_Q, MOBA_BLOCK))
        p = masked_softmax(jnp.concatenate([s_sel, s_own], -1), jnp.concatenate([m_sel, m_own], -1)).astype(v.dtype)
        p_sel = p[..., :topk * MOBA_BLOCK].reshape(B, H, MOBA_Q, topk, MOBA_BLOCK)
        return (jnp.einsum('bhqkj,bhqkjd->bhqd', p_sel, vs)
                + jnp.einsum('bhqj,bhjd->bhqd', p[..., topk * MOBA_BLOCK:], vo))

    out = lax.map(chunk, jnp.arange(Sp // MOBA_Q))
    return out.transpose(1, 2, 0, 3, 4).reshape(B, H, Sp, d)[:, :, :S]

def diff_attention(q, k, v, lam, lambda_init, subln_g):
    B, H, _, S, d = q.shape
    scale = d ** -0.5
    kpos = jnp.arange(S)

    def chunk(c):
        q0 = c * Q_BLOCK
        qc = lax.dynamic_slice_in_dim(q, q0, Q_BLOCK, axis=3)
        tq = q0 + jnp.arange(Q_BLOCK)
        p = masked_softmax(jnp.einsum('bhmqd,bhmkd->bhmqk', qc, k) * scale, kpos[None, :] <= tq[:, None])
        attn = (p[:, :, 0] - lam * p[:, :, 1]).astype(v.dtype)
        return jnp.einsum('bhqk,bhkd->bhqd', attn, v)

    o = lax.map(chunk, jnp.arange(S // Q_BLOCK))
    o = o.transpose(1, 2, 0, 3, 4).reshape(B, H, S, v.shape[-1])
    return rmsnorm(o, subln_g) * (1.0 - lambda_init)

def nsa_compress(x, pe, w1, w2):
    B, G, S, d = x.shape
    xh = x.reshape(B, G, S // NSA_CMP_STRIDE, NSA_CMP_STRIDE, d)
    blocks = jnp.concatenate([xh[:, :, :-1], xh[:, :, 1:]], axis=3) + pe
    flat = blocks.reshape(B, G, blocks.shape[2], NSA_CMP_LEN * d)
    return jax.nn.gelu(flat @ w1) @ w2

def nsa_attention(q, k_cmp, v_cmp, k_slc, v_slc, k_win, v_win, gates, positions, pe_k, pe_v, k_w1, k_w2, v_w1, v_w2):
    B, G, R, S, d = q.shape
    scale = d ** -0.5
    kc = nsa_compress(k_cmp, pe_k, k_w1, k_w2)
    vc = nsa_compress(v_cmp, pe_v, v_w1, v_w2)
    nc = kc.shape[2]
    cos_c, sin_c = rope_tables(positions[:, NSA_CMP_LEN - 1::NSA_CMP_STRIDE], ROPE_DIM)
    kc = apply_rope(kc, cos_c[:, None], sin_c[:, None])
    cmp_start = jnp.arange(nc) * NSA_CMP_STRIDE
    cmp_end = cmp_start + NSA_CMP_LEN - 1
    ns = S // NSA_SEL_BLOCK
    topk = min(NSA_SEL_TOPK, ns)
    sel_start = jnp.arange(ns) * NSA_SEL_BLOCK
    overlap = ((cmp_start[:, None] < sel_start[None, :] + NSA_SEL_BLOCK)
               & (cmp_start[:, None] + NSA_CMP_LEN > sel_start[None, :])).astype(jnp.float32)
    ksb = k_slc.reshape(B, G, ns, NSA_SEL_BLOCK, d)
    vsb = v_slc.reshape(B, G, ns, NSA_SEL_BLOCK, d)
    wpad = ((0, 0), (0, 0), (NSA_WINDOW, 0), (0, 0))
    kw_pad, vw_pad = jnp.pad(k_win, wpad), jnp.pad(v_win, wpad)
    bi = jnp.arange(B)[:, None, None, None]
    gi = jnp.arange(G)[None, :, None, None]
    blk = jnp.arange(ns)

    def chunk(c):
        q0 = c * Q_BLOCK
        qc = lax.dynamic_slice_in_dim(q, q0, Q_BLOCK, axis=3)
        tq = q0 + jnp.arange(Q_BLOCK)
        p_c = masked_softmax(jnp.einsum('bgrqd,bgnd->bgrqn', qc, kc) * scale, cmp_end[None, :] <= tq[:, None])
        o_c = jnp.einsum('bgrqn,bgnd->bgrqd', p_c.astype(vc.dtype), vc)
        imp = jnp.einsum('bgqn,ns->bgqs', p_c.sum(axis=2), overlap)
        qb = (tq // NSA_SEL_BLOCK)[:, None]
        forced = (blk[None, :] == 0) | (blk[None, :] == qb) | (blk[None, :] == qb - 1)
        imp = jnp.where(forced, imp + NSA_FORCE_BONUS, imp)
        imp = jnp.where(blk[None, :] <= qb, imp, -jnp.inf)
        ival, sel = lax.top_k(imp, topk)
        ok = jnp.isfinite(ival)
        ks = ksb[bi, gi, sel]
        vs = vsb[bi, gi, sel]
        kpos = sel[..., None] * NSA_SEL_BLOCK + jnp.arange(NSA_SEL_BLOCK)
        m_s = (ok[..., None] & (kpos <= tq[:, None, None])).reshape(B, G, 1, Q_BLOCK, topk * NSA_SEL_BLOCK)
        s_s = (jnp.einsum('bgrqd,bgqnjd->bgrqnj', qc, ks) * scale).reshape(B, G, R, Q_BLOCK, topk * NSA_SEL_BLOCK)
        p_s = masked_softmax(s_s, m_s).astype(vs.dtype).reshape(B, G, R, Q_BLOCK, topk, NSA_SEL_BLOCK)
        o_s = jnp.einsum('bgrqnj,bgqnjd->bgrqd', p_s, vs)
        kw = lax.dynamic_slice_in_dim(kw_pad, q0, NSA_WINDOW + Q_BLOCK, axis=2)
        vw = lax.dynamic_slice_in_dim(vw_pad, q0, NSA_WINDOW + Q_BLOCK, axis=2)
        wpos = q0 - NSA_WINDOW + jnp.arange(NSA_WINDOW + Q_BLOCK)
        m_w = ((wpos[None, :] <= tq[:, None]) & (wpos[None, :] > tq[:, None] - NSA_WINDOW) & (wpos[None, :] >= 0))
        p_w = masked_softmax(jnp.einsum('bgrqd,bgkd->bgrqk', qc, kw) * scale, m_w)
        o_w = jnp.einsum('bgrqk,bgkd->bgrqd', p_w.astype(vw.dtype), vw)
        g = lax.dynamic_slice_in_dim(gates, q0, Q_BLOCK, axis=3)
        return g[..., 0:1] * o_c + g[..., 1:2] * o_s + g[..., 2:3] * o_w

    o = lax.map(chunk, jnp.arange(S // Q_BLOCK))
    return o.transpose(1, 2, 3, 0, 4, 5).reshape(B, G, R, S, d)

def mla_attention(c_q, c_kv, k_pe, q_norm, w_uq, kv_norm, w_ukv, cos, sin):
    q = heads(rmsnorm(c_q, q_norm) @ w_uq, MLA_HEADS)
    kv = heads(rmsnorm(c_kv, kv_norm) @ w_ukv, MLA_HEADS)
    q_nope, q_pe = q[..., :MLA_NOPE], q[..., MLA_NOPE:]
    k_nope, v = kv[..., :MLA_NOPE], kv[..., MLA_NOPE:]
    q_pe = apply_rope(q_pe, cos[:, None], sin[:, None])
    k_pe = apply_rope(k_pe[:, None], cos[:, None], sin[:, None])
    qf = jnp.concatenate([q_nope, q_pe], -1)
    kf = jnp.concatenate([k_nope, jnp.broadcast_to(k_pe, k_nope.shape[:3] + (MLA_ROPE,))], -1)
    return causal_attention(qf, kf, v, (MLA_NOPE + MLA_ROPE) ** -0.5)

def even_mixer(h, layer_idx, cos16, sin16, w_in, w_out, lq1, lk1, lq2, lk2, subln):
    B, S, _ = h.shape
    q_a, k_a, v_a, q_b, k_b, v_b = split_cols(h @ w_in, EV_SIZES)
    cA, sA = cos16[:, None], sin16[:, None]
    q_a, k_a, v_a = apply_rope(heads(q_a, MOBA_HEADS), cA, sA), apply_rope(heads(k_a, MOBA_HEADS), cA, sA), heads(v_a, MOBA_HEADS)
    o_a = moba_attention(q_a, k_a, v_a)
    cB, sB = cos16[:, None, None], sin16[:, None, None]
    q_b = apply_rope(q_b.reshape(B, S, DIFF_HEADS, 2, HEAD_DIM).transpose(0, 2, 3, 1, 4), cB, sB)
    k_b = apply_rope(k_b.reshape(B, S, DIFF_HEADS, 2, HEAD_DIM).transpose(0, 2, 3, 1, 4), cB, sB)
    v_b = heads(v_b, DIFF_HEADS)
    lambda_init = 0.8 - 0.6 * math.exp(-0.3 * layer_idx)
    lam = (jnp.exp(jnp.sum(lq1.astype(jnp.float32) * lk1.astype(jnp.float32)))
           - jnp.exp(jnp.sum(lq2.astype(jnp.float32) * lk2.astype(jnp.float32))) + lambda_init)
    o_b = diff_attention(q_b, k_b, v_b, lam, lambda_init, subln)
    return jnp.concatenate([merge_heads(o_a), merge_heads(o_b)], -1) @ w_out

def odd_mixer(h, positions, cos16, sin16, cos32, sin32, w_in, w_out, gate_b, pe_k, pe_v,
              k_w1, k_w2, v_w1, v_w2, q_norm, w_uq, kv_norm, w_ukv):
    B, S, _ = h.shape
    G, R = NSA_GROUPS, NSA_HEADS // NSA_GROUPS
    (q_c, k_cmp, v_cmp, k_slc, v_slc, k_win, v_win, g_c, c_q, c_kv, k_pe) = split_cols(h @ w_in, OD_SIZES)
    q_c = apply_rope(q_c.reshape(B, S, G, R, HEAD_DIM).transpose(0, 2, 3, 1, 4), cos16[:, None, None], sin16[:, None, None])
    k_slc = apply_rope(heads(k_slc, G), cos16[:, None], sin16[:, None])
    k_win = apply_rope(heads(k_win, G), cos16[:, None], sin16[:, None])
    gates = jax.nn.sigmoid(g_c.astype(jnp.float32) + gate_b.astype(jnp.float32))
    gates = gates.reshape(B, S, G, R, 3).transpose(0, 2, 3, 1, 4).astype(h.dtype)
    o_c = nsa_attention(q_c, heads(k_cmp, G), heads(v_cmp, G), k_slc, heads(v_slc, G), k_win, heads(v_win, G),
                        gates, positions, pe_k, pe_v, k_w1, k_w2, v_w1, v_w2)
    o_c = o_c.transpose(0, 3, 1, 2, 4).reshape(B, S, NSA_HEADS * HEAD_DIM)
    o_d = mla_attention(c_q, c_kv, k_pe, q_norm, w_uq, kv_norm, w_ukv, cos32, sin32)
    return jnp.concatenate([o_c, merge_heads(o_d)], -1) @ w_out

def swiglu(h, wg, wu, wd):
    return (jax.nn.silu(h @ wg) * (h @ wu)) @ wd

def setup_inputs(seed: int = 0) -> dict:
    key = jax.random.key(seed)
    keys = iter(jax.random.split(key, 32))
    NE, NO = (DEPTH + 1) // 2, DEPTH // 2

    def nrm(shape, scale):
        return scale * jax.random.normal(next(keys), shape, jnp.float32)

    def gain(shape):
        return 1.0 + 0.05 * jax.random.normal(next(keys), shape, jnp.float32)

    flat_cmp = NSA_CMP_LEN * HEAD_DIM
    return {
        "x": jax.random.normal(next(keys), (BATCH, SEQ, D_MODEL), jnp.float32),
        "positions": jnp.tile(jnp.arange(SEQ, dtype=jnp.int32)[None, :], (BATCH, 1)),
        "attn_norm": gain((DEPTH, D_MODEL)),
        "ffn_norm": gain((DEPTH, D_MODEL)),
        "final_norm": gain((D_MODEL,)),
        "ffn_w_gate": nrm((DEPTH, D_MODEL, D_FF), D_MODEL ** -0.5),
        "ffn_w_up": nrm((DEPTH, D_MODEL, D_FF), D_MODEL ** -0.5),
        "ffn_w_down": nrm((DEPTH, D_FF, D_MODEL), D_FF ** -0.5),
        "ev_w_in": nrm((NE, D_MODEL, EV_IN), D_MODEL ** -0.5),
        "ev_w_out": nrm((NE, EV_OUT, D_MODEL), EV_OUT ** -0.5),
        "diff_lambda_q1": nrm((NE, HEAD_DIM), 0.1),
        "diff_lambda_k1": nrm((NE, HEAD_DIM), 0.1),
        "diff_lambda_q2": nrm((NE, HEAD_DIM), 0.1),
        "diff_lambda_k2": nrm((NE, HEAD_DIM), 0.1),
        "diff_subln": gain((NE, DIFF_V)),
        "od_w_in": nrm((NO, D_MODEL, OD_IN), D_MODEL ** -0.5),
        "od_w_out": nrm((NO, OD_OUT, D_MODEL), OD_OUT ** -0.5),
        "nsa_gate_b": nrm((NO, NSA_HEADS * 3), 0.1),
        "nsa_pe_k": nrm((NO, NSA_CMP_LEN, HEAD_DIM), 0.1),
        "nsa_pe_v": nrm((NO, NSA_CMP_LEN, HEAD_DIM), 0.1),
        "nsa_k_w1": nrm((NO, flat_cmp, NSA_CMP_HIDDEN), flat_cmp ** -0.5),
        "nsa_k_w2": nrm((NO, NSA_CMP_HIDDEN, HEAD_DIM), NSA_CMP_HIDDEN ** -0.5),
        "nsa_v_w1": nrm((NO, flat_cmp, NSA_CMP_HIDDEN), flat_cmp ** -0.5),
        "nsa_v_w2": nrm((NO, NSA_CMP_HIDDEN, HEAD_DIM), NSA_CMP_HIDDEN ** -0.5),
        "mla_q_norm": gain((NO, MLA_Q_RANK)),
        "mla_w_uq": nrm((NO, MLA_Q_RANK, MLA_HEADS * (MLA_NOPE + MLA_ROPE)), MLA_Q_RANK ** -0.5),
        "mla_kv_norm": gain((NO, MLA_KV_RANK)),
        "mla_w_ukv": nrm((NO, MLA_KV_RANK, MLA_HEADS * (MLA_NOPE + MLA_V)), MLA_KV_RANK ** -0.5),
    }

def reference(x, positions, attn_norm, ffn_norm, final_norm, ffn_w_gate, ffn_w_up, ffn_w_down,
              ev_w_in, ev_w_out, diff_lambda_q1, diff_lambda_k1, diff_lambda_q2, diff_lambda_k2, diff_subln,
              od_w_in, od_w_out, nsa_gate_b, nsa_pe_k, nsa_pe_v, nsa_k_w1, nsa_k_w2, nsa_v_w1, nsa_v_w2,
              mla_q_norm, mla_w_uq, mla_kv_norm, mla_w_ukv):
    cos16, sin16 = rope_tables(positions, ROPE_DIM)
    cos32, sin32 = rope_tables(positions, MLA_ROPE)
    h = x
    for l in range(DEPTH):
        i = l // 2
        hn = rmsnorm(h, attn_norm[l])
        if l % 2 == 0:
            h = h + even_mixer(hn, l, cos16, sin16, ev_w_in[i], ev_w_out[i], diff_lambda_q1[i], diff_lambda_k1[i],
                               diff_lambda_q2[i], diff_lambda_k2[i], diff_subln[i])
        else:
            h = h + odd_mixer(hn, positions, cos16, sin16, cos32, sin32, od_w_in[i], od_w_out[i], nsa_gate_b[i],
                              nsa_pe_k[i], nsa_pe_v[i], nsa_k_w1[i], nsa_k_w2[i], nsa_v_w1[i], nsa_v_w2[i],
                              mla_q_norm[i], mla_w_uq[i], mla_kv_norm[i], mla_w_ukv[i])
        hn = rmsnorm(h, ffn_norm[l])
        h = h + swiglu(hn, ffn_w_gate[l], ffn_w_up[l], ffn_w_down[l])
    return rmsnorm(h, final_norm)


_drawn_inputs = setup_inputs


def setup_inputs(seed=0):
    import zlib

    import numpy as np

    out = dict(_drawn_inputs(seed))
    spreads = {}
    factors = {'diff_lambda_q1': 5.927,
     'diff_lambda_k1': 8.0,
     'nsa_gate_b': 32.807,
     'nsa_pe_k': 64.0,
     'nsa_pe_v': 12.769,
     'mla_q_norm': 8.0,
     'mla_kv_norm': 6.456,
     'diff_lambda_q2': 7.615,
     'diff_lambda_k2': 8.0,
     'nsa_k_w1': 5.928,
     'nsa_k_w2': 5.943}
    for name, (base, spread) in spreads.items():
        noise = np.random.default_rng([zlib.crc32(name.encode()), seed]).standard_normal(out[name].shape)
        drawn = base * np.exp(spread * noise) if base else spread * noise
        out[name] = __import__('jax').numpy.asarray(drawn.astype(out[name].dtype))
    for name, factor in factors.items():
        out[name] = (out[name] * factor).astype(out[name].dtype)
    return out
```

```python
from contextlib import ExitStack

import numpy as np
import concourse.bass as bass
from concourse import mybir

F32 = mybir.dt.float32
F32R = mybir.dt.float32r
I32 = mybir.dt.int32
ALU = mybir.AluOpType
ACT = mybir.ActivationFunctionType
AX = mybir.AxisListType

P = 128
SEQ = 256
NT = SEQ // P
D = 1024
KT = D // P
FF = 2816
NI = FF // 256
HD = 64
NH = 8
NDH = 4
NG = 2
NCMP = SEQ // 16 - 1
NC = NCMP + 1
LQ, LKV, RO, NOPE = 256, 128, 32, 64
MD = NOPE + RO
EPS = 1e-5
THETA = 500000.0
LAMBDA_INIT = 0.8 - 0.6 * float(np.exp(-0.3 * 0))
NEG = -1e30
RING = 3
SLAB = 2048
SCORE_COLS = 3 * P
OD_W = [512, 512, 512, 184]
PI = float(np.float32(np.pi))
TWO_PI_PARTS = (6.28125, 1.93500518798828125e-3, 3.01991598196e-7)
ROUND = 1.5 * 2.0 ** 23


class Step:

    def __init__(self, kind,
                 acc=None, bank=None, banks=None, base=None, buf=None, chunks=None, combined=None,
                 combined_before=None, diff=None, down_base=None, dst=None, end=None, evac=None,
                 first=None, g0=None, gain=None, gate_wait=None, group=None, h_needed=None,
                 half=None, head=None, hid=None, k=None, k0=None, kts=None, kv=None, last=None,
                 layer=None, m=None, maps=None, n=None, needs=None, out=None, part=None, pt=None,
                 pv_before=None, read=None, ready=None, released=None, roped=None, s0=None,
                 slab=None, src=None, t=None, t_needed=None, u0=None, uid=None, unit=None,
                 up_wait=None, v_needs=None, what=None, where=None, which=None, width=None,
                 x_needed=None):
        self.kind = kind
        self.acc = acc
        self.bank = bank
        self.banks = banks
        self.base = base
        self.buf = buf
        self.chunks = chunks
        self.combined = combined
        self.combined_before = combined_before
        self.diff = diff
        self.down_base = down_base
        self.dst = dst
        self.end = end
        self.evac = evac
        self.first = first
        self.g0 = g0
        self.gain = gain
        self.gate_wait = gate_wait
        self.group = group
        self.h_needed = h_needed
        self.half = half
        self.head = head
        self.hid = hid
        self.k = k
        self.k0 = k0
        self.kts = kts
        self.kv = kv
        self.last = last
        self.layer = layer
        self.m = m
        self.maps = maps
        self.n = n
        self.needs = needs
        self.out = out
        self.part = part
        self.pt = pt
        self.pv_before = pv_before
        self.read = read
        self.ready = ready
        self.released = released
        self.roped = roped
        self.s0 = s0
        self.slab = slab
        self.src = src
        self.t = t
        self.t_needed = t_needed
        self.u0 = u0
        self.uid = uid
        self.unit = unit
        self.up_wait = up_wait
        self.v_needs = v_needs
        self.what = what
        self.where = where
        self.which = which
        self.width = width
        self.x_needed = x_needed


class Plan:

    def __init__(self):
        self.steps, self.slabs = [], []
        self.count = {}
        self.bank_free = [None] * 8
        self.bank_fills = [0] * 8
        for b in range(2):
            self.take(b, ("small_made", b + 1))
        self.tbank = 0
        self.maps = self.units = 0

    def tick(self, name, n=1):
        self.count[name] = self.count.get(name, 0) + n
        return self.count[name]

    def add(self, kind, **fields):
        s = Step(kind, **fields)
        self.steps.append(s)
        return s

    def take(self, b, release):
        wait, self.bank_free[b] = self.bank_free[b], release
        self.bank_fills[b] += 1
        return (b, wait, self.bank_fills[b])

    def turn(self, release):
        b = 2 + self.tbank % 2
        self.tbank += 1
        return self.take(b, release)

    def slab(self, what, n, *where):
        self.slabs.append(Step("slab", what=what, n=n, where=where, released=None))
        return len(self.slabs) - 1

    def norm(self, k):
        self.add("norm", k=k, h_needed=self.count.get("h_ready", 0))

    def x_transposed(self, src, ready, chunks, gain):
        n = self.tick("xlo_made")
        self.tick("xhi_made")
        self.add("xt", src=src, ready=ready, chunks=chunks, gain=gain, n=n, bank=self.turn(("xlo_made", n)))
        return n

    def projection(self, what, group, width, slabs, banks, x_needed, kts, x0=0, acc="evac_made"):
        uses = []
        for t in range(NT):
            uses.append(self.take(banks[t], (acc, self.tick(acc))))
        at = x0
        for i, s in enumerate(slabs):
            last = i == len(slabs) - 1
            for t in range(NT):
                end = t == NT - 1
                if end:
                    self.slabs[s].released = ("filled", uses[t][0], uses[t][2]) if last else \
                        ("slab_used", self.tick("slab_used"))
                self.add("proj", what=what, group=group, width=width, slab=s, t=t, bank=uses[t], kts=kts[i],
                         k0=at, first=i == 0, last=last, end=end, x_needed=x_needed[i], acc=acc)
            at += kts[i]
        return uses

    def transposed(self, kind, **fields):
        n = self.tick("t_made")
        self.add(kind, n=n, bank=self.turn(("t_made", n)), **fields)
        return n

    def ffn(self, layer):
        s0 = len(self.slabs)
        order = [("gate", 0), ("up", 0)]
        for i in range(1, NI):
            order += [("gate", i), ("up", i), ("down", i - 1)]
        order.append(("down", NI - 1))
        st = self.add("ffn", layer=layer, s0=s0, base=NI * layer, down_base=(NI - 1) * layer,
                      g0=self.bank_fills[0], u0=self.bank_fills[1],
                      gate_wait=self.bank_free[0], up_wait=self.bank_free[1])
        for what, i in order:
            s = self.slab(what, SLAB, layer, i)
            rel = {"gate": ("filled", 0, st.g0 + i + 1), "up": ("filled", 1, st.u0 + i + 1),
                   "down": ("down_done", st.down_base + i + 1)}[what]
            self.slabs[s].released = rel
        self.bank_fills[0] += NI
        self.bank_fills[1] += NI
        self.bank_free[0] = ("gated", st.base + NI)
        self.bank_free[1] = ("h_made", st.base + NI)
        st.x_needed = self.count["xlo_made"]
        st.out = [self.take(4 + b, ("h_ready", self.tick("h_ready"))) for b in range(4)]
        self.slabs[-1].released = ("filled", 7, st.out[3][2])


def interleave(*lists):
    out, keyed = [], []
    for n, steps in enumerate(lists):
        keyed += [((i + 0.5) / len(steps), n, s) for i, s in enumerate(steps)]
    for _, _, s in sorted(keyed, key=lambda k: k[:2]):
        out.append(s)
    return out


def attention_order(n_units, maps_per_unit, name):
    out = []
    for u in range(n_units + 2):
        if u < n_units:
            out += [(name, "scores", u, i) for i in range(maps_per_unit)]
        if 1 <= u <= n_units:
            out.append((name, "turn", u - 1, 0))
        if u >= 2:
            out.append((name, "value", u - 2, 0))
    return out + [(name, "out", 0, 0)]


def make_plan():
    p = Plan()

    def emit(tokens, groups):
        for tok in tokens:
            if callable(tok):
                tok()
                continue
            name, what, u, i = tok
            g = groups[name]
            if what == "scores":
                m = p.maps
                p.maps += 1
                g["maps"].append(m)
                b = m % 2
                p.add("scores", group=name, unit=u, part=i, m=m, bank=p.take(b, ("masked", 2 * (m + 1))),
                      needs=g["needs"])
            elif what == "turn":
                n_maps = g["per"]
                uid = p.units
                p.units += 1
                g["uids"].append(uid)
                n = p.tick(f"pt_made{uid % 2}")
                p.add("turn", group=name, unit=u, uid=uid, maps=g["maps"][u * n_maps:(u + 1) * n_maps], n=n,
                      bank=p.turn((f"pt_made{uid % 2}", n)), diff=n_maps == 2, pv_before=g_pv.get(uid - 2),
                      combined_before=p.count.get("combined", 0))
                if n_maps == 2:
                    p.steps[-1].combined = p.tick("combined")
            elif what == "value":
                last = u == g["n"] - 1
                if u == 0:
                    g["banks"] = [p.take(4 + t, ("o_banks_read", p.tick("o_banks_read"))) for t in range(NT)]
                uid = g["uids"][u]
                rel = ("filled", 5, g["banks"][1][2]) if last else ("pv_done", p.tick("pv_done"))
                g_pv[uid] = rel
                pt = next(s for s in p.steps if s.kind == "turn" and s.uid == uid)
                p.add("value", group=name, unit=u, uid=uid, pt=pt.n, banks=g["banks"], first=u == 0, last=last,
                      needs=g["v_needs"])
            else:
                p.add("out", group=name, banks=g["banks"], maps=g["maps"], read=p.count["o_banks_read"])
                if name == "diff":
                    p.tick("o_ready")

    g_pv = {}

    def group(n, per):
        return {"n": n, "per": per, "maps": [], "uids": [], "needs": None, "v_needs": None}

    p.norm(0)
    for j in range(KT // 2):
        p.x_transposed("hs", 1, (2 * j, 2 * j + 1), 0)
    p.add("tables")
    ev = []
    for g in range(6):
        ev.append([p.slab("ev_in", SLAB, g, h) for h in range(2)])
    evac = {}

    def ev_proj(g):
        banks = (6, 7) if g % 2 == 0 or g > 2 else (4, 5)
        start = len(p.steps)
        p.projection("ev_in", g, 512, ev[g], banks, [2, 4] if g == 0 else [4, 4], [4, 4])
        evac[g] = p.count["evac_made"]
        sub = p.steps[start:]
        del p.steps[start:]
        return sub

    def place(s):
        return lambda: p.steps.append(s)

    def rope_and_turn(g, buf):
        n = p.tick("roped")
        p.add("rope", what="nat", buf=buf, evac=evac[g], n=n, width=16)
        for half in range(2):
            p.transposed("qkt", dst=(g, half), buf=buf, roped=n)

    groups = {"moba": group(NH, 1), "diff": group(NDH, 2)}
    for s in ev_proj(0):
        p.steps.append(s)
    for s in ev_proj(1):
        p.steps.append(s)
    rope_and_turn(0, 0)
    for s in ev_proj(2):
        p.steps.append(s)
    rope_and_turn(1, 1)
    groups["moba"]["needs"] = p.count["t_made"]
    groups["moba"]["v_needs"] = evac[2]
    fill = [place(s) for s in ev_proj(3)] + [place(s) for s in ev_proj(4)] + [lambda: rope_and_turn(3, 0)] + \
        [place(s) for s in ev_proj(5)] + [lambda: rope_and_turn(4, 1)]
    emit(interleave(attention_order(NH, 1, "moba"), fill), groups)
    groups["diff"]["needs"] = p.count["t_made"]
    groups["diff"]["v_needs"] = evac[5]
    emit(attention_order(NDH, 2, "diff"), groups)

    def out_projection(what):
        base = p.count["xlo_made"]
        ready = (p.count["o_banks_read"], p.count["o_ready"])
        for j in range(KT // 2):
            p.x_transposed("o", ready, (2 * j, 2 * j + 1), None)
        for g in range(2):
            slabs = [p.slab(what, SLAB, g, h) for h in range(2)]
            p.projection(what, g, 512, slabs, (6, 7) if g == 0 else (4, 5), [base + 2, base + 4], [4, 4],
                         acc="h_ready")

    def norm_and_ffn(layer):
        base = p.count["xlo_made"]
        k = 2 * layer + 1
        p.norm(k)
        for j in range(KT // 2):
            p.x_transposed("hs", k + 1, (2 * j, 2 * j + 1), 16 + 8 * layer)
        p.ffn(layer)

    out_projection("ev_out")
    norm_and_ffn(0)

    p.norm(2)
    base = p.count["xlo_made"]
    for j in range(KT // 2):
        p.x_transposed("hs", 3, (2 * j, 2 * j + 1), 8)

    def od_proj(g, banks):
        slabs = [p.slab("od_in", 4 * OD_W[g], g, h) for h in range(2)]
        start = len(p.steps)
        p.projection("od_in", g, OD_W[g], slabs, banks, [base + 2, base + 4], [4, 4])
        evac["o%d" % g] = p.count["evac_made"]
        sub = p.steps[start:]
        del p.steps[start:]
        return sub

    groups = {"slc": group(NH, 1), "win": group(NH, 1), "mla": group(NH, 1)}
    p.steps += od_proj(0, (6, 7))
    p.steps += od_proj(1, (4, 5))
    n = p.tick("roped")
    p.add("rope", what="nat", buf=0, evac=evac["o0"], n=n, width=16)
    for half in range(2):
        p.transposed("qkt", dst=(6, half), buf=0, roped=n)
    nk = p.tick("roped")
    p.add("rope", what="kslc", evac=evac["o1"], n=nk, width=16)
    p.transposed("kdt", which=0, roped=nk, evac=evac["o1"])
    groups["slc"]["needs"] = p.count["t_made"]
    groups["slc"]["v_needs"] = evac["o1"]
    for kv in range(2):
        n = p.tick("xc_lo_made")
        p.tick("xc_made")
        p.add("blocks", kv=kv, n=n, evac=evac["o1"], bank=p.turn(("xc_made", n)))
    p.steps += od_proj(2, (6, 7))
    nk = p.tick("roped")
    p.add("rope", what="kwin", evac=evac["o2"], n=nk, width=16)
    p.transposed("kdt", which=1, roped=nk, evac=evac["o2"])
    groups["win"]["needs"] = p.count["t_made"]
    groups["win"]["v_needs"] = evac["o2"]
    p.add("gates", evac=evac["o2"])

    def compress(kv):
        slabs = [p.slab("w1", SLAB, kv, h) for h in range(2)]
        n = p.tick("hid_read")
        uses = [p.take(c, ("hid_read", n)) for c in range(2)]
        for h in range(2):
            p.slabs[slabs[h]].released = ("filled", 1, uses[1][2]) if h else ("slab_used", p.tick("slab_used"))
            p.add("compress", kv=kv, half=h, slab=slabs[h], banks=uses, x_needed=kv + 1, n=n)
        n = p.tick("t_made")
        p.add("second", kv=kv, n=n, bank=p.turn(("t_made", n)), hid=kv + 1)
        if kv == 0:
            nk = p.tick("roped")
            n2 = p.tick("t_made")
            p.add("kcmp", roped=nk, evac=n, n=n2, bank=p.turn(("t_made", n2)))

    compress(0)
    compress(1)
    cs = p.add("cscores", banks=None, t_needed=p.count["t_made"])
    cs.banks = [p.take(b, ("c_masked", b + 1)) for b in range(2)]
    g3 = [place(s) for s in od_proj(3, (6, 7))]
    emit(interleave(attention_order(NH, 1, "slc"), g3), groups)
    n = p.tick("roped")
    p.add("rope", what="kpe", evac=evac["o3"], n=n, width=RO)
    p.add("latent_norm", evac=evac["o3"], n=n)
    xb = p.count["xlo_made"]
    p.x_transposed("latent", 1, (0, 1), 32)
    p.x_transposed("latent", 1, (2,), 32)
    uq = p.slab("uq", 2 * 768, 0)
    ukv = p.slab("ukv", 1024, 0)
    start = len(p.steps)
    for what, s, k0, kts, need in (("uq", uq, 0, 2, xb + 1), ("ukv", ukv, 2, 1, xb + 2)):
        for half in range(2):
            uses = [p.take(6 + t, ("evac_made", p.tick("evac_made"))) for t in range(NT)]
            for t in range(NT):
                if half and t:
                    p.slabs[s].released = ("filled", 7, uses[t][2])
                p.add("up", what=what, half=half, slab=s, t=t, bank=uses[t], kts=kts, k0=k0, x_needed=need,
                      end=bool(half and t), acc="evac_made", width=768 if what == "uq" else 1024)
    evac["mla"] = p.count["evac_made"]
    ups = p.steps[start:]
    del p.steps[start:]
    emit(interleave(attention_order(NH, 1, "win"), [place(s) for s in ups]), groups)
    p.add("cturn", bank=p.turn(("pct_made", 1)))
    b4 = [p.take(4 + t, ("o_banks_read", p.tick("o_banks_read"))) for t in range(NT)]
    p.add("cvalue", banks=b4)
    p.add("out", group="cmp", banks=b4, maps=[], read=p.count["o_banks_read"])
    p.tick("o_ready")
    n = p.tick("roped")
    p.add("rope", what="qpe", evac=evac["mla"], n=n, width=RO)
    for h in range(NH):
        p.transposed("mqkt", head=h, roped=n, evac=evac["mla"])
    groups["mla"]["needs"] = p.count["t_made"]
    groups["mla"]["v_needs"] = evac["mla"]
    emit(attention_order(NH, 1, "mla"), groups)
    out_projection("od_out")
    norm_and_ffn(1)
    p.norm(4)
    return p


def build(nc, t_in, out):
    plan = make_plan()
    steps, slabs = plan.steps, plan.slabs
    n_slabs = len(slabs)
    with ExitStack() as ctx:
        def sb(name, shape, dt=F32):
            return ctx.enter_context(nc.sbuf_tensor(name, shape, dt))

        raw = [sb(f"raw{i}", [P, SLAB]) for i in range(RING)]
        whi = [sb(f"whi{i}", [P, SLAB], F32R) for i in range(RING)]
        wlo = [sb(f"wlo{i}", [P, SLAB], F32R) for i in range(RING)]
        h = sb("h", [P, NT, D])
        hs = sb("hs", [P, NT, D])
        xhi = sb("xhi", [P, KT, SEQ], F32R)
        xlo = sb("xlo", [P, KT, SEQ], F32R)
        o = hs
        nat = sb("nat", [P, 2, NT, 512])
        qk = sb("qk", [P, 4, 4, SEQ])
        vals = sb("vals", [P, 2, NT, 512])
        vnsa = sb("vnsa", [P, 2, NT, P])
        nat2 = sb("nat2", [P, NT, 4, NG, 2, HD])
        kd = sb("kd", [P, 2, NG, SEQ])
        masked = sb("masked", [P, 2, SCORE_COLS])
        prob = sb("prob", [P, 4, SCORE_COLS])
        comb = sb("comb", [P, 2, SCORE_COLS])
        pt = sb("pt", [P, 2, SCORE_COLS])
        n_maps = plan.maps
        nmax = sb("nmax", [P, 2 * n_maps])
        sums = sb("sums", [P, 2 * n_maps])
        rinv = sb("rinv", [P, 2 * n_maps])
        coef = sb("coef", [P, NT, NH])
        rope_a = sb("rope_a", [P, NT, NH, RO])
        rope_b = sb("rope_b", [P, NT, NH, RO])
        otmp = sb("otmp", [P, 512])
        xc = sb("xc", [P, 16, NG, NC])
        xch = sb("xch", [P, 2, 16, NG * NC], F32R)
        xcl = sb("xcl", [P, 2, 16, NG * NC], F32R)
        hid = sb("hid", [P, 2, NG * NC])
        hid2 = sb("hid2", [P, 2, NG * NC])
        hid3 = sb("hid3", [P, 2, NG * NC])
        hk = sb("hk", [P, 2, NG * NC])
        hv = sb("hv", [P, 2, NH, NC])
        kcn = sb("kcn", [NG * NC, 2, HD])
        kct = sb("kct", [P, NG * NC])
        vbd = sb("vbd", [P, NH, HD])
        cs = sb("cs", [P, NT, NH, NC])
        cmx = sb("cmx", [P, NT * NH])
        csum = sb("csum", [P, NT * NH])
        pct = sb("pct", [P, NT, P])
        gate = sb("gate", [P, NT, NH * 3])
        lat = sb("lat", [P, NT, LQ + LKV])
        lats = comb[:, :, :].rearrange("p a n -> p (a n)").rearrange("p (t n) -> p t n", t=NT)
        kpe = sb("kpe", [P, NT, RO])
        def room(flat, d):
            return flat[:, 0:NT * NH * d].rearrange("p (t h d) -> p t h d", t=NT, h=NH)

        qm = room(nat[:, :, :, :].rearrange("p b t n -> p (b t n)"), MD)
        km = room(nat2[:, :, :, :, :, :].rearrange("p t w g u d -> p (t w g u d)"), MD)
        vm = room(vals[:, 0].rearrange("p t n -> p (t n)"), HD)
        free = masked[:, :, :].rearrange("p a n -> p (a n)"), prob[:, :, :].rearrange("p a n -> p (a n)")
        th, ga, hf = free[0][:, 0:512], free[1][:, 0:512], free[1][:, 512:1024]
        hhi, hlo = (x[:, 0].rearrange("p j n -> p (j n)") for x in (xch, xcl))
        ident = sb("ident", [P, P])
        tri = sb("tri", [P, SCORE_COLS])
        cmask = sb("cmask", [P, NT, NC])
        cvalid = sb("cvalid", [P, NT, NC])
        bdm = sb("bdm", [P, NH])
        invf = sb("invf", [P, 16])
        mhalf = sb("mhalf", [P, 8])
        posi = sb("posi", [P, 3], I32)
        posf = sb("posf", [P, 3])
        ang = sb("ang", [P, 3, 16])
        turns = sb("turns", [P, 3, 16])
        red = sb("red", [P, 2, 3, 16])
        trig = sb("trig", [P, 2, 3, 16])
        cc8 = sb("cc8", [P, 3, 16])
        sn8 = sb("sn8", [P, 3, 16])
        cc16 = sb("cc16", [P, 3, 32])
        sn16 = sb("sn16", [P, 3, 32])
        grow = sb("grow", [35, P])
        gains = sb("gains", [P, 35])
        perow = sb("perow", [32, 2, 2, HD])
        pet = sb("pet", [P, 2, 32])
        w2 = sb("w2", [P, 2, 2, HD])
        gfin = sb("gfin", [P, D])
        subln = sb("subln", [P, 2 * HD])
        gateb = sb("gateb", [P, NH * 3])
        lqk = sb("lqk", [P, 4, HD])
        lam = sb("lam", [P, 4])
        ssq = sb("ssq", [P, 8])
        msq = sb("msq", [P, 8])
        rstd = sb("rstd", [P, 8])

        def mla_qk(head, which):
            return qk[0:MD, 2 * which + head // 4, head % 4, :]

        psum = [ctx.enter_context(nc.psum_tensor(f"bank{b}", [P, 512], F32)) for b in range(8)]

        sem = {n: ctx.enter_context(nc.semaphore(n)) for n in (
            "x_landed", "small_landed", "hi_made", "lo_made", "slab_used", "ssq_made", "rstd_made", "hs0_made",
            "hs1_made", "xhi_made", "xlo_made", "evac_made", "roped", "t_made", "masked", "exped", "pt_made0",
            "pt_made1", "pv_done", "o_banks_read", "o_ready", "combined", "tanh_made", "gated", "h_made",
            "hhi_made", "hlo_made", "down_done", "h_ready", "dve_step", "pool_step", "consts_made", "angles_made",
            "sin_made", "turned_small", "small_made", "lam_dots", "lam_exp", "ob_ssq", "ob_rstd", "xc_made",
            "xch_made", "xc_lo_made", "hid_copied", "gelu_in", "gelu_th", "gelu_out", "hid_read", "kc_copied",
            "c_masked", "c_centred", "c_exped", "c_ready", "pct_made", "gate_in", "gate_th", "gates_made",
            "lat_ssq", "lat_rstd", "lat_made", "kpe_spread", "fin_made", "stored")}
        filled = [ctx.enter_context(nc.semaphore(f"filled{b}")) for b in range(8)]
        landed = [ctx.enter_context(nc.semaphore(f"landed{i}")) for i in range(RING)]
        block = ctx.enter_context(nc.Block())

        def wait(eng, what):
            if what is None:
                return
            if what[0] == "filled":
                eng.wait_ge(filled[what[1]], what[2])
            else:
                eng.wait_ge(sem[what[0]], what[1])

        prob_free, comb_free = {}, {}
        for st in steps:
            if st.kind == "turn":
                turned = ("filled", st.bank[0], st.bank[2])
                for m in st.maps:
                    prob_free[m] = ("combined", st.combined) if st.diff else turned
                if st.diff:
                    comb_free[st.unit] = turned

        def bank_filled(eng, bank):
            eng.wait_ge(filled[bank[0]], bank[2])

        def tiles(ap):
            return ap.rearrange("(k p) n -> p k n", p=P)

        ev_in, ev_out = tiles(t_in["ev_w_in"][0]), tiles(t_in["ev_w_out"][0])
        od_in, od_out = tiles(t_in["od_w_in"][0]), tiles(t_in["od_w_out"][0])
        w_gate = [tiles(t_in["ffn_w_gate"][l]) for l in range(2)]
        w_up = [tiles(t_in["ffn_w_up"][l]) for l in range(2)]
        w_down = [tiles(t_in["ffn_w_down"][l]) for l in range(2)]
        w1 = [tiles(t_in[n][0]) for n in ("nsa_k_w1", "nsa_v_w1")]

        def slab_source(s):
            what, w = s.what, s.where
            if what in ("ev_in", "ev_out", "od_out"):
                v = {"ev_in": ev_in, "ev_out": ev_out, "od_out": od_out}[what]
                return v[:, 4 * w[1]:4 * w[1] + 4, 512 * w[0]:512 * (w[0] + 1)]
            if what == "od_in":
                return od_in[:, 4 * w[1]:4 * w[1] + 4, 512 * w[0]:512 * w[0] + OD_W[w[0]]]
            if what == "w1":
                return w1[w[0]][:, 8 * w[1]:8 * w[1] + 8, :]
            if what == "uq":
                return tiles(t_in["mla_w_uq"][0])
            if what == "ukv":
                return tiles(t_in["mla_w_ukv"][0])
            return ffn_source(what, *w)

        def ffn_source(what, layer, i):
            if what == "gate":
                return w_gate[layer][:, :, bass.ds(256 * i, 256)]
            if what == "up":
                return w_up[layer][:, :, bass.ds(256 * i, 256)]
            return w_down[layer][:, bass.ds(2 * i, 2), :]

        def parts(tile, k, n):
            return tile[:, 0:k * n].rearrange("p (k n) -> p k n", k=k)

        n_small = 21

        @block.sync
        def _(sp):
            x = t_in["x"][0].rearrange("(t p) d -> p t d", p=P)
            sp.dma_start(h[:, :, :], x).then_inc(sem["x_landed"], 16)

            def load(slot, source, n, k, lo_wait):
                if lo_wait is not None:
                    sp.wait_ge(sem["lo_made"], lo_wait)
                sp.dma_start(parts(raw[slot], k, n // k), source).then_inc(landed[slot], 16)

            ffn_at = {s.s0: s for s in steps if s.kind == "ffn"}
            s = 0
            while s < n_slabs:
                sl = slabs[s]
                if s in ffn_at:
                    st = ffn_at[s]
                    lyr, s0 = st.layer, st.s0

                    def ffn_slab(k, what, i):
                        load((s0 + k) % RING, ffn_source(what, lyr, i), SLAB, 2 if what == "down" else KT, None)

                    for k, (what, i) in enumerate((("gate", 0), ("up", 0), ("gate", 1), ("up", 1), ("down", 0))):
                        sp.wait_ge(sem["lo_made"], s0 + k - RING + 1)
                        ffn_slab(k, what, i)
                    with sp.Fori(2, NI) as i:
                        for j, (what, back) in enumerate((("gate", 0), ("up", 0), ("down", 1))):
                            sp.wait_ge(sem["lo_made"], i * RING + (s0 - 1 + j - RING + 1))
                            ffn_slab(2 + j, what, i - back)
                    sp.wait_ge(sem["lo_made"], s0 + 3 * NI - 1 - RING + 1)
                    ffn_slab(3 * NI - 1, "down", NI - 1)
                    s += 3 * NI
                    continue
                k = slab_source(sl).shape[1]
                load(s % RING, slab_source(sl), sl.n, k, s - RING + 1 if s >= RING else None)
                s += 1
            for t in range(NT):
                sp.wait_ge(sem["fin_made"], t + 1)
                sp.dma_start(out[0, t * P:(t + 1) * P, :], hs[:, t, :]).then_inc(sem["stored"], 16)
            sp.wait_ge(sem["stored"], 32)

        @block.gpsimd
        def _(pool):
            loads = [
                (grow[0:16, :], t_in["attn_norm"].rearrange("l (k p) -> (l k) p", p=P)),
                (grow[16:32, :], t_in["ffn_norm"].rearrange("l (k p) -> (l k) p", p=P)),
                (grow[32:34, :], t_in["mla_q_norm"].rearrange("l (k p) -> (l k) p", p=P)),
                (grow[34:35, :], t_in["mla_kv_norm"]),
                (gfin[:, :], t_in["final_norm"].partition_broadcast(P)),
                (subln[:, :], t_in["diff_subln"][0].partition_broadcast(P)),
                (gateb[:, :], t_in["nsa_gate_b"][0].partition_broadcast(P)),
            ]
            for j, n in enumerate(("diff_lambda_q1", "diff_lambda_k1", "diff_lambda_q2", "diff_lambda_k2")):
                loads.append((lqk[:, j, :], t_in[n][0].partition_broadcast(P)))
            for kv, n in enumerate(("nsa_pe_k", "nsa_pe_v")):
                for dup in range(2):
                    loads.append((perow[:, kv, dup, :], t_in[n][0]))
            for kv, n in enumerate(("nsa_k_w2", "nsa_v_w2")):
                loads.append((w2[:, kv, :, :], tiles(t_in[n][0])))
            pool.memset(posi[:, :], 0).then_inc(sem["pool_step"], 1)
            for dst, src in loads:
                pool.dma_start(dst, src).then_inc(sem["small_landed"], 16)
            pos = t_in["positions"]
            pool.wait_ge(sem["pool_step"], 1)
            for t in range(NT):
                pool.dma_start(posi[:, t:t + 1], pos[0, t * P:(t + 1) * P].unsqueeze(1),
                               allow_slow_non_contiguous=True).then_inc(sem["small_landed"], 16)
            ends = pos[0, 16:SEQ].rearrange("(n s) -> n s", s=16)[:, 15:16]
            for g in range(NG):
                pool.dma_start(posi[g * NC:g * NC + NCMP, 2:3], ends,
                               allow_slow_non_contiguous=True).then_inc(sem["small_landed"], 16)
            assert len(loads) + 2 * NT == n_small
            step = [1]

            def made(ins):
                step[0] += 1
                ins.then_inc(sem["pool_step"], 1)

            made(pool.memset(ident[:, :], 0.0))
            made(pool.memset(tri[:, :], 0.0))
            made(pool.memset(cmask[:, :, :], 0.0))
            made(pool.memset(cvalid[:, :, :], 1.0))
            made(pool.memset(bdm[:, :], 1.0))
            made(pool.memset(mhalf[:, :], -0.5))
            for i in range(16):
                pool.memset(invf[:, i:i + 1], float(np.float32(1.0 / THETA ** (i / 16))))
            pool.memset(xc[:, :, :, :], 0.0)
            pool.wait_ge(sem["pool_step"], step[0])
            made(pool.affine_select(out=ident[:, :], in_=ident[:, :], compare_op=ALU.not_equal, fill=1.0, base=0,
                                    pattern=[[-1, P]], channel_multiplier=1))
            for c in (0, 2 * P):
                made(pool.affine_select(out=tri[:, c:c + P], in_=tri[:, c:c + P], compare_op=ALU.is_ge, fill=NEG,
                                        base=0, pattern=[[-1, P]], channel_multiplier=1))
            for m, fill in ((cmask, NEG), (cvalid, 0.0)):
                made(pool.affine_select(out=m[:, :, :], in_=m[:, :, :], compare_op=ALU.is_ge, fill=fill, base=-31,
                                        pattern=[[P, NT], [-16, NC]], channel_multiplier=1))
            made(pool.affine_select(out=bdm[:, :], in_=bdm[:, :], compare_op=ALU.is_ge, fill=0.0, base=0,
                                    pattern=[[-NC, NH]], channel_multiplier=1))
            pool.wait_ge(sem["pool_step"], step[0])
            pool.affine_select(out=bdm[:, :], in_=bdm[:, :], compare_op=ALU.is_ge, fill=0.0, base=NC - 1,
                               pattern=[[NC, NH]], channel_multiplier=-1).then_inc(sem["consts_made"], 1)

            def root(n_in, value, counts, col, n, scale, sig):
                pool.wait_ge(sem[n_in], value)
                for c0, c1, s in scale:
                    step[0] += 1
                    pool.tensor_scalar(msq[:, c0:c1], ssq[:, c0:c1], s, EPS, ALU.mult, ALU.add)\
                        .then_inc(sem["pool_step"], 1)
                pool.wait_ge(sem["pool_step"], step[0])
                pool.tensor_tensor(rstd[:, col:col + n], msq[:, col:col + n], mhalf[:, col:col + n], ALU.pow)\
                    .then_inc(sem[sig], 1)

            for st in steps:
                if st.kind == "norm":
                    root("ssq_made", 2 * (st.k + 1), None, 0, 2, [(0, 2, 1.0 / D)], "rstd_made")
                elif st.kind == "out" and st.group == "diff":
                    root("ob_ssq", 1, None, 0, 8, [(0, 8, 1.0 / (2 * HD))], "ob_rstd")
                elif st.kind == "latent_norm":
                    root("lat_ssq", 1, None, 0, 4, [(0, 2, 1.0 / LQ), (2, 4, 1.0 / LKV)], "lat_rstd")

        def evac_copies(what, group, t, bank, half=0):
            b = psum[bank]
            if what == "ev_in":
                if group in (2, 5):
                    return [(vals[:, group // 3, t, :], b[:, :])]
                return [(nat[:, group % 3 % 2, t, :], b[:, :])]
            if what == "uq":
                return [(qm[:, t, 4 * half:4 * half + 4, :], b[:, 0:4 * MD].rearrange("p (h d) -> p h d", h=4))]
            if what == "ukv":
                v = b[:, :].rearrange("p (h d) -> p h d", h=4)
                return [(km[:, t, 4 * half:4 * half + 4, 0:NOPE], v[:, :, 0:NOPE]),
                        (vm[:, t, 4 * half:4 * half + 4, :], v[:, :, NOPE:])]

            def twice(c):
                v = b[:, c:c + P].rearrange("p (g d) -> p g d", g=NG).unsqueeze(2)
                return v.broadcast_to([P, NG, 2, HD])

            if group == 0:
                return [(nat[:, 0, t, :], b[:, :])]
            if group == 1:
                return [(nat2[:, t, 2], twice(0)), (nat2[:, t, 3], twice(128)), (nat2[:, t, 0], twice(256)),
                        (vnsa[:, 0, t, :], b[:, 384:512])]
            if group == 2:
                return [(nat2[:, t, 1], twice(0)), (vnsa[:, 1, t, :], b[:, 128:256]),
                        (gate[:, t, :], b[:, 256:280]), (lat[:, t, 0:232], b[:, 280:512])]
            return [(lat[:, t, 232:384], b[:, 0:152]), (kpe[:, t, :], b[:, 152:184])]

        def score_operands(group, unit, part):
            if group == "mla":
                return mla_qk(unit, 0), mla_qk(unit, 1), MD ** -0.5
            if group == "diff":
                lo = 64 * part
                return qk[lo:lo + HD, 2, unit, :], qk[lo:lo + HD, 3, unit, :], HD ** -0.5
            lo = 64 * (unit % 2)
            q = qk[lo:lo + HD, 0, unit // 2, :]
            if group == "moba":
                return q, qk[lo:lo + HD, 1, unit // 2, :], HD ** -0.5
            return q, kd[lo:lo + HD, 0 if group == "slc" else 1, unit // 4, :], HD ** -0.5

        def value_operand(group, unit, kt):
            if group == "mla":
                return vm[:, kt, unit, :]
            if group == "diff":
                return vals[:, 1, kt, unit * P:(unit + 1) * P]
            if group == "moba":
                return vals[:, 0, kt, unit * HD:(unit + 1) * HD]
            g = unit // 4
            return vnsa[:, 0 if group == "slc" else 1, kt, g * HD:(g + 1) * HD]

        def source(name):
            return {"hs": hs, "o": o, "latent": lats}[name]

        def t_dst(st):
            if st.kind == "qkt":
                g, half = st.dst
                row = {0: 0, 1: 1, 3: 2, 4: 3, 6: 0}[g]
                return qk[:, row, 2 * half:2 * half + 2, :]
            return kd[:, st.which]

        def split_hi(act, slot, rounds_wait, n):
            act.wait_ge(landed[slot], rounds_wait)
            nc.scalar.activation(whi[slot][:, 0:n], raw[slot][:, 0:n], ACT.Copy).then_inc(sem["hi_made"], 1)

        def split_lo(dve, slot, count, n):
            dve.wait_ge(sem["hi_made"], count)
            nc.vector.tensor_tensor(wlo[slot][:, 0:n], raw[slot][:, 0:n], whi[slot][:, 0:n].bitcast(F32),
                                    ALU.subtract).then_inc(sem["lo_made"], 1)

        @block.tensor
        def _(pe):
            def turn(dst, src, rows=P):
                return nc.tensor.transpose(dst, src, ident[0:rows, 0:rows])

            def three(dst, a, b, first, last):
                nc.tensor.matmul(dst, a[0], b[0], start=first, stop=False)
                nc.tensor.matmul(dst, a[1], b[0], start=False, stop=False)
                return nc.tensor.matmul(dst, a[0], b[1], start=False, stop=last)

            pe.wait_ge(sem["consts_made"], 1)
            pe.wait_ge(sem["small_landed"], 16 * n_small)
            turn(psum[0][:, 0:35], grow[:, :], 35).then_inc(filled[0], 1)
            for kv in range(2):
                last = turn(psum[1][:, 32 * kv:32 * kv + 32], perow[:, kv].rearrange("t u d -> t (u d)"), 32)
            last.then_inc(filled[1], 1)

            def gate_or_up(which, lo_count, s0, i_slot, bank_sem, bank_value):
                slot = i_slot
                pe.wait_ge(sem["lo_made"], lo_count)
                if bank_sem is not None:
                    pe.wait_ge(bank_sem, bank_value)
                hi, lo = parts(whi[slot], KT, 256), parts(wlo[slot], KT, 256)
                for c in range(2):
                    cols = slice(c * P, (c + 1) * P)
                    for k in range(KT):
                        last = three(psum[which][:, c * SEQ:(c + 1) * SEQ], (hi[:, k, cols], lo[:, k, cols]),
                                     (xhi[:, k, :], xlo[:, k, :]), k == 0, k == KT - 1)
                last.then_inc(filled[which], 1)

            def down(slot, lo_count, hid_count, first, final):
                pe.wait_ge(sem["lo_made"], lo_count)
                pe.wait_ge(sem["hlo_made"], hid_count)
                hi, lo = parts(whi[slot], 2, D), parts(wlo[slot], 2, D)
                for t in range(NT):
                    for n in range(2):
                        for c in range(2):
                            rows = slice(c * SEQ + t * P, c * SEQ + (t + 1) * P)
                            cols = slice(n * 512, (n + 1) * 512)
                            last = three(psum[4 + 2 * t + n][:, :], (hhi[:, rows], hlo[:, rows]),
                                         (hi[:, c, cols], lo[:, c, cols]), first and c == 0, final and c == 1)
                        if final:
                            last.then_inc(filled[4 + 2 * t + n], 1)
                if not final:
                    last.then_inc(sem["down_done"], 1)

            for st in steps:
                if st.kind == "xt":
                    if st.src == "hs":
                        pe.wait_ge(sem["hs0_made"], st.ready)
                        pe.wait_ge(sem["hs1_made"], st.ready)
                    elif st.src == "o":
                        pe.wait_ge(sem["o_banks_read"], st.ready[0])
                        pe.wait_ge(sem["o_ready"], st.ready[1])
                    else:
                        pe.wait_ge(sem["lat_made"], 1)
                    b, w, _ = st.bank
                    wait(pe, w)
                    for i, c in enumerate(st.chunks):
                        for t in range(NT):
                            last = turn(psum[b][:, i * SEQ + t * P:i * SEQ + (t + 1) * P],
                                        source(st.src)[:, t, c * P:(c + 1) * P])
                    last.then_inc(filled[b], 1)
                elif st.kind == "proj":
                    slot = st.slab % RING
                    b, w, _ = st.bank
                    pe.wait_ge(sem["lo_made"], st.slab + 1)
                    pe.wait_ge(sem["xlo_made"], st.x_needed)
                    if st.first:
                        wait(pe, w)
                    hi, lo = parts(whi[slot], st.kts, st.width), parts(wlo[slot], st.kts, st.width)
                    rows = slice(st.t * P, (st.t + 1) * P)
                    for k in range(st.kts):
                        last = three(psum[b][:, 0:st.width], (xhi[:, st.k0 + k, rows], xlo[:, st.k0 + k, rows]),
                                     (hi[:, k, :], lo[:, k, :]), st.first and k == 0, st.last and k == st.kts - 1)
                    if st.last:
                        last.then_inc(filled[b], 1)
                    elif st.end:
                        last.then_inc(sem["slab_used"], 1)
                elif st.kind == "up":
                    slot = st.slab % RING
                    b, w, _ = st.bank
                    pe.wait_ge(sem["lo_made"], st.slab + 1)
                    pe.wait_ge(sem["xlo_made"], st.x_needed)
                    wait(pe, w)
                    hi, lo = parts(whi[slot], st.kts, st.width), parts(wlo[slot], st.kts, st.width)
                    rows = slice(st.t * P, (st.t + 1) * P)
                    n = st.width // 2
                    cols = slice(st.half * n, (st.half + 1) * n)
                    for k in range(st.kts):
                        last = three(psum[b][:, 0:n], (xhi[:, st.k0 + k, rows], xlo[:, st.k0 + k, rows]),
                                     (hi[:, k, cols], lo[:, k, cols]), k == 0, k == st.kts - 1)
                    last.then_inc(filled[b], 1)
                elif st.kind == "qkt":
                    b, w, _ = st.bank
                    pe.wait_ge(sem["roped"], st.roped)
                    wait(pe, w)
                    for i in range(2):
                        c = 2 * st.dst[1] + i
                        for t in range(NT):
                            last = turn(psum[b][:, i * SEQ + t * P:i * SEQ + (t + 1) * P],
                                        nat[:, st.buf, t, c * P:(c + 1) * P])
                    last.then_inc(filled[b], 1)
                elif st.kind in ("kdt", "blocks"):
                    b, w, _ = st.bank
                    pe.wait_ge(sem["evac_made"], st.evac)
                    if st.kind == "kdt":
                        pe.wait_ge(sem["roped"], st.roped)
                    which = st.which if st.kind == "kdt" else 2 + st.kv
                    wait(pe, w)
                    for g in range(NG):
                        for t in range(NT):
                            last = turn(psum[b][:, g * SEQ + t * P:g * SEQ + (t + 1) * P],
                                        nat2[:, t, which, g].rearrange("p u d -> p (u d)"))
                    last.then_inc(filled[b], 1)
                elif st.kind == "mqkt":
                    b, w, _ = st.bank
                    pe.wait_ge(sem["roped"], st.roped)
                    pe.wait_ge(sem["kpe_spread"], 1)
                    wait(pe, w)
                    for i, src in enumerate((qm, km)):
                        for t in range(NT):
                            last = turn(psum[b][0:MD, i * SEQ + t * P:i * SEQ + (t + 1) * P], src[:, t, st.head, :])
                    last.then_inc(filled[b], 1)
                elif st.kind == "scores":
                    b, w, _ = st.bank
                    q, k, _ = score_operands(st.group, st.unit, st.part)
                    pe.wait_ge(sem["t_made"], st.needs)
                    wait(pe, w)
                    nc.tensor.matmul(psum[b][:, 0:P], q[:, 0:P], k[:, 0:P], start=True, stop=True)
                    nc.tensor.matmul(psum[b][:, P:3 * P], q[:, P:2 * P], k, start=True, stop=True)\
                        .then_inc(filled[b], 1)
                elif st.kind == "turn":
                    b, w, _ = st.bank
                    if st.diff:
                        pe.wait_ge(sem["combined"], st.combined)
                        src = comb[:, st.unit % 2, :]
                    else:
                        pe.wait_ge(sem["exped"], 2 * (st.maps[0] + 1))
                        src = prob[:, st.maps[0] % 4, :]
                    wait(pe, w)
                    for i in range(3):
                        last = turn(psum[b][:, i * P:(i + 1) * P], src[:, i * P:(i + 1) * P])
                    last.then_inc(filled[b], 1)
                elif st.kind == "value":
                    pe.wait_ge(sem[f"pt_made{st.uid % 2}"], st.pt)
                    pe.wait_ge(sem["evac_made"], st.needs)
                    if st.first:
                        wait(pe, st.banks[0][1])
                        wait(pe, st.banks[1][1])
                    v0, v1 = value_operand(st.group, st.unit, 0), value_operand(st.group, st.unit, 1)
                    n = v0.shape[-1]
                    cols = slice(st.unit * n, (st.unit + 1) * n)
                    w = pt[:, st.uid % 2, :]
                    m0 = nc.tensor.matmul(psum[4][:, cols], w[:, 0:P], v0, start=True, stop=True)
                    nc.tensor.matmul(psum[5][:, cols], w[:, P:2 * P], v0, start=True, stop=False)
                    m1 = nc.tensor.matmul(psum[5][:, cols], w[:, 2 * P:3 * P], v1, start=False, stop=True)
                    if st.last:
                        m0.then_inc(filled[4], 1)
                        m1.then_inc(filled[5], 1)
                    else:
                        m1.then_inc(sem["pv_done"], 1)
                elif st.kind == "compress":
                    slot = st.slab % RING
                    pe.wait_ge(sem["lo_made"], st.slab + 1)
                    pe.wait_ge(sem["xc_lo_made"], st.x_needed)
                    hi, lo = parts(whi[slot], 8, 256), parts(wlo[slot], 8, 256)
                    for c in range(2):
                        if st.half == 0:
                            wait(pe, st.banks[c][1])
                        cols = slice(c * P, (c + 1) * P)
                        for j in range(8):
                            jj = 8 * st.half + j
                            last = three(psum[c][:, 0:NG * NC], (hi[:, j, cols], lo[:, j, cols]),
                                         (xch[:, st.kv, jj, :], xcl[:, st.kv, jj, :]), jj == 0, jj == 15)
                        if st.half:
                            last.then_inc(filled[c], 1)
                    if not st.half:
                        last.then_inc(sem["slab_used"], 1)
                elif st.kind == "second":
                    b, w, _ = st.bank
                    pe.wait_ge(sem["gelu_out"], st.kv + 1)
                    wait(pe, w)
                    for c in range(2):
                        lhs = hk[:, c, :] if st.kv == 0 else hv[:, c].rearrange("p h n -> p (h n)")
                        m = lhs.shape[-1]
                        last = nc.tensor.matmul(psum[b][0:m, 0:HD], lhs, w2[:, st.kv, c, :],
                                                start=c == 0, stop=c == 1)
                    last.then_inc(filled[b], 1)
                elif st.kind == "kcmp":
                    b, w, _ = st.bank
                    pe.wait_ge(sem["roped"], st.roped)
                    wait(pe, w)
                    turn(psum[b][:, 0:NG * NC], kcn[:, :, :].rearrange("p u d -> p (u d)"), NG * NC)\
                        .then_inc(filled[b], 1)
                elif st.kind == "cscores":
                    pe.wait_ge(sem["t_made"], st.t_needed)
                    for par in range(2):
                        b, w, _ = st.banks[par]
                        wait(pe, w)
                        for t in range(NT):
                            for j in range(NH // 2):
                                g = j // 2
                                at = (t * 4 + j) * NC
                                last = nc.tensor.matmul(
                                    psum[b][:, at:at + NC], qk[64 * par:64 * par + HD, 0, j, t * P:(t + 1) * P],
                                    kct[64 * par:64 * par + HD, g * NC:(g + 1) * NC], start=True, stop=True)
                        last.then_inc(filled[b], 1)
                elif st.kind == "cturn":
                    b, w, _ = st.bank
                    pe.wait_ge(sem["c_ready"], 1)
                    wait(pe, w)
                    for t in range(NT):
                        last = turn(psum[b][:, t * P:(t + 1) * P], cs[:, t].rearrange("p h n -> p (h n)"))
                    last.then_inc(filled[b], 1)
                elif st.kind == "cvalue":
                    pe.wait_ge(sem["pct_made"], 1)
                    for t in range(NT):
                        b, w, _ = st.banks[t]
                        wait(pe, w)
                        nc.tensor.matmul(psum[b][:, :], pct[:, t, :], vbd[:, :, :].rearrange("p h d -> p (h d)"),
                                         start=True, stop=True).then_inc(filled[b], 1)
                elif st.kind == "ffn":
                    s0, g0, u0, base = st.s0, st.g0, st.u0, st.base
                    pe.wait_ge(sem["xlo_made"], st.x_needed)
                    wait(pe, st.gate_wait)
                    gate_or_up(0, s0 + 1, s0, s0 % RING, None, None)
                    wait(pe, st.up_wait)
                    gate_or_up(1, s0 + 2, s0, (s0 + 1) % RING, None, None)

                    def body(i, first):
                        a = i * RING + (s0 - 1)
                        gate_or_up(0, a + 1, s0, (s0 + 2) % RING, sem["gated"], i + base)
                        gate_or_up(1, a + 2, s0, (s0 + 3) % RING, sem["h_made"], i + base)
                        down((s0 + 4) % RING, a + 3, i + base, first, False)

                    for o_use in st.out:
                        wait(pe, o_use[1])
                    body(1, True)
                    with pe.Fori(2, NI) as i:
                        body(i, False)
                    down((s0 + 3 * NI - 1) % RING, s0 + 3 * NI, base + NI, False, True)

        @block.scalar
        def _(act):
            A = nc.scalar.activation

            def next_split(k):
                s = k + RING
                if s < n_slabs:
                    wait(act, slabs[k].released)
                    split_hi(act, s % RING, 16 * (s // RING + 1), slabs[s].n)

            for st in steps:
                if st.kind == "norm":
                    if st.k == 0:
                        act.wait_ge(sem["x_landed"], 16)
                    else:
                        act.wait_ge(sem["h_ready"], st.h_needed)
                    A(hs[:, 1, :], h[:, 1, :], ACT.Square, accum_out=ssq[:, 1:2]).then_inc(sem["ssq_made"], 1)
                    if st.k < 4:
                        act.wait_ge(sem["rstd_made"], st.k + 1)
                        A(hs[:, 1, :], h[:, 1, :], ACT.Copy, scale=rstd[:, 1:2]).then_inc(sem["hs1_made"], 1)
                    if st.k == 0:
                        act.wait_ge(filled[0], 1)
                        A(gains[:, :], psum[0][:, 0:35], ACT.Copy).then_inc(sem["small_made"], 1)
                        act.wait_ge(filled[1], 1)
                        A(pet[:, :, :].rearrange("p a b -> p (a b)"), psum[1][:, 0:64], ACT.Copy)\
                            .then_inc(sem["small_made"], 1)
                        split_hi(act, 0, 16, slabs[0].n)
                elif st.kind == "xt":
                    b = st.bank[0]
                    if st.n == 1:
                        act.wait_ge(sem["small_made"], 2)
                    bank_filled(act, st.bank)
                    if st.gain is None:
                        A(xhi[:, st.chunks[0]:st.chunks[0] + 2, :].rearrange("p k n -> p (k n)"), psum[b][:, :],
                          ACT.Copy).then_inc(sem["xhi_made"], 1)
                    else:
                        for i, c in enumerate(st.chunks):
                            last = A(xhi[:, c, :], psum[b][:, i * SEQ:(i + 1) * SEQ], ACT.Copy,
                                     scale=gains[:, st.gain + c:st.gain + c + 1])
                        last.then_inc(sem["xhi_made"], 1)
                elif st.kind in ("proj", "up"):
                    if st.acc == "evac_made" and (st.kind == "up" or st.last):
                        if st.kind == "proj" and st.what == "ev_in" and st.group in (3, 4):
                            act.wait_ge(sem["t_made"], 2 * (st.group - 2))
                        bank_filled(act, st.bank)
                        for dst, src in evac_copies(st.what, st.group if st.kind == "proj" else 0, st.t, st.bank[0],
                                                    0 if st.kind == "proj" else st.half):
                            last = A(dst, src, ACT.Copy)
                        last.then_inc(sem["evac_made"], 1)
                    if st.end:
                        next_split(st.slab)
                elif st.kind in ("qkt", "kdt"):
                    bank_filled(act, st.bank)
                    A(t_dst(st), psum[st.bank[0]][:, :].rearrange("p (a n) -> p a n", a=2), ACT.Copy)\
                        .then_inc(sem["t_made"], 1)
                elif st.kind == "mqkt":
                    bank_filled(act, st.bank)
                    b = psum[st.bank[0]]
                    A(mla_qk(st.head, 0), b[0:MD, 0:SEQ], ACT.Copy)
                    A(mla_qk(st.head, 1), b[0:MD, SEQ:], ACT.Copy).then_inc(sem["t_made"], 1)
                elif st.kind == "tables":
                    for s in range(1, RING):
                        split_hi(act, s, 16, slabs[s].n)
                    act.wait_ge(sem["angles_made"], 1)
                    A(trig[:, :, :, :].rearrange("p a b c -> p (a b c)"),
                      red[:, :, :, :].rearrange("p a b c -> p (a b c)"), ACT.Sin).then_inc(sem["sin_made"], 1)
                    act.wait_ge(sem["lam_dots"], 1)
                    A(lam[:, 2:4], lam[:, 0:2], ACT.Exp).then_inc(sem["lam_exp"], 1)
                elif st.kind == "scores":
                    m = st.m
                    if m >= 4:
                        wait(act, prob_free[m - 4])
                    for t, cols in ((0, slice(0, P)), (1, slice(P, 3 * P))):
                        act.wait_ge(sem["masked"], 2 * m + t + 1)
                        A(prob[:, m % 4, cols], masked[:, m % 2, cols], ACT.Exp, bias=nmax[:, 2 * m + t:2 * m + t + 1],
                          scale=-1.0, accum_out=sums[:, 2 * m + t:2 * m + t + 1]).then_inc(sem["exped"], 1)
                elif st.kind == "turn" and st.diff:
                    bank_filled(act, st.bank)
                    wait(act, st.pv_before)
                    A(pt[:, st.uid % 2, :], psum[st.bank[0]][:, 0:SCORE_COLS], ACT.Copy)\
                        .then_inc(sem[f"pt_made{st.uid % 2}"], 1)
                elif st.kind == "blocks":
                    act.wait_ge(sem["xc_made"], st.kv + 1)
                    A(xch[:, st.kv].rearrange("p j n -> p (j n)"), xc[:, :, :, :].rearrange("p j g n -> p (j g n)"),
                      ACT.Copy).then_inc(sem["xch_made"], 1)
                elif st.kind == "compress":
                    if st.half:
                        for c in range(2):
                            bank_filled(act, st.banks[c])
                            last = A(hid[:, c, :], psum[c][:, 0:NG * NC], ACT.Copy)
                        last.then_inc(sem["hid_read"], 1)
                    next_split(st.slab)
                elif st.kind == "second":
                    act.wait_ge(sem["gelu_in"], st.kv + 1)
                    A(hid3[:, :, :], hid2[:, :, :], ACT.Tanh, scale=float(np.sqrt(2 / np.pi)))\
                        .then_inc(sem["gelu_th"], 1)
                    if st.kv == 0:
                        bank_filled(act, st.bank)
                        src = psum[st.bank[0]][0:NG * NC, 0:HD].unsqueeze(1).broadcast_to([NG * NC, 2, HD])
                        A(kcn[:, :, :], src, ACT.Copy).then_inc(sem["t_made"], 1)
                elif st.kind == "kcmp":
                    bank_filled(act, st.bank)
                    A(kct[:, :], psum[st.bank[0]][:, 0:NG * NC], ACT.Copy).then_inc(sem["t_made"], 1)
                elif st.kind == "cscores":
                    act.wait_ge(sem["c_centred"], 1)
                    A(cs[:, :, :, :].rearrange("p t h n -> p (t h n)"), cs[:, :, :, :].rearrange("p t h n -> p (t h n)"),
                      ACT.Exp, scale=HD ** -0.5).then_inc(sem["c_exped"], 1)
                elif st.kind == "cturn":
                    bank_filled(act, st.bank)
                    A(pct[:, :, :].rearrange("p t n -> p (t n)"), psum[st.bank[0]][:, 0:NT * P], ACT.Copy)\
                        .then_inc(sem["pct_made"], 1)
                elif st.kind == "gates":
                    act.wait_ge(sem["gate_in"], 1)
                    A(gate[:, :, :], gate[:, :, :], ACT.Tanh, scale=0.5).then_inc(sem["gate_th"], 1)
                elif st.kind == "ffn":
                    s0, g0, u0, base = st.s0, st.g0, st.u0, st.base

                    def tanh(i):
                        act.wait_ge(filled[0], i + (g0 + 1))
                        if not isinstance(i, int) or base + i > 0:
                            act.wait_ge(sem["gated"], i + base)
                        A(th[:, :], psum[0][:, :], ACT.Tanh, scale=0.5).then_inc(sem["tanh_made"], 1)

                    def hidden(i):
                        act.wait_ge(sem["h_made"], i + (base + 1))
                        A(hhi[:, :], hf[:, :], ACT.Copy).then_inc(sem["hhi_made"], 1)

                    def body(i, more=True):
                        r = i * 16
                        q = [(s0 - 1 + RING + j) for j in range(3)]
                        tanh(i)
                        if more or s0 - 1 + 3 * i + RING < n_slabs:
                            split_hi(act, q[0] % RING, r + 16 * (q[0] // RING + 1), SLAB)
                        if more or s0 + 3 * i + RING < n_slabs:
                            act.wait_ge(filled[1], i + (u0 + 1))
                            split_hi(act, q[1] % RING, r + 16 * (q[1] // RING + 1), SLAB)
                        act.wait_ge(sem["down_done"], down_at + i)
                        hidden(i)
                        if more or s0 + 1 + 3 * i + RING < n_slabs:
                            split_hi(act, q[2] % RING, r + 16 * (q[2] // RING + 1), SLAB)

                    down_at = st.down_base
                    tanh(0)
                    split_hi(act, (s0 + 3) % RING, 16 * ((s0 + 3) // RING + 1), SLAB)
                    act.wait_ge(filled[1], u0 + 1)
                    split_hi(act, (s0 + 4) % RING, 16 * ((s0 + 4) // RING + 1), SLAB)
                    hidden(0)
                    body(1)
                    with act.Fori(2, NI - 1) as i:
                        body(i)
                    body(NI - 1, more=False)
                    next_split(s0 + 3 * NI - 1)

        @block.vector
        def _(dve):
            V = nc.vector
            step = [0]

            def link(ins):
                step[0] += 1
                ins.then_inc(sem["dve_step"], 1)
                dve.wait_ge(sem["dve_step"], step[0])

            def next_split(k):
                s = k + RING
                if s < n_slabs:
                    split_lo(dve, s % RING, s + 1, slabs[s].n)

            def rope(x, cos, sin, w, n):
                if n > 1:
                    dve.wait_ge(sem["roped"], n - 1)
                r = w // 2
                shape = list(x.shape)
                a = rope_a[0:shape[0], 0:shape[1], 0:shape[2], 0:w]
                b = rope_b[0:shape[0], 0:shape[1], 0:shape[2], 0:w]

                def per_head(t):
                    return t.unsqueeze(2).broadcast_to(shape[:3] + [t.shape[-1]])

                V.tensor_tensor(a, x, per_head(cos), ALU.mult)
                V.tensor_tensor(b[:, :, :, 0:r], x[:, :, :, r:w], per_head(sin[:, :, 0:r]), ALU.mult)
                link(V.tensor_tensor(b[:, :, :, r:w], x[:, :, :, 0:r], per_head(sin[:, :, r:w]), ALU.mult))
                V.tensor_tensor(x, a, b, ALU.add).then_inc(sem["roped"], 1)

            for st in steps:
                if st.kind == "norm":
                    if st.k == 0:
                        dve.wait_ge(sem["x_landed"], 16)
                    else:
                        dve.wait_ge(sem["h_ready"], st.h_needed)
                    V.tensor_tensor_reduce(hs[:, 0, :], h[:, 0, :], h[:, 0, :], 1.0, 0.0, ALU.mult, ALU.add,
                                           ssq[:, 0:1]).then_inc(sem["ssq_made"], 1)
                    dve.wait_ge(sem["rstd_made"], st.k + 1)
                    if st.k < 4:
                        V.tensor_scalar(hs[:, 0, :], h[:, 0, :], rstd[:, 0:1], None, ALU.mult)\
                            .then_inc(sem["hs0_made"], 1)
                    else:
                        for t in range(NT):
                            V.scalar_tensor_tensor(hs[:, t, :], h[:, t, :], rstd[:, t:t + 1], gfin[:, :], ALU.mult,
                                                   ALU.mult).then_inc(sem["fin_made"], 1)
                    if st.k == 0:
                        split_lo(dve, 0, 1, slabs[0].n)
                elif st.kind == "xt":
                    b = st.bank[0]
                    dve.wait_ge(sem["xhi_made"], st.n)
                    if st.gain is None:
                        c = st.chunks[0]
                        V.tensor_tensor(xlo[:, c:c + 2, :].rearrange("p k n -> p (k n)"), psum[b][:, :],
                                        xhi[:, c:c + 2, :].rearrange("p k n -> p (k n)").bitcast(F32),
                                        ALU.subtract).then_inc(sem["xlo_made"], 1)
                    else:
                        for i, c in enumerate(st.chunks):
                            last = V.scalar_tensor_tensor(
                                xlo[:, c, :], psum[b][:, i * SEQ:(i + 1) * SEQ],
                                gains[:, st.gain + c:st.gain + c + 1], xhi[:, c, :].bitcast(F32), ALU.mult,
                                ALU.subtract)
                        last.then_inc(sem["xlo_made"], 1)
                elif st.kind == "tables":
                    for s in range(1, RING):
                        split_lo(dve, s, s + 1, slabs[s].n)
                    dve.wait_ge(sem["small_landed"], 16 * n_small)
                    dve.wait_ge(sem["consts_made"], 1)
                    link(V.tensor_copy(posf[:, :], posi[:, :]))
                    link(V.tensor_tensor(ang[:, :, :], posf[:, :].unsqueeze(2).broadcast_to([P, 3, 16]),
                                         invf[:, :].unsqueeze(1).broadcast_to([P, 3, 16]), ALU.mult))
                    link(V.tensor_scalar(turns[:, :, :], ang[:, :, :], 1.0 / (2 * np.pi), ROUND, ALU.mult, ALU.add))
                    link(V.tensor_scalar(turns[:, :, :], turns[:, :, :], ROUND, None, ALU.subtract))
                    for part in TWO_PI_PARTS:
                        link(V.scalar_tensor_tensor(ang[:, :, :], turns[:, :, :], -part, ang[:, :, :], ALU.mult,
                                                    ALU.add))
                    link(V.tensor_scalar(red[:, 0], ang[:, :, :], 3.1415925, -3.1415925, ALU.min, ALU.max))
                    link(V.scalar_tensor_tensor(ang[:, :, :], red[:, 0], -1.0, red[:, 0], ALU.mult, ALU.max))
                    V.tensor_scalar(red[:, 1], ang[:, :, :], -1.0, PI / 2, ALU.mult, ALU.add)\
                        .then_inc(sem["angles_made"], 1)
                    for j in range(2):
                        last = V.tensor_tensor_reduce(otmp[:, j * HD:(j + 1) * HD], lqk[:, 2 * j], lqk[:, 2 * j + 1], 1.0, 0.0,
                                                      ALU.mult, ALU.add, lam[:, j:j + 1])
                    last.then_inc(sem["lam_dots"], 1)
                    V.tensor_scalar(subln[:, :], subln[:, :], 1.0 - LAMBDA_INIT, None, ALU.mult)
                    dve.wait_ge(sem["sin_made"], 1)
                    for cc, sn, w, every in ((cc8, sn8, 16, 2), (cc16, sn16, 32, 1)):
                        r = w // 2
                        s_, c_ = trig[:, 0, :, 0:16:every], trig[:, 1, :, 0:16:every]
                        V.tensor_copy(cc[:, :, 0:r], c_)
                        V.tensor_copy(cc[:, :, r:w], c_)
                        V.tensor_scalar(sn[:, :, 0:r], s_, -1.0, None, ALU.mult)
                        link(V.tensor_copy(sn[:, :, r:w], s_))
                    dve.wait_ge(sem["lam_exp"], 1)
                    link(V.scalar_tensor_tensor(lam[:, 0:1], lam[:, 2:3], -1.0, lam[:, 3:4], ALU.mult, ALU.add))
                    link(V.tensor_scalar(lam[:, 0:1], lam[:, 0:1], -LAMBDA_INIT, None, ALU.add))
                elif st.kind in ("proj", "up"):
                    if st.kind == "proj" and st.acc == "h_ready" and st.last:
                        bank_filled(dve, st.bank)
                        cols = slice(st.group * 512, (st.group + 1) * 512)
                        V.tensor_tensor(h[:, st.t, cols], psum[st.bank[0]][:, :], h[:, st.t, cols], ALU.add)\
                            .then_inc(sem["h_ready"], 1)
                    if st.end:
                        next_split(st.slab)
                elif st.kind == "rope":
                    dve.wait_ge(sem["evac_made"], st.evac)
                    if st.what == "nat":
                        v = nat[:, st.buf].rearrange("p t (h d) -> p t h d", d=HD)
                        rope(v[:, :, :, 0:16], cc8[:, 0:NT, :], sn8[:, 0:NT, :], 16, st.n)
                    elif st.what in ("kslc", "kwin"):
                        w = 0 if st.what == "kslc" else 1
                        v = nat2[:, :, w].rearrange("p t g u d -> p t (g u) d")
                        rope(v[:, :, :, 0:16], cc8[:, 0:NT, :], sn8[:, 0:NT, :], 16, st.n)
                    elif st.what == "kpe":
                        rope(kpe[:, :, :].unsqueeze(2), cc16[:, 0:NT, :], sn16[:, 0:NT, :], RO, st.n)
                        dve.wait_ge(sem["roped"], st.n)
                        for t in range(NT):
                            last = V.tensor_copy(km[:, t, :, NOPE:], kpe[:, t].unsqueeze(1).broadcast_to([P, NH, RO]))
                        last.then_inc(sem["kpe_spread"], 1)
                    else:
                        rope(qm[:, :, :, NOPE:], cc16[:, 0:NT, :], sn16[:, 0:NT, :], RO, st.n)
                elif st.kind == "scores":
                    m, b = st.m, psum[st.bank[0]]
                    bank_filled(dve, st.bank)
                    if m >= 2:
                        dve.wait_ge(sem["exped"], 2 * (m - 1))
                    scale = score_operands(st.group, st.unit, st.part)[2]
                    for t, cols in ((0, slice(0, P)), (1, slice(P, 3 * P))):
                        V.tensor_tensor_reduce(masked[:, m % 2, cols], b[:, cols], tri[:, cols], -scale, 3e38, ALU.add,
                                               ALU.min, nmax[:, 2 * m + t:2 * m + t + 1]).then_inc(sem["masked"], 1)
                elif st.kind == "turn":
                    if st.diff:
                        m0, m1 = st.maps
                        dve.wait_ge(sem["exped"], 2 * (m1 + 1))
                        c = slice(2 * m0, 2 * m0 + 4)
                        link(V.tensor_scalar(rinv[:, c], sums[:, c], 1e-30, None, ALU.max))
                        link(V.reciprocal(rinv[:, c], rinv[:, c]))
                        link(V.tensor_scalar(rinv[:, 2 * m1:2 * m1 + 2], rinv[:, 2 * m1:2 * m1 + 2], lam[:, 0:1], None,
                                             ALU.mult))
                        if st.unit >= 2:
                            wait(dve, comb_free[st.unit - 2])
                        for t, cols in ((0, slice(0, P)), (1, slice(P, 3 * P))):
                            ins = V.tensor_scalar(comb[:, st.unit % 2, cols], prob[:, m0 % 4, cols],
                                                  rinv[:, 2 * m0 + t:2 * m0 + t + 1], None, ALU.mult)
                        link(ins)
                        for t, cols in ((0, slice(0, P)), (1, slice(P, 3 * P))):
                            ins = V.scalar_tensor_tensor(comb[:, st.unit % 2, cols], prob[:, m1 % 4, cols],
                                                         rinv[:, 2 * m1 + t:2 * m1 + t + 1],
                                                         comb[:, st.unit % 2, cols], ALU.mult, ALU.add)
                        ins.then_inc(sem["combined"], 1)
                    else:
                        bank_filled(dve, st.bank)
                        wait(dve, st.pv_before)
                        V.tensor_copy(pt[:, st.uid % 2, :], psum[st.bank[0]][:, 0:SCORE_COLS])\
                            .then_inc(sem[f"pt_made{st.uid % 2}"], 1)
                elif st.kind == "out":
                    bank_filled(dve, st.banks[0])
                    bank_filled(dve, st.banks[1])
                    if st.group == "diff":
                        ob = o[:, :, 512:1024]
                        for t in range(NT):
                            last = V.tensor_copy(ob[:, t, :], psum[4 + t][:, :])
                            last.then_inc(sem["o_banks_read"], 1)
                        dve.wait_ge(sem["o_banks_read"], st.read)
                        for t in range(NT):
                            last = V.tensor_tensor(nat[:, 0, t, :], ob[:, t, :], ob[:, t, :],
                                                   ALU.mult)
                        link(last)
                        V.tensor_reduce(ssq[:, 0:8], nat[:, 0].rearrange("p t n -> p (t n)").rearrange("p (a d) -> p a d", d=2 * HD), AX.X,
                                        ALU.add).then_inc(sem["ob_ssq"], 1)
                        dve.wait_ge(sem["ob_rstd"], 1)
                        for t in range(NT):
                            v = ob[:, t, :].rearrange("p (a d) -> p a d", d=2 * HD)
                            r = rstd[:, 4 * t:4 * t + 4].unsqueeze(2).broadcast_to([P, NDH, 2 * HD])
                            last = V.tensor_tensor(v, v, r, ALU.mult)
                        link(last)
                        for t in range(NT):
                            v = ob[:, t, :].rearrange("p (a d) -> p a d", d=2 * HD)
                            g = subln[:, :].unsqueeze(1).broadcast_to([P, NDH, 2 * HD])
                            last = V.tensor_tensor(v, v, g, ALU.mult)
                        last.then_inc(sem["o_ready"], 1)
                        continue
                    if st.group == "cmp":
                        src = csum[:, :].rearrange("p (t h) -> p t h", t=NT)
                    else:
                        dve.wait_ge(sem["exped"], 2 * (st.maps[-1] + 1))
                        c = slice(2 * st.maps[0], 2 * st.maps[-1] + 2)
                        src = sums[:, c].rearrange("p (h t) -> p t h", t=NT)
                    link(V.tensor_scalar(coef[:, :, :], src, 1e-30, None, ALU.max))
                    link(V.reciprocal(coef[:, :, :], coef[:, :, :]))
                    branch = {"cmp": 0, "slc": 1, "win": 2}.get(st.group)
                    if branch is not None:
                        dve.wait_ge(sem["gates_made"], 1)
                        gv = gate[:, :, :].rearrange("p t (h b) -> p t h b", b=3)[:, :, :, branch]
                        link(V.tensor_tensor(coef[:, :, :], coef[:, :, :], gv, ALU.mult))
                    lo = 512 if st.group == "mla" else 0
                    for t in range(NT):
                        v = psum[4 + t][:, :].rearrange("p (h d) -> p h d", d=HD)
                        c = coef[:, t].unsqueeze(2).broadcast_to([P, NH, HD])
                        if st.group in ("win", "cmp"):
                            V.tensor_tensor(otmp[:, :].rearrange("p (h d) -> p h d", d=HD), v, c, ALU.mult)\
                                .then_inc(sem["o_banks_read"], 1)
                            dve.wait_ge(sem["o_banks_read"], st.read - NT + t + 1)
                            add = V.tensor_tensor(o[:, t, 0:512], o[:, t, 0:512], otmp[:, :], ALU.add)
                            if st.group == "cmp" and t == NT - 1:
                                add.then_inc(sem["o_ready"], 1)
                            else:
                                link(add)
                        else:
                            V.tensor_tensor(o[:, t, lo:lo + 512].rearrange("p (h d) -> p h d", d=HD), v, c, ALU.mult)\
                                .then_inc(sem["o_banks_read"], 1)
                    dve.wait_ge(sem["o_banks_read"], st.read)
                elif st.kind == "blocks":
                    b = psum[st.bank[0]]
                    bank_filled(dve, st.bank)
                    if st.kv == 0:
                        dve.wait_ge(sem["small_made"], 2)
                    else:
                        dve.wait_ge(sem["xch_made"], 1)
                        dve.wait_ge(sem["xc_lo_made"], 1)
                    v = b[:, :].rearrange("p (g n s) -> p s g n", g=NG, s=16)
                    for par in range(2):
                        rows = slice(64 * par, 64 * par + 64)
                        for late in range(2):
                            pe_cols = pet[rows, st.kv, 16 * late + par:16 * late + 16:2]
                            last = V.tensor_tensor(
                                xc[rows, 8 * late:8 * late + 8, :, 0:NCMP], v[rows, par:16:2, :, late:late + NCMP],
                                pe_cols.unsqueeze(2).unsqueeze(3).broadcast_to([64, 8, NG, NCMP]), ALU.add)
                    last.then_inc(sem["xc_made"], 1)
                    dve.wait_ge(sem["xch_made"], st.kv + 1)
                    dve.wait_ge(sem["xc_made"], st.kv + 1)
                    V.tensor_tensor(xcl[:, st.kv].rearrange("p j n -> p (j n)"),
                                    xc[:, :, :, :].rearrange("p j g n -> p (j g n)"),
                                    xch[:, st.kv].rearrange("p j n -> p (j n)").bitcast(F32), ALU.subtract)\
                        .then_inc(sem["xc_lo_made"], 1)
                elif st.kind == "compress":
                    next_split(st.slab)
                elif st.kind == "second":
                    dve.wait_ge(sem["hid_read"], st.hid)
                    link(V.tensor_tensor(hid2[:, :, :], hid[:, :, :], hid[:, :, :], ALU.mult))
                    link(V.tensor_scalar(hid2[:, :, :], hid2[:, :, :], 0.044715, 1.0, ALU.mult, ALU.add))
                    V.tensor_tensor(hid2[:, :, :], hid2[:, :, :], hid[:, :, :], ALU.mult).then_inc(sem["gelu_in"], 1)
                    dve.wait_ge(sem["gelu_th"], st.kv + 1)
                    link(V.scalar_tensor_tensor(hid3[:, :, :], hid3[:, :, :], 1.0, hid[:, :, :], ALU.add, ALU.mult))
                    if st.kv == 0:
                        V.tensor_scalar(hk[:, :, :], hid3[:, :, :], 0.5, None, ALU.mult).then_inc(sem["gelu_out"], 1)
                    else:
                        v = hid3[:, :, :].rearrange("p c (g n) -> p (c g) n", g=NG).unsqueeze(2)
                        V.tensor_scalar(hv[:, :, :, :].rearrange("p c (g r) n -> p (c g) r n", g=NG),
                                        v.broadcast_to([P, 2 * NG, NH // NG, NC]), 0.5, None, ALU.mult)\
                            .then_inc(sem["gelu_out"], 1)
                        bank_filled(dve, st.bank)
                        src = psum[st.bank[0]][:, 0:HD].unsqueeze(1).broadcast_to([P, NH, HD])
                        V.tensor_tensor(vbd[:, :, :], src, bdm[:, :].unsqueeze(2).broadcast_to([P, NH, HD]), ALU.mult)\
                            .then_inc(sem["t_made"], 1)
                elif st.kind == "kcmp":
                    dve.wait_ge(sem["t_made"], st.evac)
                    rope(kcn[:, :, 0:16].unsqueeze(1), cc8[0:NG * NC, 2:3, :], sn8[0:NG * NC, 2:3, :], 16, st.roped)
                elif st.kind == "cscores":
                    for par in range(2):
                        bank_filled(dve, st.banks[par])
                        v = psum[st.banks[par][0]][:, 0:NT * 4 * NC].rearrange("p (t j n) -> p t j n", t=NT, n=NC)
                        dst = cs[:, :, :, :].rearrange("p t (j u) n -> p t j u n", u=2)[:, :, :, par]
                        V.tensor_tensor(dst, v, cmask[:, :, :].unsqueeze(2).broadcast_to([P, NT, 4, NC]), ALU.add)\
                            .then_inc(sem["c_masked"], 1)
                    dve.wait_ge(sem["c_masked"], 2)
                    rows = cs[:, :, :, :].rearrange("p t h n -> p (t h) n")
                    link(V.tensor_reduce(cmx[:, :], rows, AX.X, ALU.max))
                    V.tensor_tensor(rows, rows, cmx[:, :].unsqueeze(2).broadcast_to([P, NT * NH, NC]), ALU.subtract)\
                        .then_inc(sem["c_centred"], 1)
                    dve.wait_ge(sem["c_exped"], 1)
                    link(V.tensor_tensor(cs[:, :, :, :], cs[:, :, :, :],
                                         cvalid[:, :, :].unsqueeze(2).broadcast_to([P, NT, NH, NC]), ALU.mult))
                    V.tensor_reduce(csum[:, :], rows, AX.X, ALU.add).then_inc(sem["c_ready"], 1)
                elif st.kind == "gates":
                    dve.wait_ge(sem["evac_made"], st.evac)
                    V.tensor_tensor(gate[:, :, :], gate[:, :, :],
                                    gateb[:, :].unsqueeze(1).broadcast_to([P, NT, NH * 3]), ALU.add)\
                        .then_inc(sem["gate_in"], 1)
                    dve.wait_ge(sem["gate_th"], 1)
                    V.tensor_scalar(gate[:, :, :], gate[:, :, :], 1.0, 0.5, ALU.add, ALU.mult)\
                        .then_inc(sem["gates_made"], 1)
                elif st.kind == "latent_norm":
                    dve.wait_ge(sem["evac_made"], st.evac)
                    for j, (lo, hi) in enumerate(((0, LQ), (LQ, LQ + LKV))):
                        for t in range(NT):
                            last = V.tensor_tensor_reduce(lats[:, t, lo:hi], lat[:, t, lo:hi], lat[:, t, lo:hi],
                                                          1.0, 0.0, ALU.mult, ALU.add,
                                                          ssq[:, 2 * j + t:2 * j + t + 1])
                    last.then_inc(sem["lat_ssq"], 1)
                    dve.wait_ge(sem["lat_rstd"], 1)
                    for j, (lo, hi) in enumerate(((0, LQ), (LQ, LQ + LKV))):
                        for t in range(NT):
                            last = V.tensor_scalar(lats[:, t, lo:hi], lat[:, t, lo:hi],
                                                   rstd[:, 2 * j + t:2 * j + t + 1], None, ALU.mult)
                    last.then_inc(sem["lat_made"], 1)
                elif st.kind == "ffn":
                    s0, u0, base = st.s0, st.u0, st.base

                    def gated(i):
                        dve.wait_ge(sem["tanh_made"], i + (base + 1))
                        V.scalar_tensor_tensor(ga[:, :], th[:, :], 1.0, psum[0][:, :], ALU.add, ALU.mult)\
                            .then_inc(sem["gated"], 1)

                    def hidden(i):
                        dve.wait_ge(filled[1], i + (u0 + 1))
                        dve.wait_ge(sem["gated"], i + (base + 1))
                        V.scalar_tensor_tensor(hf[:, :], ga[:, :], 0.5, psum[1][:, :], ALU.mult, ALU.mult)\
                            .then_inc(sem["h_made"], 1)

                    def hidden_lo(i):
                        dve.wait_ge(sem["hhi_made"], i + (base + 1))
                        V.tensor_tensor(hlo[:, :], hf[:, :], hhi[:, :].bitcast(F32), ALU.subtract)\
                            .then_inc(sem["hlo_made"], 1)

                    def body(i, more=True):
                        r = i * RING
                        gated(i)
                        if more or s0 - 1 + 3 * i + RING < n_slabs:
                            split_lo(dve, (s0 + 2) % RING, r + (s0 - 1 + RING + 1), SLAB)
                        hidden(i)
                        if more or s0 + 3 * i + RING < n_slabs:
                            split_lo(dve, (s0 + 3) % RING, r + (s0 + RING + 1), SLAB)
                        hidden_lo(i)
                        if more or s0 + 1 + 3 * i + RING < n_slabs:
                            split_lo(dve, (s0 + 4) % RING, r + (s0 + 1 + RING + 1), SLAB)

                    gated(0)
                    split_lo(dve, s0 % RING, s0 + 4, SLAB)
                    hidden(0)
                    split_lo(dve, (s0 + 1) % RING, s0 + 5, SLAB)
                    hidden_lo(0)
                    body(1)
                    with dve.Fori(2, NI - 1) as i:
                        body(i)
                    body(NI - 1, more=False)
                    next_split(s0 + 3 * NI - 1)
                    for t in range(NT):
                        for n in range(2):
                            use = st.out[2 * t + n]
                            bank_filled(dve, use)
                            cols = slice(n * 512, (n + 1) * 512)
                            V.tensor_tensor(h[:, t, cols], psum[use[0]][:, :], h[:, t, cols], ALU.add)\
                                .then_inc(sem["h_ready"], 1)


_INS = ["x", "positions", "attn_norm", "ffn_norm", "final_norm", "ffn_w_gate", "ffn_w_up", "ffn_w_down", "ev_w_in",
        "ev_w_out", "diff_lambda_q1", "diff_lambda_k1", "diff_lambda_q2", "diff_lambda_k2", "diff_subln", "od_w_in",
        "od_w_out", "nsa_gate_b", "nsa_pe_k", "nsa_pe_v", "nsa_k_w1", "nsa_k_w2", "nsa_v_w1", "nsa_v_w2",
        "mla_q_norm", "mla_w_uq", "mla_kv_norm", "mla_w_ukv"]


def kernel(**inputs):
    import concourse.bacc as bacc
    from concourse.bass_utils import run_bass_kernel_spmd

    nc = bacc.Bacc("TRN2", target_bir_lowering=False, num_devices=1)
    arrays, aps = {}, {}
    for name in _INS:
        a = np.ascontiguousarray(inputs[name])
        arrays[f"in_{name}"] = a
        aps[name] = nc.dram_tensor(f"in_{name}", a.shape, mybir.dt.from_np(a.dtype), kind="ExternalInput").ap()
    out = nc.dram_tensor("out", (1, SEQ, D), F32, kind="ExternalOutput").ap()
    build(nc, aps, out)
    r = run_bass_kernel_spmd(nc, [arrays], core_ids=[0])
    return r.results[0]["out"]
```

```python
from contextlib import ExitStack

import numpy as np
import concourse.bass as bass
from concourse import mybir

F32 = mybir.dt.float32
F32R = mybir.dt.float32r
I32 = mybir.dt.int32
ALU = mybir.AluOpType
ACT = mybir.ActivationFunctionType
AX = mybir.AxisListType

P = 128
SEQ = 256
NT = SEQ // P
D = 1024
KT = D // P
FF = 2816
NI = FF // 256
HD = 64
NH = 8
NDH = 4
NG = 2
NCMP = SEQ // 16 - 1
NC = NCMP + 1
LQ, LKV, RO, NOPE = 256, 128, 32, 64
MD = NOPE + RO
EPS = 1e-5
THETA = 500000.0
LAMBDA_INIT = 0.8 - 0.6 * float(np.exp(-0.3 * 0))
NEG = -1e30
RING = 3
SLAB = 2048
SCORE_COLS = 3 * P
OD_W = [512, 512, 512, 184]
MLA_ROOM = 6
PI = float(np.float32(np.pi))
TWO_PI_PARTS = (6.28125, 1.93500518798828125e-3, 3.01991598196e-7)
ROUND = 1.5 * 2.0 ** 23


TILE_ORDER = [(t, n) for t in range(NT) for n in range(2)]


class Step:

    def __init__(self, kind,
                 acc=None, bank=None, banks=None, base=None, buf=None, chunks=None, combined=None,
                 combined_before=None, diff=None, down_base=None, dst=None, end=None, evac=None,
                 first=None, g0=None, gain=None, gate_wait=None, group=None, h_needed=None,
                 half=None, head=None, hid=None, k=None, k0=None, kts=None, kv=None, last=None,
                 layer=None, m=None, maps=None, n=None, needs=None, out=None, part=None, pt=None,
                 pv_before=None, read=None, ready=None, released=None, free=None, roped=None, s0=None,
                 slab=None, src=None, t=None, t_needed=None, u0=None, uid=None, unit=None,
                 up_wait=None, v_needs=None, what=None, where=None, which=None, width=None,
                 x_needed=None):
        self.kind = kind
        self.acc = acc
        self.bank = bank
        self.banks = banks
        self.base = base
        self.buf = buf
        self.chunks = chunks
        self.combined = combined
        self.combined_before = combined_before
        self.diff = diff
        self.down_base = down_base
        self.dst = dst
        self.end = end
        self.evac = evac
        self.first = first
        self.free = free
        self.g0 = g0
        self.gain = gain
        self.gate_wait = gate_wait
        self.group = group
        self.h_needed = h_needed
        self.half = half
        self.head = head
        self.hid = hid
        self.k = k
        self.k0 = k0
        self.kts = kts
        self.kv = kv
        self.last = last
        self.layer = layer
        self.m = m
        self.maps = maps
        self.n = n
        self.needs = needs
        self.out = out
        self.part = part
        self.pt = pt
        self.pv_before = pv_before
        self.read = read
        self.ready = ready
        self.released = released
        self.roped = roped
        self.s0 = s0
        self.slab = slab
        self.src = src
        self.t = t
        self.t_needed = t_needed
        self.u0 = u0
        self.uid = uid
        self.unit = unit
        self.up_wait = up_wait
        self.v_needs = v_needs
        self.what = what
        self.where = where
        self.which = which
        self.width = width
        self.x_needed = x_needed


class Plan:

    def __init__(self):
        self.steps, self.slabs = [], []
        self.count = {}
        self.bank_free = [None] * 8
        self.bank_fills = [0] * 8
        for b in range(2):
            self.take(b, (("gains_made", "pe_made")[b], 1))
        self.tbank = 0
        self.maps = self.units = 0

    def tick(self, name, n=1):
        self.count[name] = self.count.get(name, 0) + n
        return self.count[name]

    def add(self, kind, **fields):
        s = Step(kind, **fields)
        self.steps.append(s)
        return s

    def take(self, b, release):
        wait, self.bank_free[b] = self.bank_free[b], release
        self.bank_fills[b] += 1
        return (b, wait, self.bank_fills[b])

    def turn(self, release):
        b = 2 + self.tbank % 2
        self.tbank += 1
        return self.take(b, release)

    def slab(self, what, n, *where):
        self.slabs.append(Step("slab", what=what, n=n, where=where, released=None))
        return len(self.slabs) - 1

    def norm(self, k, order):
        self.add("norm", k=k, h_needed=self.count.get("h_ready", 0), chunks=order, n=self.tick("msq_made"))

    def x_transposed(self, src, ready, chunks, gain):
        n = self.tick("xlo_made")
        self.tick("xhi_made")
        self.add("xt", src=src, ready=ready, chunks=chunks, gain=gain, n=n, bank=self.turn(("xlo_made", n)))
        return n

    def projection(self, what, group, width, slabs, banks, x_needed, kts, x0=0, acc="evac_made"):
        uses = []
        for t in range(NT):
            uses.append(self.take(banks[t], (acc, self.tick(acc))))
        at = x0
        for i, s in enumerate(slabs):
            last = i == len(slabs) - 1
            for t in range(NT):
                end = t == NT - 1
                if end:
                    self.slabs[s].released = ("filled", uses[t][0], uses[t][2]) if last else \
                        ("slab_used", self.tick("slab_used"))
                self.add("proj", what=what, group=group, width=width, slab=s, t=t, bank=uses[t], kts=kts[i],
                         k0=at, first=i == 0, last=last, end=end, x_needed=x_needed[i], acc=acc)
            at += kts[i]
        return uses

    def transposed(self, kind, **fields):
        n = self.tick("t_made")
        self.add(kind, n=n, bank=self.turn(("t_made", n)), **fields)
        return n

    def ffn(self, layer):
        s0 = len(self.slabs)
        order = [("gate", 0), ("up", 0)]
        for i in range(1, NI):
            order += [("gate", i), ("up", i), ("down", i - 1)]
        order.append(("down", NI - 1))
        st = self.add("ffn", layer=layer, s0=s0, base=NI * layer, down_base=(NI - 1) * layer,
                      g0=self.bank_fills[0], u0=self.bank_fills[1],
                      gate_wait=self.bank_free[0], up_wait=self.bank_free[1])
        for what, i in order:
            s = self.slab(what, SLAB, layer, i)
            rel = {"gate": ("filled", 0, st.g0 + i + 1), "up": ("filled", 1, st.u0 + i + 1),
                   "down": ("down_done", st.down_base + i + 1)}[what]
            self.slabs[s].released = rel
        self.bank_fills[0] += NI
        self.bank_fills[1] += NI
        self.bank_free[0] = ("gated", st.base + NI)
        self.bank_free[1] = ("h_made", st.base + NI)
        st.x_needed = self.count["xlo_made"]
        st.out = [self.take(4 + b, ("h_ready", self.tick("h_ready"))) for b in range(4)]
        self.slabs[-1].released = ("filled", 7, st.out[3][2])
        st.end, st.slab = True, len(self.slabs) - 1


def interleave(*lists):
    keyed = []
    for n, steps in enumerate(lists):
        work = [5 if isinstance(s, Step) else 1 for s in steps]
        done = 0
        for w, s in zip(work, steps):
            keyed.append(((done + w / 2) / sum(work), n, s))
            done += w
    return [s for _, _, s in sorted(keyed, key=lambda k: k[:2])]


def attention_rounds(*groups):
    units = [(name, u, per) for name, n, per in groups for u in range(n)]
    n_units = {name: n for name, n, _ in groups}
    rounds = []
    for r in range(len(units) + 3):
        out = []
        if 2 <= r < len(units) + 2:
            name, u, _ = units[r - 2]
            out.append((name, "turn", u, 0))
        if r >= 3:
            name, u, _ = units[r - 3]
            out.append((name, "value", u, 0))
            if u == n_units[name] - 1:
                out.append((name, "out", 0, 0))
        if r < len(units):
            name, u, per = units[r]
            out += [(name, "scores", u, i) for i in range(per)]
        if 1 <= r < len(units) + 1:
            name, u, per = units[r - 1]
            if per == 2:
                out.append((name, "combine", u, 0))
        rounds.append(out)
    return rounds


def later_splits(steps):
    out, due = [], []
    for i, s in enumerate(steps):
        if s.kind == "ffn":
            out += [Step("split", slab=k) for k, _ in due]
            due = []
        out.append(s)
        if s.kind in ("norm", "xt"):
            continue
        following = steps[i + 1].kind if i + 1 < len(steps) else None
        while due and due[0][1] <= i and following not in ("norm", "xt"):
            out.append(Step("split", slab=due.pop(0)[0]))
        if s.end:
            due.append((s.slab, i + (1 if following == "proj" else 3)))
    return out


def make_plan():
    p = Plan()

    def read_out(name, banks, maps):
        for b, _, fill in banks:
            assert p.bank_fills[b] == fill
            p.bank_free[b] = ("o_banks_read", p.tick("o_banks_read"))
        read[name] = p.count["o_banks_read"]
        p.add("out", group=name, banks=banks, maps=maps, read=read[name],
              n=p.tick("msq_made") if name == "diff" else None)
        if name in ("diff", "cmp"):
            p.tick("o_ready")

    read = {}

    def emit(tokens, groups):
        for tok in tokens:
            if isinstance(tok, Step):
                p.steps.append(tok)
                continue
            if callable(tok):
                tok()
                continue
            name, what, u, i = tok
            g = groups[name]
            if what == "scores":
                m = p.maps
                p.maps += 1
                g["maps"].append(m)
                b = m % 2
                p.add("scores", group=name, unit=u, part=i, m=m, bank=p.take(b, ("masked", 2 * (m + 1))),
                      needs=g["needs"])
            elif what == "combine":
                p.add("combine", group=name, unit=u, maps=g["maps"][2 * u:2 * u + 2], n=p.tick("combined"))
            elif what == "turn":
                n_maps = g["per"]
                uid = p.units
                p.units += 1
                g["uids"].append(uid)
                n = p.tick(f"pt_made{uid % 2}")
                p.add("turn", group=name, unit=u, uid=uid, maps=g["maps"][u * n_maps:(u + 1) * n_maps], n=n,
                      bank=p.turn((f"pt_made{uid % 2}", n)), diff=n_maps == 2, pv_before=g_pv.get(uid - 2),
                      combined=u + 1)
            elif what == "value":
                last = u == g["n"] - 1
                if u == 0:
                    g["banks"] = [p.take(4 + t, None) for t in range(NT)]
                uid = g["uids"][u]
                rel = ("filled", 5, g["banks"][1][2]) if last else ("pv_done", p.tick("pv_done"))
                g_pv[uid] = rel
                pt = next(s for s in p.steps if s.kind == "turn" and s.uid == uid)
                p.add("value", group=name, unit=u, uid=uid, pt=pt.n, banks=g["banks"], first=u == 0, last=last,
                      needs=g["v_needs"])
            else:
                read_out(name, g["banks"], g["maps"])

    g_pv = {}

    def group(n, per):
        return {"n": n, "per": per, "maps": [], "uids": [], "needs": None, "v_needs": None}

    evac = {}

    def cut(start):
        made = p.steps[start:]
        del p.steps[start:]
        return made

    def project(key, what, group, width, slabs, banks, x_needed):
        start = len(p.steps)
        p.projection(what, group, width, slabs, banks, x_needed, [4] * len(slabs))
        evac[key] = p.count["evac_made"]
        return cut(start)

    def rope_step(what, key, w=16, buf=None):
        def step():
            roped[key] = p.tick("roped")
            p.add("rope", what=what, buf=buf, evac=evac[key], n=roped[key], t_needed=p.count.get("t_made", 0))
        return step

    def qk_turn(g, key, buf, half):
        return lambda: p.transposed("qkt", dst=(g, half), buf=buf, roped=roped[key])

    def now(g):
        def step():
            groups[g]["needs"] = p.count["t_made"]
        return step

    roped = {}
    groups = {"moba": group(NH, 1), "diff": group(NDH, 2), "slc": group(NH, 1), "win": group(NH, 1),
              "mla": group(NH, 1)}

    p.norm(0, TILE_ORDER)
    for j in range(KT // 2):
        p.x_transposed("h", 1, (2 * j, 2 * j + 1), 0)
    p.add("tables")
    ev = {}
    for i, g in enumerate((3, 4, 5, 0, 1, 2)):
        slabs = [p.slab("ev_in", SLAB, g, h) for h in range(2)]
        ev[g] = project(g, "ev_in", g, 512, slabs, (4, 5) if g == 4 else (6, 7), [2, 4] if i == 0 else [4, 4])
    groups["diff"]["v_needs"] = evac[5]
    groups["moba"]["v_needs"] = evac[2]
    rounds = attention_rounds(("diff", NDH, 2), ("moba", NH, 1))

    def over(first, last, fill):
        emit(interleave([tok for r in rounds[first:last] for tok in r], fill), groups)

    emit(ev[3] + ev[4][:2] + [rope_step("nat", 3, buf=0)] + ev[4][2:]
         + ev[5][:1] + [qk_turn(3, 3, 0, 0), rope_step("nat", 4, buf=1)] + ev[5][1:2] + [qk_turn(3, 3, 0, 1)]
         + ev[5][2:3] + [qk_turn(4, 4, 1, 0)] + ev[5][3:] + [qk_turn(4, 4, 1, 1), now("diff")], groups)
    over(0, 4, ev[0] + ev[1][:1] + [rope_step("nat", 0, buf=0)] + ev[1][1:3] + [qk_turn(0, 0, 0, 0)] + ev[1][3:]
         + [qk_turn(0, 0, 0, 1), rope_step("nat", 1, buf=1)] + ev[2][:1])
    emit([qk_turn(1, 1, 1, 0)] + ev[2][1:2] + [qk_turn(1, 1, 1, 1), now("moba")], groups)
    over(4, 6, ev[2][2:])
    over(6, 9, [])

    def out_half(what, half, ready):
        base = p.count["xlo_made"]
        before = p.count.get("h_ready", 0)
        turns = [lambda j=j: p.x_transposed("o", ready, (2 * j, 2 * j + 1), None) for j in (2 * half, 2 * half + 1)]
        start = len(p.steps)
        for g in range(2):
            slab = p.slab(what, SLAB, g, half)
            p.projection(what, g, 512, [slab], (6, 7), [base + 2], [4], x0=4 * half, acc="h_ready")
            for s in p.steps[-NT:]:
                s.h_needed = before
        return turns + cut(start)

    over(9, len(rounds), out_half("ev_out", 1, (read["diff"], 1)))
    emit(out_half("ev_out", 0, (read["moba"], 1)), groups)

    def norm_and_ffn(layer):
        k = 2 * layer + 1
        p.norm(k, [(t, n) for n, t in TILE_ORDER])
        for j in range(KT // 2):
            p.x_transposed("h", k + 1, (2 * j, 2 * j + 1), 16 + 8 * layer)
        p.ffn(layer)

    norm_and_ffn(0)

    p.norm(2, TILE_ORDER)
    base = p.count["xlo_made"]
    for j in range(KT // 2):
        p.x_transposed("h", 3, (2 * j, 2 * j + 1), 8)
    od = {}
    for i, g in enumerate((2, 3, 0, 1)):
        slabs = [p.slab("od_in", 4 * OD_W[g], g, h) for h in range(2)]
        od[g] = project("o%d" % g, "od_in", g, OD_W[g], slabs, (4, 5) if g == 3 else (6, 7),
                        [base + 2 if i == 0 else base + 4, base + 4])

    def k_turn(which, key):
        return lambda: p.transposed("kdt", which=which, roped=roped[key + "k"], evac=evac[key])

    def k_rope(what, key):
        def step():
            roped[key + "k"] = p.tick("roped")
            p.add("rope", what=what, evac=evac[key], n=roped[key + "k"])
        return step

    def blocks(kv):
        def step():
            n = p.tick("xc_lo_made")
            p.tick("xc_made")
            p.add("blocks", kv=kv, n=n, evac=evac["o1"], bank=p.turn(("xc_made", n)))
        return step

    emit(od[2] + od[3][:2] + [k_rope("kwin", "o2")] + od[3][2:]
         + od[0][:2] + [k_turn(1, "o2"), lambda: p.add("gates", evac=evac["o2"]),
                        lambda: p.add("latent_norm", evac=evac["o3"], n=p.tick("msq_made"))] + od[0][2:]
         + [rope_step("nat", "o0", buf=0)] + od[1][:1] + [qk_turn(6, "o0", 0, 0), qk_turn(6, "o0", 0, 1), now("win")],
         groups)
    groups["win"]["v_needs"] = evac["o2"]
    groups["slc"]["v_needs"] = evac["o1"]

    def latents():
        xb = p.count["xlo_made"]
        turns = [lambda: p.x_transposed("latent", 1, (0, 1), 32), lambda: p.x_transposed("latent", 1, (2,), 32)]
        start = len(p.steps)
        uq = p.slab("uq", 2 * 768, 0)
        ukv = p.slab("ukv", 1024, 0)
        for what, s, k0, kts, need in (("uq", uq, 0, 2, xb + 1), ("ukv", ukv, 2, 1, xb + 2)):
            for half in range(2):
                uses = [p.take(6 + t, ("evac_made", p.tick("evac_made"))) for t in range(NT)]
                for t in range(NT):
                    if half and t:
                        p.slabs[s].released = ("filled", 7, uses[t][2])
                    p.add("up", what=what, half=half, slab=s, t=t, bank=uses[t], kts=kts, k0=k0, x_needed=need,
                          end=bool(half and t), acc="evac_made",
                          width=768 if what == "uq" else 1024)
        evac["mla"] = p.count["evac_made"]
        return turns + cut(start)

    rounds = attention_rounds(("win", NH, 1), ("slc", NH, 1), ("mla", NH, 1))
    over(0, 4, od[1][1:])
    ups = latents()
    over(4, 8, [k_rope("kslc", "o1"), blocks(0), blocks(1), k_turn(0, "o1"), now("slc"), rope_step("kpe", "o3")]
         + ups[:2])

    def compress(kv):
        def half(h):
            def step():
                if h == 0:
                    c["slabs"] = [p.slab("w1", SLAB, kv, i) for i in range(2)]
                    c["bank"] = p.take(6 + kv, ("he_made", kv + 1))
                p.slabs[c["slabs"][h]].released = ("filled", 6 + kv, c["bank"][2]) if h else \
                    ("slab_used", p.tick("slab_used"))
                p.add("compress", kv=kv, half=h, slab=c["slabs"][h], bank=c["bank"], x_needed=kv + 1, end=True)
            return step

        def turned():
            p.add("hid_turn", kv=kv, bank=p.turn(("hid_read", kv + 1)))
        c = {}
        return [half(0), half(1), turned]

    def gelu(kv):
        return lambda: p.add("gelu", kv=kv, hid=kv + 1)

    def second(kv):
        def step():
            if kv == 0:
                c["n"] = p.tick("kcn_made")
                p.add("second", kv=kv, bank=p.turn(("kcn_made", 1)))
            else:
                p.add("second", kv=kv, bank=p.turn(("vbd_made", 1)))
        c = {}
        return step

    def c_rope():
        roped["kc"] = p.tick("roped")
        p.add("rope", what="kcmp", n=roped["kc"])

    def c_turn():
        n2 = p.tick("t_made")
        p.add("kcmp", roped=roped["kc"], n=n2, bank=p.turn(("t_made", n2)))

    def c_scores():
        p.add("cscores", t_needed=p.count["t_made"], bank=p.take(6, ("c_masked", 1)))

    def c_probs():
        p.add("cturn", bank=p.turn(("pct_made", 1)))

    def c_values():
        b4 = [p.take(6 + t, None) for t in range(NT)]
        p.add("cvalue", banks=b4)
        read_out("cmp", b4, [])

    def mla_turn(h):
        def step():
            free = None
            if h >= MLA_ROOM:
                s = next(s for s in p.steps if s.kind == "scores" and s.group == "mla" and s.unit == h - MLA_ROOM)
                free = ("filled", s.bank[0], s.bank[2])
            p.transposed("mqkt", head=h, roped=roped["mla"], free=free)
            groups["mla"]["needs"] = p.count["t_made"]
        return step

    groups["mla"]["v_needs"] = evac["mla"]
    k_layer, v_layer = compress(0), compress(1)
    over(8, 16, ups[2:] + [rope_step("qpe", "mla")] + k_layer + v_layer[:1] + [gelu(0)] + v_layer[1:]
         + [second(0), c_rope, gelu(1), c_turn, mla_turn(0), second(1), c_scores, mla_turn(1), mla_turn(2)])
    over(16, 18, [mla_turn(3), c_probs, mla_turn(4)])
    over(18, 19, [mla_turn(5)])
    over(19, 21, [c_values, mla_turn(6), mla_turn(7)])
    over(21, len(rounds), out_half("od_out", 0, (read["cmp"], 2)))
    emit(out_half("od_out", 1, (read["mla"], 2)), groups)
    norm_and_ffn(1)
    p.norm(4, TILE_ORDER)
    p.steps = later_splits(p.steps)
    return p


def build(nc, t_in, out):
    plan = make_plan()
    steps, slabs = plan.steps, plan.slabs
    n_slabs = len(slabs)
    with ExitStack() as ctx:
        def sb(name, shape, dt=F32):
            return ctx.enter_context(nc.sbuf_tensor(name, shape, dt))

        raw = [sb(f"raw{i}", [P, SLAB]) for i in range(RING)]
        whi = [sb(f"whi{i}", [P, SLAB], F32R) for i in range(RING)]
        wlo = [sb(f"wlo{i}", [P, SLAB], F32R) for i in range(RING)]
        h = sb("h", [P, NT, D])
        o = sb("o", [P, NT, D])
        xhi = sb("xhi", [P, KT, SEQ], F32R)
        xlo = sb("xlo", [P, KT, SEQ], F32R)
        nat = sb("nat", [P, 2, NT, 512])
        qk = sb("qk", [P, 4, 4, SEQ])
        vals = sb("vals", [P, 2, NT, 512])
        vnsa = sb("vnsa", [P, 2, NT, P])
        nat2 = sb("nat2", [P, NT, 4, NG, 2, HD])
        kd = sb("kd", [P, 2, NG, SEQ])
        masked = sb("masked", [P, 2, SCORE_COLS])
        prob = sb("prob", [P, 4, SCORE_COLS])
        comb = sb("comb", [P, 2, SCORE_COLS])
        pt = sb("pt", [P, 2, SCORE_COLS])
        n_maps = plan.maps
        nmax = sb("nmax", [P, 2 * n_maps])
        sums = sb("sums", [P, 2 * n_maps])
        rinv = sb("rinv", [P, 2 * n_maps])
        coef = sb("coef", [P, NT, NH])
        rope_a = sb("rope_a", [P, NT, NH, RO])
        rope_b = sb("rope_b", [P, NT, NH, RO])
        otmp = sb("otmp", [P, 512])
        xc = sb("xc", [P, 16, NG, NC])
        xcs = sb("xcs", [P, 16, 4 * NG * NC], F32R)
        fold = sb("fold", [P, NG * NC])
        hid = sb("hid", [P, 2, NG * NC])
        hid2 = sb("hid2", [P, 2, NG * NC])
        hid3 = sb("hid3", [P, 2, NG * NC])
        hk = sb("hk", [P, 2, NG * NC])
        hv = sb("hv", [P, 2, NH, NC])
        kcn = sb("kcn", [NG * NC, 2, HD])
        kct = sb("kct", [P, NG, 2, NC])
        vbd = sb("vbd", [P, NH, HD])
        cs = sb("cs", [P, NT, NH, NC])
        cmx = sb("cmx", [P, NT * NH])
        csum = sb("csum", [P, NT * NH])
        pct = sb("pct", [P, NT, P])
        gate = sb("gate", [P, NT, NH * 3])
        lat = sb("lat", [P, NT, LQ + LKV])
        lats = comb[:, :, :].rearrange("p a n -> p (a n)").rearrange("p (t n) -> p t n", t=NT)
        kpe = sb("kpe", [P, NT, RO])
        def room(flat, d):
            return flat[:, 0:NT * NH * d].rearrange("p (t h d) -> p t h d", t=NT, h=NH)

        qm = room(nat[:, :, :, :].rearrange("p b t n -> p (b t n)"), MD)
        km = room(nat2[:, :, :, :, :, :].rearrange("p t w g u d -> p (t w g u d)"), MD)
        vm = room(vals[:, 0].rearrange("p t n -> p (t n)"), HD)
        free = masked[:, :, :].rearrange("p a n -> p (a n)"), prob[:, :, :].rearrange("p a n -> p (a n)")
        dg = free[0][:, 0:NT * P].rearrange("p (t n) -> p t n", t=NT)
        th, ga, hf = free[0][:, 0:512], free[1][:, 0:512], free[1][:, 512:1024]
        flat = xcs[:, :, :].rearrange("p j n -> p (j n)")
        hhi, hlo = flat[:, 0:512], flat[:, 512:1024]
        he = otmp[:, 0:256]
        ident = sb("ident", [P, P])
        tri = sb("tri", [P, SCORE_COLS])
        cmask = sb("cmask", [P, NT, NC])
        cvalid = sb("cvalid", [P, NT, NC])
        bdm = sb("bdm", [P, NH])
        invf = sb("invf", [P, 16])
        mhalf = sb("mhalf", [P, 8])
        posi = sb("posi", [P, 3], I32)
        posf = sb("posf", [P, 3])
        ang = sb("ang", [P, 3, 16])
        turns = sb("turns", [P, 3, 16])
        red = sb("red", [P, 2, 3, 16])
        trig = sb("trig", [P, 2, 3, 16])
        cc8 = sb("cc8", [P, 3, 16])
        sn8 = sb("sn8", [P, 3, 16])
        cc16 = sb("cc16", [P, 3, 32])
        sn16 = sb("sn16", [P, 3, 32])
        grow = sb("grow", [35, P])
        gains = sb("gains", [P, 35])
        perow = sb("perow", [32, 2, 2, HD])
        pet = sb("pet", [P, 2, 32])
        w2 = sb("w2", [P, 2, 2, HD])
        gfin = sb("gfin", [P, D])
        subln = sb("subln", [P, 2 * HD])
        gateb = sb("gateb", [P, NH * 3])
        lqk = sb("lqk", [P, 4, HD])
        lam = sb("lam", [P, 4])
        ssq = sb("ssq", [P, 8])
        msq = sb("msq", [P, 8])
        rstd = sb("rstd", [P, 8])

        def mla_qk(head, which):
            slot = 4 + 2 * (head % MLA_ROOM) + which
            return qk[0:MD, slot // 4, slot % 4, :]

        psum = [ctx.enter_context(nc.psum_tensor(f"bank{b}", [P, 512], F32)) for b in range(8)]

        sem = {n: ctx.enter_context(nc.semaphore(n)) for n in (
            "x0_landed", "x1_landed", "small_landed", "hi_made", "lo_made", "slab_used", "ssq_made", "rstd_made", "msq_made",
            "diag_made", "gains_landed", "gains_made", "ident_made", "pe_made", "xhi_made", "xlo_made", "evac_made", "roped", "t_made", "masked", "exped", "pt_made0",
            "pt_made1", "pv_done", "o_banks_read", "o_ready", "combined", "tanh_made", "gated", "h_made",
            "hhi_made", "hlo_made", "down_done", "h_ready", "dve_step", "pool_step", "posi_cleared", "consts_made", "angles_made",
            "sin_made", "lam_dots", "lam_exp", "xc_made",
            "xch_made", "xc_lo_made", "he_made", "kcn_made", "vbd_made", "gelu_in", "gelu_th", "gelu_out", "hid_read", 
            "c_masked", "c_centred", "c_exped", "c_ready", "pct_made", "gate_in", "gate_th", "gates_made",
            "lat_made", "kpe_spread", "fin_made", "stored")}
        filled = [ctx.enter_context(nc.semaphore(f"filled{b}")) for b in range(8)]
        landed = [ctx.enter_context(nc.semaphore(f"landed{i}")) for i in range(RING)]
        block = ctx.enter_context(nc.Block())

        def wait(eng, what):
            if what is None:
                return
            if what[0] == "filled":
                eng.wait_ge(filled[what[1]], what[2])
            else:
                eng.wait_ge(sem[what[0]], what[1])

        prob_free, comb_free = {}, {}
        for st in steps:
            if st.kind == "turn":
                turned = ("filled", st.bank[0], st.bank[2])
                for m in st.maps:
                    prob_free[m] = ("combined", st.combined) if st.diff else turned
                if st.diff:
                    comb_free[st.unit] = turned

        def bank_filled(eng, bank):
            eng.wait_ge(filled[bank[0]], bank[2])

        def tiles(ap):
            return ap.rearrange("(k p) n -> p k n", p=P)

        ev_in, ev_out = tiles(t_in["ev_w_in"][0]), tiles(t_in["ev_w_out"][0])
        od_in, od_out = tiles(t_in["od_w_in"][0]), tiles(t_in["od_w_out"][0])
        w_gate = [tiles(t_in["ffn_w_gate"][l]) for l in range(2)]
        w_up = [tiles(t_in["ffn_w_up"][l]) for l in range(2)]
        w_down = [tiles(t_in["ffn_w_down"][l]) for l in range(2)]
        w1 = [tiles(t_in[n][0]) for n in ("nsa_k_w1", "nsa_v_w1")]

        def slab_source(s):
            what, w = s.what, s.where
            if what in ("ev_in", "ev_out", "od_out"):
                v = {"ev_in": ev_in, "ev_out": ev_out, "od_out": od_out}[what]
                return v[:, 4 * w[1]:4 * w[1] + 4, 512 * w[0]:512 * (w[0] + 1)]
            if what == "od_in":
                return od_in[:, 4 * w[1]:4 * w[1] + 4, 512 * w[0]:512 * w[0] + OD_W[w[0]]]
            if what == "w1":
                return w1[w[0]][:, 8 * w[1]:8 * w[1] + 8, :]
            if what == "uq":
                return tiles(t_in["mla_w_uq"][0])
            if what == "ukv":
                return tiles(t_in["mla_w_ukv"][0])
            return ffn_source(what, *w)

        def ffn_source(what, layer, i):
            if what == "gate":
                return w_gate[layer][:, :, bass.ds(256 * i, 256)]
            if what == "up":
                return w_up[layer][:, :, bass.ds(256 * i, 256)]
            return w_down[layer][:, bass.ds(2 * i, 2), :]

        def parts(tile, k, n):
            return tile[:, 0:k * n].rearrange("p (k n) -> p k n", k=k)

        n_gains, n_small = 4, 17

        def pool_splits(k):
            return k < n_slabs and slabs[k].what not in ("gate", "up", "down") and k >= RING and \
                slabs[k - RING].what != "down"

        @block.sync
        def _(sp):
            x = t_in["x"][0].rearrange("(t p) d -> p t d", p=P)
            for t in range(NT):
                sp.dma_start(h[:, t, :], x[:, t, :]).then_inc(sem[f"x{t}_landed"], 16)

            def load(slot, source, n, k, lo_wait):
                if lo_wait is not None:
                    sp.wait_ge(sem["lo_made"], lo_wait)
                sp.dma_start(parts(raw[slot], k, n // k), source).then_inc(landed[slot], 16)

            ffn_at = {s.s0: s for s in steps if s.kind == "ffn"}
            s = 0
            while s < n_slabs:
                sl = slabs[s]
                if s in ffn_at:
                    st = ffn_at[s]
                    lyr, s0 = st.layer, st.s0

                    def ffn_slab(k, what, i):
                        load((s0 + k) % RING, ffn_source(what, lyr, i), SLAB, 2 if what == "down" else KT, None)

                    for k, (what, i) in enumerate((("gate", 0), ("up", 0), ("gate", 1), ("up", 1), ("down", 0))):
                        sp.wait_ge(sem["lo_made"], s0 + k - RING + 1)
                        ffn_slab(k, what, i)
                    with sp.Fori(2, NI) as i:
                        for j, (what, back) in enumerate((("gate", 0), ("up", 0), ("down", 1))):
                            sp.wait_ge(sem["lo_made"], i * RING + (s0 - 1 + j - RING + 1))
                            ffn_slab(2 + j, what, i - back)
                    sp.wait_ge(sem["lo_made"], s0 + 3 * NI - 1 - RING + 1)
                    ffn_slab(3 * NI - 1, "down", NI - 1)
                    s += 3 * NI
                    continue
                k = slab_source(sl).shape[1]
                load(s % RING, slab_source(sl), sl.n, k, s - RING + 1 if s >= RING else None)
                s += 1
            for j, (t, n) in enumerate(TILE_ORDER):
                cols = slice(512 * n, 512 * (n + 1))
                sp.wait_ge(sem["fin_made"], j + 1)
                sp.dma_start(out[0, t * P:(t + 1) * P, cols], o[:, t, cols]).then_inc(sem["stored"], 16)
            sp.wait_ge(sem["stored"], 64)

        @block.gpsimd
        def _(pool):
            step = [0]

            def made(ins):
                step[0] += 1
                ins.then_inc(sem["pool_step"], 1)

            made(pool.memset(ident[:, :], 0.0))
            pool.wait_ge(sem["pool_step"], step[0])
            pool.affine_select(out=ident[:, :], in_=ident[:, :], compare_op=ALU.not_equal, fill=1.0, base=0,
                               pattern=[[-1, P]], channel_multiplier=1).then_inc(sem["ident_made"], 1)
            pool.memset(posi[:, :], 0).then_inc(sem["posi_cleared"], 1)
            made(pool.memset(mhalf[:, :], -0.5))
            pool.wait_ge(sem["pool_step"], step[0])

            def root(st, n):
                pool.wait_ge(sem["msq_made"], st.n)
                pool.tensor_tensor(rstd[:, 0:n], msq[:, 0:n], mhalf[:, 0:n], ALU.pow).then_inc(sem["rstd_made"], 1)

            root(steps[0], NT)
            made(pool.memset(tri[:, :], 0.0))
            made(pool.memset(cmask[:, :, :], 0.0))
            made(pool.memset(cvalid[:, :, :], 1.0))
            made(pool.memset(bdm[:, :], 1.0))
            made(pool.memset(kct[:, :, :, :], 0.0))
            for i in range(16):
                pool.memset(invf[:, i:i + 1], float(np.float32(1.0 / THETA ** (i / 16))))
            pool.memset(xc[:, :, :, :], 0.0)
            pool.wait_ge(sem["pool_step"], step[0])
            for c in (0, 2 * P):
                made(pool.affine_select(out=tri[:, c:c + P], in_=tri[:, c:c + P], compare_op=ALU.is_ge, fill=NEG,
                                        base=0, pattern=[[-1, P]], channel_multiplier=1))
            for m, fill in ((cmask, NEG), (cvalid, 0.0)):
                made(pool.affine_select(out=m[:, :, :], in_=m[:, :, :], compare_op=ALU.is_ge, fill=fill, base=-31,
                                        pattern=[[P, NT], [-16, NC]], channel_multiplier=1))
            made(pool.affine_select(out=bdm[:, :], in_=bdm[:, :], compare_op=ALU.is_ge, fill=0.0, base=0,
                                    pattern=[[-NC, NH]], channel_multiplier=1))
            pool.wait_ge(sem["pool_step"], step[0])
            pool.affine_select(out=bdm[:, :], in_=bdm[:, :], compare_op=ALU.is_ge, fill=0.0, base=NC - 1,
                               pattern=[[NC, NH]], channel_multiplier=-1).then_inc(sem["consts_made"], 1)

            for st in steps[1:]:
                if st.kind == "norm":
                    root(st, NT)
                elif st.kind == "out" and st.group == "diff":
                    root(st, NT * NDH)
                elif st.kind == "latent_norm":
                    root(st, 2 * NT)
                elif st.kind == "split" and pool_splits(st.slab + RING):
                    k = st.slab + RING
                    pool.wait_ge(sem["lo_made"], k)
                    pool.wait_ge(sem["hi_made"], k + 1)
                    n = slabs[k].n
                    pool.tensor_tensor(wlo[k % RING][:, 0:n], raw[k % RING][:, 0:n],
                                       whi[k % RING][:, 0:n].bitcast(F32), ALU.subtract).then_inc(sem["lo_made"], 1)

        def evac_copies(what, group, t, bank, half=0):
            b = psum[bank]
            if what == "ev_in":
                if group in (2, 5):
                    return [(vals[:, group // 3, t, :], b[:, :])]
                return [(nat[:, group % 3 % 2, t, :], b[:, :])]
            if what == "uq":
                return [(qm[:, t, 4 * half:4 * half + 4, :], b[:, 0:4 * MD].rearrange("p (h d) -> p h d", h=4))]
            if what == "ukv":
                v = b[:, :].rearrange("p (h d) -> p h d", h=4)
                return [(km[:, t, 4 * half:4 * half + 4, 0:NOPE], v[:, :, 0:NOPE]),
                        (vm[:, t, 4 * half:4 * half + 4, :], v[:, :, NOPE:])]

            def twice(c):
                v = b[:, c:c + P].rearrange("p (g d) -> p g d", g=NG).unsqueeze(2)
                return v.broadcast_to([P, NG, 2, HD])

            if group == 0:
                return [(nat[:, 0, t, :], b[:, :])]
            if group == 1:
                return [(nat2[:, t, 2], twice(0)), (nat2[:, t, 3], twice(128)), (nat2[:, t, 0], twice(256)),
                        (vnsa[:, 0, t, :], b[:, 384:512])]
            if group == 2:
                return [(nat2[:, t, 1], twice(0)), (vnsa[:, 1, t, :], b[:, 128:256]),
                        (gate[:, t, :], b[:, 256:280]), (lat[:, t, 0:232], b[:, 280:512])]
            return [(lat[:, t, 232:384], b[:, 0:152]), (kpe[:, t, :], b[:, 152:184])]

        def score_operands(group, unit, part):
            if group == "mla":
                return mla_qk(unit, 0), mla_qk(unit, 1), MD ** -0.5
            if group == "diff":
                lo = 64 * part
                return qk[lo:lo + HD, 2, unit, :], qk[lo:lo + HD, 3, unit, :], HD ** -0.5
            lo = 64 * (unit % 2)
            q = qk[lo:lo + HD, 0, unit // 2, :]
            if group == "moba":
                return q, qk[lo:lo + HD, 1, unit // 2, :], HD ** -0.5
            return q, kd[lo:lo + HD, 0 if group == "slc" else 1, unit // 4, :], HD ** -0.5

        def value_operand(group, unit, kt):
            if group == "mla":
                return vm[:, kt, unit, :]
            if group == "diff":
                return vals[:, 1, kt, unit * P:(unit + 1) * P]
            if group == "moba":
                return vals[:, 0, kt, unit * HD:(unit + 1) * HD]
            g = unit // 4
            return vnsa[:, 0 if group == "slc" else 1, kt, g * HD:(g + 1) * HD]

        def source(name):
            return {"h": h, "o": o, "latent": lats}[name]

        def t_dst(st):
            if st.kind == "qkt":
                g, half = st.dst
                row = {0: 0, 1: 1, 3: 2, 4: 3, 6: 0}[g]
                return qk[:, row, 2 * half:2 * half + 2, :]
            return kd[:, st.which]

        def split_hi(act, slot, rounds_wait, n):
            act.wait_ge(landed[slot], rounds_wait)
            nc.scalar.activation(whi[slot][:, 0:n], raw[slot][:, 0:n], ACT.Copy).then_inc(sem["hi_made"], 1)

        def split_lo(dve, slot, count, n):
            dve.wait_ge(sem["hi_made"], count)
            nc.vector.tensor_tensor(wlo[slot][:, 0:n], raw[slot][:, 0:n], whi[slot][:, 0:n].bitcast(F32),
                                    ALU.subtract).then_inc(sem["lo_made"], 1)

        @block.tensor
        def _(pe):
            def turn(dst, src, rows=P):
                return nc.tensor.transpose(dst, src, ident[0:rows, 0:rows])

            def three(dst, a, b, first, last):
                nc.tensor.matmul(dst, a[0], b[0], start=first, stop=False)
                nc.tensor.matmul(dst, a[1], b[0], start=False, stop=False)
                return nc.tensor.matmul(dst, a[0], b[1], start=False, stop=last)

            pe.wait_ge(sem["ident_made"], 1)
            pe.wait_ge(sem["gains_landed"], 16 * n_gains)
            turn(psum[0][:, 0:35], grow[:, :], 35).then_inc(filled[0], 1)

            def gate_or_up(which, lo_count, s0, i_slot, bank_sem, bank_value):
                slot = i_slot
                pe.wait_ge(sem["lo_made"], lo_count)
                if bank_sem is not None:
                    pe.wait_ge(bank_sem, bank_value)
                hi, lo = parts(whi[slot], KT, 256), parts(wlo[slot], KT, 256)
                for c in range(2):
                    cols = slice(c * P, (c + 1) * P)
                    for k in range(KT):
                        last = three(psum[which][:, c * SEQ:(c + 1) * SEQ], (hi[:, k, cols], lo[:, k, cols]),
                                     (xhi[:, k, :], xlo[:, k, :]), k == 0, k == KT - 1)
                last.then_inc(filled[which], 1)

            def down(slot, lo_count, hid_count, first, final):
                pe.wait_ge(sem["lo_made"], lo_count)
                pe.wait_ge(sem["hlo_made"], hid_count)
                hi, lo = parts(whi[slot], 2, D), parts(wlo[slot], 2, D)
                for t in range(NT):
                    for n in range(2):
                        for c in range(2):
                            rows = slice(c * SEQ + t * P, c * SEQ + (t + 1) * P)
                            cols = slice(n * 512, (n + 1) * 512)
                            last = three(psum[4 + 2 * t + n][:, :], (hhi[:, rows], hlo[:, rows]),
                                         (hi[:, c, cols], lo[:, c, cols]), first and c == 0, final and c == 1)
                        if final:
                            last.then_inc(filled[4 + 2 * t + n], 1)
                if not final:
                    last.then_inc(sem["down_done"], 1)

            for st in steps:
                if st.kind == "tables":
                    pe.wait_ge(sem["small_landed"], 16 * n_small)
                    for kv in range(2):
                        last = turn(psum[1][:, 32 * kv:32 * kv + 32], perow[:, kv].rearrange("t u d -> t (u d)"), 32)
                    last.then_inc(filled[1], 1)
                elif st.kind == "xt":
                    if st.src == "h":
                        pe.wait_ge(sem["diag_made"], st.ready)
                    elif st.src == "o":
                        pe.wait_ge(sem["o_banks_read"], st.ready[0])
                        pe.wait_ge(sem["o_ready"], st.ready[1])
                    else:
                        pe.wait_ge(sem["lat_made"], 1)
                    b, w, _ = st.bank
                    wait(pe, w)
                    for i, c in enumerate(st.chunks):
                        for t in range(NT):
                            dst = psum[b][:, i * SEQ + t * P:i * SEQ + (t + 1) * P]
                            src = source(st.src)[:, t, c * P:(c + 1) * P]
                            if st.src == "h":
                                last = nc.tensor.matmul(dst, src, dg[:, t, :], start=True, stop=True)
                            else:
                                last = turn(dst, src)
                    last.then_inc(filled[b], 1)
                elif st.kind == "proj":
                    slot = st.slab % RING
                    b, w, _ = st.bank
                    pe.wait_ge(sem["lo_made"], st.slab + 1)
                    pe.wait_ge(sem["xlo_made"], st.x_needed)
                    if st.first:
                        wait(pe, w)
                    hi, lo = parts(whi[slot], st.kts, st.width), parts(wlo[slot], st.kts, st.width)
                    rows = slice(st.t * P, (st.t + 1) * P)
                    for k in range(st.kts):
                        last = three(psum[b][:, 0:st.width], (xhi[:, st.k0 + k, rows], xlo[:, st.k0 + k, rows]),
                                     (hi[:, k, :], lo[:, k, :]), st.first and k == 0, st.last and k == st.kts - 1)
                    if st.last:
                        last.then_inc(filled[b], 1)
                    elif st.end:
                        last.then_inc(sem["slab_used"], 1)
                elif st.kind == "up":
                    slot = st.slab % RING
                    b, w, _ = st.bank
                    pe.wait_ge(sem["lo_made"], st.slab + 1)
                    pe.wait_ge(sem["xlo_made"], st.x_needed)
                    wait(pe, w)
                    hi, lo = parts(whi[slot], st.kts, st.width), parts(wlo[slot], st.kts, st.width)
                    rows = slice(st.t * P, (st.t + 1) * P)
                    n = st.width // 2
                    cols = slice(st.half * n, (st.half + 1) * n)
                    for k in range(st.kts):
                        last = three(psum[b][:, 0:n], (xhi[:, st.k0 + k, rows], xlo[:, st.k0 + k, rows]),
                                     (hi[:, k, cols], lo[:, k, cols]), k == 0, k == st.kts - 1)
                    last.then_inc(filled[b], 1)
                elif st.kind == "qkt":
                    b, w, _ = st.bank
                    pe.wait_ge(sem["roped"], st.roped)
                    wait(pe, w)
                    for i in range(2):
                        c = 2 * st.dst[1] + i
                        for t in range(NT):
                            last = turn(psum[b][:, i * SEQ + t * P:i * SEQ + (t + 1) * P],
                                        nat[:, st.buf, t, c * P:(c + 1) * P])
                    last.then_inc(filled[b], 1)
                elif st.kind in ("kdt", "blocks"):
                    b, w, _ = st.bank
                    pe.wait_ge(sem["evac_made"], st.evac)
                    if st.kind == "kdt":
                        pe.wait_ge(sem["roped"], st.roped)
                    which = st.which if st.kind == "kdt" else 2 + st.kv
                    wait(pe, w)
                    for g in range(NG):
                        for t in range(NT):
                            last = turn(psum[b][:, g * SEQ + t * P:g * SEQ + (t + 1) * P],
                                        nat2[:, t, which, g].rearrange("p u d -> p (u d)"))
                    last.then_inc(filled[b], 1)
                elif st.kind == "mqkt":
                    b, w, _ = st.bank
                    pe.wait_ge(sem["roped"], st.roped)
                    pe.wait_ge(sem["kpe_spread"], 1)
                    wait(pe, w)
                    for i, src in enumerate((qm, km)):
                        for t in range(NT):
                            last = turn(psum[b][0:MD, i * SEQ + t * P:i * SEQ + (t + 1) * P], src[:, t, st.head, :])
                    last.then_inc(filled[b], 1)
                elif st.kind == "scores":
                    b, w, _ = st.bank
                    q, k, _ = score_operands(st.group, st.unit, st.part)
                    pe.wait_ge(sem["t_made"], st.needs)
                    wait(pe, w)
                    nc.tensor.matmul(psum[b][:, 0:P], q[:, 0:P], k[:, 0:P], start=True, stop=True)
                    nc.tensor.matmul(psum[b][:, P:3 * P], q[:, P:2 * P], k, start=True, stop=True)\
                        .then_inc(filled[b], 1)
                elif st.kind == "turn":
                    b, w, _ = st.bank
                    if st.diff:
                        pe.wait_ge(sem["combined"], st.combined)
                        src = comb[:, st.unit % 2, :]
                    else:
                        pe.wait_ge(sem["exped"], 2 * (st.maps[0] + 1))
                        src = prob[:, st.maps[0] % 4, :]
                    wait(pe, w)
                    for i in range(3):
                        last = turn(psum[b][:, i * P:(i + 1) * P], src[:, i * P:(i + 1) * P])
                    last.then_inc(filled[b], 1)
                elif st.kind == "value":
                    pe.wait_ge(sem[f"pt_made{st.uid % 2}"], st.pt)
                    pe.wait_ge(sem["evac_made"], st.needs)
                    if st.first:
                        wait(pe, st.banks[0][1])
                        wait(pe, st.banks[1][1])
                    v0, v1 = value_operand(st.group, st.unit, 0), value_operand(st.group, st.unit, 1)
                    n = v0.shape[-1]
                    cols = slice(st.unit * n, (st.unit + 1) * n)
                    w = pt[:, st.uid % 2, :]
                    m0 = nc.tensor.matmul(psum[4][:, cols], w[:, 0:P], v0, start=True, stop=True)
                    nc.tensor.matmul(psum[5][:, cols], w[:, P:2 * P], v0, start=True, stop=False)
                    m1 = nc.tensor.matmul(psum[5][:, cols], w[:, 2 * P:3 * P], v1, start=False, stop=True)
                    if st.last:
                        m0.then_inc(filled[4], 1)
                        m1.then_inc(filled[5], 1)
                    else:
                        m1.then_inc(sem["pv_done"], 1)
                elif st.kind == "compress":
                    slot = st.slab % RING
                    b, w, _ = st.bank
                    pe.wait_ge(sem["lo_made"], st.slab + 1)
                    pe.wait_ge(sem["xc_lo_made"], NG)
                    if st.half == 0:
                        wait(pe, w)
                    hi, lo = parts(whi[slot], 8, 256), parts(wlo[slot], 8, 256)
                    for j in range(8):
                        jj = 8 * st.half + j
                        nc.tensor.matmul(psum[b][:, 0:256], xcs[:, jj, :], hi[:, j, :], start=jj == 0, stop=False)
                        last = nc.tensor.matmul(psum[b][:, 0:256], xcs[:, jj, :], lo[:, j, :], start=False,
                                                stop=jj == 15)
                    if st.half:
                        last.then_inc(filled[b], 1)
                    else:
                        last.then_inc(sem["slab_used"], 1)
                elif st.kind == "hid_turn":
                    b, w, _ = st.bank
                    pe.wait_ge(sem["he_made"], st.kv + 1)
                    wait(pe, w)
                    rows = slice(64 * st.kv, 64 * st.kv + 64)
                    for c in range(2):
                        last = nc.tensor.matmul(psum[b][:, c * NG * NC:(c + 1) * NG * NC],
                                                he[rows, c * P:(c + 1) * P], fold[rows, :], start=True, stop=True)
                    last.then_inc(filled[b], 1)
                elif st.kind == "second":
                    b, w, _ = st.bank
                    pe.wait_ge(sem["gelu_out"], st.kv + 1)
                    wait(pe, w)
                    for c in range(2):
                        lhs = hk[:, c, :] if st.kv == 0 else hv[:, c].rearrange("p h n -> p (h n)")
                        m = lhs.shape[-1]
                        last = nc.tensor.matmul(psum[b][0:m, 0:HD], lhs, w2[:, st.kv, c, :],
                                                start=c == 0, stop=c == 1)
                    last.then_inc(filled[b], 1)
                elif st.kind == "kcmp":
                    b, w, _ = st.bank
                    pe.wait_ge(sem["roped"], st.roped)
                    wait(pe, w)
                    turn(psum[b][:, 0:NG * NC], kcn[:, :, :].rearrange("p u d -> p (u d)"), NG * NC)\
                        .then_inc(filled[b], 1)
                elif st.kind == "cscores":
                    pe.wait_ge(sem["t_made"], st.t_needed)
                    b, w, _ = st.bank
                    wait(pe, w)
                    for t in range(NT):
                        for j in range(NH // 2):
                            at = (t * NH + 2 * j) * NC
                            last = nc.tensor.matmul(psum[b][:, at:at + 2 * NC], qk[:, 0, j, t * P:(t + 1) * P],
                                                    kct[:, 2 * j // (NH // NG)].rearrange("p u n -> p (u n)"),
                                                    start=True, stop=True)
                    last.then_inc(filled[b], 1)
                elif st.kind == "cturn":
                    b, w, _ = st.bank
                    pe.wait_ge(sem["c_ready"], 1)
                    wait(pe, w)
                    for t in range(NT):
                        last = turn(psum[b][:, t * P:(t + 1) * P], cs[:, t].rearrange("p h n -> p (h n)"))
                    last.then_inc(filled[b], 1)
                elif st.kind == "cvalue":
                    pe.wait_ge(sem["pct_made"], 1)
                    pe.wait_ge(sem["vbd_made"], 1)
                    for t in range(NT):
                        b, w, _ = st.banks[t]
                        wait(pe, w)
                        nc.tensor.matmul(psum[b][:, :], pct[:, t, :], vbd[:, :, :].rearrange("p h d -> p (h d)"),
                                         start=True, stop=True).then_inc(filled[b], 1)
                elif st.kind == "ffn":
                    s0, g0, u0, base = st.s0, st.g0, st.u0, st.base
                    pe.wait_ge(sem["xlo_made"], st.x_needed)
                    wait(pe, st.gate_wait)
                    gate_or_up(0, s0 + 1, s0, s0 % RING, None, None)
                    wait(pe, st.up_wait)
                    gate_or_up(1, s0 + 2, s0, (s0 + 1) % RING, None, None)

                    def body(i, first):
                        a = i * RING + (s0 - 1)
                        gate_or_up(0, a + 1, s0, (s0 + 2) % RING, sem["gated"], i + base)
                        gate_or_up(1, a + 2, s0, (s0 + 3) % RING, sem["h_made"], i + base)
                        down((s0 + 4) % RING, a + 3, i + base, first, False)

                    for o_use in st.out:
                        wait(pe, o_use[1])
                    body(1, True)
                    with pe.Fori(2, NI) as i:
                        body(i, False)
                    down((s0 + 3 * NI - 1) % RING, s0 + 3 * NI, base + NI, False, True)

        @block.scalar
        def _(act):
            A = nc.scalar.activation
            gain_loads = [
                (grow[0:16, :], t_in["attn_norm"].rearrange("l (k p) -> (l k) p", p=P)),
                (grow[16:32, :], t_in["ffn_norm"].rearrange("l (k p) -> (l k) p", p=P)),
                (grow[32:34, :], t_in["mla_q_norm"].rearrange("l (k p) -> (l k) p", p=P)),
                (grow[34:35, :], t_in["mla_kv_norm"]),
            ]
            loads = [
                (gfin[:, :], t_in["final_norm"].partition_broadcast(P)),
                (subln[:, :], t_in["diff_subln"][0].partition_broadcast(P)),
                (gateb[:, :], t_in["nsa_gate_b"][0].partition_broadcast(P)),
            ]
            for j, n in enumerate(("diff_lambda_q1", "diff_lambda_k1", "diff_lambda_q2", "diff_lambda_k2")):
                loads.append((lqk[:, j, :], t_in[n][0].partition_broadcast(P)))
            for kv, n in enumerate(("nsa_pe_k", "nsa_pe_v")):
                for dup in range(2):
                    loads.append((perow[:, kv, dup, :], t_in[n][0]))
            for kv, n in enumerate(("nsa_k_w2", "nsa_v_w2")):
                loads.append((w2[:, kv, :, :], tiles(t_in[n][0])))
            for dst, src in gain_loads:
                act.dma_start(dst, src).then_inc(sem["gains_landed"], 16)
            for dst, src in loads:
                act.dma_start(dst, src).then_inc(sem["small_landed"], 16)
            pos = t_in["positions"]
            act.wait_ge(sem["posi_cleared"], 1)
            for t in range(NT):
                act.dma_start(posi[:, t:t + 1], pos[0, t * P:(t + 1) * P].unsqueeze(1),
                               allow_slow_non_contiguous=True).then_inc(sem["small_landed"], 16)
            ends = pos[0, 16:SEQ].rearrange("(n s) -> n s", s=16)[:, 15:16]
            for g in range(NG):
                act.dma_start(posi[g * NC:g * NC + NCMP, 2:3], ends,
                               allow_slow_non_contiguous=True).then_inc(sem["small_landed"], 16)
            assert len(loads) + 2 * NT == n_small and len(gain_loads) == n_gains

            def next_split(k):
                s = k + RING
                if s < n_slabs:
                    wait(act, slabs[k].released)
                    split_hi(act, s % RING, 16 * (s // RING + 1), slabs[s].n)

            for st in steps:
                if st.kind == "norm":
                    for j, (t, n) in enumerate(st.chunks):
                        if st.k == 0:
                            act.wait_ge(sem[f"x{t}_landed"], 16)
                        else:
                            act.wait_ge(sem["h_ready"], st.h_needed - 3 + j)
                        cols = slice(512 * n, 512 * (n + 1))
                        A(o[:, t, cols], h[:, t, cols], ACT.Square, accum_out=ssq[:, 2 * t + n:2 * t + n + 1])\
                            .then_inc(sem["ssq_made"], 1)
                    if st.k == 0:
                        act.wait_ge(filled[0], 1)
                        A(gains[:, :], psum[0][:, 0:35], ACT.Copy).then_inc(sem["gains_made"], 1)
                        split_hi(act, 0, 16, slabs[0].n)
                elif st.kind == "xt":
                    b = st.bank[0]
                    if st.n == 1:
                        act.wait_ge(sem["gains_made"], 1)
                    bank_filled(act, st.bank)
                    if st.gain is None:
                        A(xhi[:, st.chunks[0]:st.chunks[0] + 2, :].rearrange("p k n -> p (k n)"), psum[b][:, :],
                          ACT.Copy).then_inc(sem["xhi_made"], 1)
                    else:
                        for i, c in enumerate(st.chunks):
                            last = A(xhi[:, c, :], psum[b][:, i * SEQ:(i + 1) * SEQ], ACT.Copy,
                                     scale=gains[:, st.gain + c:st.gain + c + 1])
                        last.then_inc(sem["xhi_made"], 1)
                elif st.kind in ("proj", "up"):
                    if st.acc == "evac_made" and (st.kind == "up" or st.last):
                        if st.kind == "proj" and st.what == "ev_in" and st.group in (0, 1):
                            act.wait_ge(sem["t_made"], 2 * (st.group + 1))
                        bank_filled(act, st.bank)
                        for dst, src in evac_copies(st.what, st.group if st.kind == "proj" else 0, st.t, st.bank[0],
                                                    0 if st.kind == "proj" else st.half):
                            last = A(dst, src, ACT.Copy)
                        last.then_inc(sem["evac_made"], 1)
                elif st.kind == "split":
                    next_split(st.slab)
                elif st.kind in ("qkt", "kdt"):
                    bank_filled(act, st.bank)
                    A(t_dst(st), psum[st.bank[0]][:, :].rearrange("p (a n) -> p a n", a=2), ACT.Copy)\
                        .then_inc(sem["t_made"], 1)
                elif st.kind == "mqkt":
                    bank_filled(act, st.bank)
                    wait(act, st.free)
                    b = psum[st.bank[0]]
                    A(mla_qk(st.head, 0), b[0:MD, 0:SEQ], ACT.Copy)
                    A(mla_qk(st.head, 1), b[0:MD, SEQ:], ACT.Copy).then_inc(sem["t_made"], 1)
                elif st.kind == "tables":
                    for s in range(1, RING):
                        split_hi(act, s, 16, slabs[s].n)
                    act.wait_ge(filled[1], 1)
                    A(pet[:, :, :].rearrange("p a b -> p (a b)"), psum[1][:, 0:64], ACT.Copy)\
                        .then_inc(sem["pe_made"], 1)
                    act.wait_ge(sem["angles_made"], 1)
                    A(trig[:, :, :, :].rearrange("p a b c -> p (a b c)"),
                      red[:, :, :, :].rearrange("p a b c -> p (a b c)"), ACT.Sin).then_inc(sem["sin_made"], 1)
                    act.wait_ge(sem["lam_dots"], 1)
                    A(lam[:, 2:4], lam[:, 0:2], ACT.Exp).then_inc(sem["lam_exp"], 1)
                elif st.kind == "scores":
                    m = st.m
                    if m >= 4:
                        wait(act, prob_free[m - 4])
                    for t, cols in ((0, slice(0, P)), (1, slice(P, 3 * P))):
                        act.wait_ge(sem["masked"], 2 * m + t + 1)
                        A(prob[:, m % 4, cols], masked[:, m % 2, cols], ACT.Exp, bias=nmax[:, 2 * m + t:2 * m + t + 1],
                          scale=-1.0, accum_out=sums[:, 2 * m + t:2 * m + t + 1]).then_inc(sem["exped"], 1)
                elif st.kind == "turn" and st.diff:
                    bank_filled(act, st.bank)
                    wait(act, st.pv_before)
                    A(pt[:, st.uid % 2, :], psum[st.bank[0]][:, 0:SCORE_COLS], ACT.Copy)\
                        .then_inc(sem[f"pt_made{st.uid % 2}"], 1)
                elif st.kind == "blocks":
                    act.wait_ge(sem["xc_made"], st.kv + 1)
                    at = 64 * st.kv
                    A(xcs[:, :, at:at + NG * NC], xc[:, :, :, :].rearrange("p j g n -> p j (g n)"),
                      ACT.Copy).then_inc(sem["xch_made"], 1)
                elif st.kind == "compress":
                    if st.half:
                        bank_filled(act, st.bank)
                        rows = slice(64 * st.kv, 64 * st.kv + 64)
                        A(he[rows, :], psum[st.bank[0]][rows, 0:256], ACT.Copy).then_inc(sem["he_made"], 1)
                elif st.kind == "hid_turn":
                    bank_filled(act, st.bank)
                    if st.kv:
                        act.wait_ge(sem["gelu_out"], st.kv)
                    A(hid[:, :, :].rearrange("p c n -> p (c n)"), psum[st.bank[0]][:, 0:2 * NG * NC], ACT.Copy)\
                        .then_inc(sem["hid_read"], 1)
                elif st.kind == "gelu":
                    act.wait_ge(sem["gelu_in"], st.kv + 1)
                    A(hid3[:, :, :], hid2[:, :, :], ACT.Tanh, scale=float(np.sqrt(2 / np.pi)))\
                        .then_inc(sem["gelu_th"], 1)
                elif st.kind == "second":
                    if st.kv == 0:
                        bank_filled(act, st.bank)
                        src = psum[st.bank[0]][0:NG * NC, 0:HD].unsqueeze(1).broadcast_to([NG * NC, 2, HD])
                        A(kcn[:, :, :], src, ACT.Copy).then_inc(sem["kcn_made"], 1)
                elif st.kind == "kcmp":
                    bank_filled(act, st.bank)
                    act.wait_ge(sem["consts_made"], 1)
                    for u in range(2):
                        rows = slice(64 * u, 64 * u + 64)
                        last = A(kct[rows, :, u, :],
                                 psum[st.bank[0]][rows, 0:NG * NC].rearrange("p (g n) -> p g n", g=NG), ACT.Copy)
                    last.then_inc(sem["t_made"], 1)
                elif st.kind == "cscores":
                    act.wait_ge(sem["c_centred"], 1)
                    A(cs[:, :, :, :].rearrange("p t h n -> p (t h n)"), cs[:, :, :, :].rearrange("p t h n -> p (t h n)"),
                      ACT.Exp, scale=HD ** -0.5).then_inc(sem["c_exped"], 1)
                elif st.kind == "cturn":
                    bank_filled(act, st.bank)
                    A(pct[:, :, :].rearrange("p t n -> p (t n)"), psum[st.bank[0]][:, 0:NT * P], ACT.Copy)\
                        .then_inc(sem["pct_made"], 1)
                elif st.kind == "gates":
                    act.wait_ge(sem["gate_in"], 1)
                    A(gate[:, :, :], gate[:, :, :], ACT.Tanh, scale=0.5).then_inc(sem["gate_th"], 1)
                elif st.kind == "ffn":
                    s0, g0, u0, base = st.s0, st.g0, st.u0, st.base

                    def tanh(i):
                        act.wait_ge(filled[0], i + (g0 + 1))
                        if not isinstance(i, int) or base + i > 0:
                            act.wait_ge(sem["gated"], i + base)
                        A(th[:, :], psum[0][:, :], ACT.Tanh, scale=0.5).then_inc(sem["tanh_made"], 1)

                    def hidden(i):
                        act.wait_ge(sem["h_made"], i + (base + 1))
                        A(hhi[:, :], hf[:, :], ACT.Copy).then_inc(sem["hhi_made"], 1)

                    def body(i, more=True):
                        r = i * 16
                        q = [(s0 - 1 + RING + j) for j in range(3)]
                        tanh(i)
                        if more or s0 - 1 + 3 * i + RING < n_slabs:
                            split_hi(act, q[0] % RING, r + 16 * (q[0] // RING + 1), SLAB)
                        if more or s0 + 3 * i + RING < n_slabs:
                            act.wait_ge(filled[1], i + (u0 + 1))
                            split_hi(act, q[1] % RING, r + 16 * (q[1] // RING + 1), SLAB)
                        act.wait_ge(sem["down_done"], down_at + i)
                        hidden(i)
                        if more or s0 + 1 + 3 * i + RING < n_slabs:
                            split_hi(act, q[2] % RING, r + 16 * (q[2] // RING + 1), SLAB)

                    down_at = st.down_base
                    tanh(0)
                    split_hi(act, (s0 + 3) % RING, 16 * ((s0 + 3) // RING + 1), SLAB)
                    act.wait_ge(filled[1], u0 + 1)
                    split_hi(act, (s0 + 4) % RING, 16 * ((s0 + 4) // RING + 1), SLAB)
                    hidden(0)
                    body(1)
                    with act.Fori(2, NI - 1) as i:
                        body(i)
                    body(NI - 1, more=False)

        @block.vector
        def _(dve):
            V = nc.vector
            step = [0]

            def link(ins):
                step[0] += 1
                ins.then_inc(sem["dve_step"], 1)
                dve.wait_ge(sem["dve_step"], step[0])

            def next_split(k):
                s = k + RING
                if s < n_slabs and not pool_splits(s):
                    if s and pool_splits(s - 1):
                        dve.wait_ge(sem["lo_made"], s)
                    split_lo(dve, s % RING, s + 1, slabs[s].n)

            def root(src, scales, n):
                for c0, c1, scale in scales:
                    last = V.tensor_scalar(msq[:, c0:c1], src[:, c0:c1], scale, EPS, ALU.mult, ALU.add)
                last.then_inc(sem["msq_made"], 1)
                dve.wait_ge(sem["rstd_made"], n)

            def rope(x, cos, sin, w, n):
                if n > 1:
                    dve.wait_ge(sem["roped"], n - 1)
                r = w // 2
                shape = list(x.shape)
                a = rope_a[0:shape[0], 0:shape[1], 0:shape[2], 0:w]
                b = rope_b[0:shape[0], 0:shape[1], 0:shape[2], 0:w]

                def per_head(t):
                    return t.unsqueeze(2).broadcast_to(shape[:3] + [t.shape[-1]])

                V.tensor_tensor(a, x, per_head(cos), ALU.mult)
                V.tensor_tensor(b[:, :, :, 0:r], x[:, :, :, r:w], per_head(sin[:, :, 0:r]), ALU.mult)
                link(V.tensor_tensor(b[:, :, :, r:w], x[:, :, :, 0:r], per_head(sin[:, :, r:w]), ALU.mult))
                V.tensor_tensor(x, a, b, ALU.add).then_inc(sem["roped"], 1)

            for st in steps:
                if st.kind == "norm":
                    if st.k == 0:
                        dve.wait_ge(sem["ident_made"], 1)
                    dve.wait_ge(sem["ssq_made"], 4 * (st.k + 1))
                    v = ssq[:, 0:4].rearrange("p (t n) -> p t n", n=2)
                    link(V.tensor_tensor(msq[:, 0:2], v[:, :, 0], v[:, :, 1], ALU.add))
                    root(msq, [(0, NT, 1.0 / D)], st.n)
                    if st.k < 4:
                        for t in range(NT):
                            last = V.tensor_scalar(dg[:, t, :], ident[:, :], rstd[:, t:t + 1], None, ALU.mult)
                        last.then_inc(sem["diag_made"], 1)
                    else:
                        for t, n in TILE_ORDER:
                            cols = slice(512 * n, 512 * (n + 1))
                            V.scalar_tensor_tensor(o[:, t, cols], h[:, t, cols], rstd[:, t:t + 1], gfin[:, cols],
                                                   ALU.mult, ALU.mult).then_inc(sem["fin_made"], 1)
                    if st.k == 0:
                        split_lo(dve, 0, 1, slabs[0].n)
                elif st.kind == "xt":
                    b = st.bank[0]
                    dve.wait_ge(sem["xhi_made"], st.n)
                    if st.gain is None:
                        c = st.chunks[0]
                        V.tensor_tensor(xlo[:, c:c + 2, :].rearrange("p k n -> p (k n)"), psum[b][:, :],
                                        xhi[:, c:c + 2, :].rearrange("p k n -> p (k n)").bitcast(F32),
                                        ALU.subtract).then_inc(sem["xlo_made"], 1)
                    else:
                        for i, c in enumerate(st.chunks):
                            last = V.scalar_tensor_tensor(
                                xlo[:, c, :], psum[b][:, i * SEQ:(i + 1) * SEQ],
                                gains[:, st.gain + c:st.gain + c + 1], xhi[:, c, :].bitcast(F32), ALU.mult,
                                ALU.subtract)
                        last.then_inc(sem["xlo_made"], 1)
                elif st.kind == "tables":
                    for s in range(1, RING):
                        split_lo(dve, s, s + 1, slabs[s].n)
                    dve.wait_ge(sem["small_landed"], 16 * n_small)
                    dve.wait_ge(sem["consts_made"], 1)
                    V.tensor_reduce(fold[:, :], ident[:, :].rearrange("p (k n) -> p n k", n=NG * NC), AX.X, ALU.add)
                    link(V.tensor_copy(posf[:, :], posi[:, :]))
                    link(V.tensor_tensor(ang[:, :, :], posf[:, :].unsqueeze(2).broadcast_to([P, 3, 16]),
                                         invf[:, :].unsqueeze(1).broadcast_to([P, 3, 16]), ALU.mult))
                    link(V.tensor_scalar(turns[:, :, :], ang[:, :, :], 1.0 / (2 * np.pi), ROUND, ALU.mult, ALU.add))
                    link(V.tensor_scalar(turns[:, :, :], turns[:, :, :], ROUND, None, ALU.subtract))
                    for part in TWO_PI_PARTS:
                        link(V.scalar_tensor_tensor(ang[:, :, :], turns[:, :, :], -part, ang[:, :, :], ALU.mult,
                                                    ALU.add))
                    link(V.tensor_scalar(red[:, 0], ang[:, :, :], 3.1415925, -3.1415925, ALU.min, ALU.max))
                    link(V.scalar_tensor_tensor(ang[:, :, :], red[:, 0], -1.0, red[:, 0], ALU.mult, ALU.max))
                    V.tensor_scalar(red[:, 1], ang[:, :, :], -1.0, PI / 2, ALU.mult, ALU.add)\
                        .then_inc(sem["angles_made"], 1)
                    for j in range(2):
                        last = V.tensor_tensor_reduce(otmp[:, j * HD:(j + 1) * HD], lqk[:, 2 * j], lqk[:, 2 * j + 1], 1.0, 0.0,
                                                      ALU.mult, ALU.add, lam[:, j:j + 1])
                    last.then_inc(sem["lam_dots"], 1)
                    V.tensor_scalar(subln[:, :], subln[:, :], 1.0 - LAMBDA_INIT, None, ALU.mult)
                    dve.wait_ge(sem["sin_made"], 1)
                    for cc, sn, w, every in ((cc8, sn8, 16, 2), (cc16, sn16, 32, 1)):
                        r = w // 2
                        s_, c_ = trig[:, 0, :, 0:16:every], trig[:, 1, :, 0:16:every]
                        V.tensor_copy(cc[:, :, 0:r], c_)
                        V.tensor_copy(cc[:, :, r:w], c_)
                        V.tensor_scalar(sn[:, :, 0:r], s_, -1.0, None, ALU.mult)
                        link(V.tensor_copy(sn[:, :, r:w], s_))
                    dve.wait_ge(sem["lam_exp"], 1)
                    link(V.scalar_tensor_tensor(lam[:, 0:1], lam[:, 2:3], -1.0, lam[:, 3:4], ALU.mult, ALU.add))
                    link(V.tensor_scalar(lam[:, 0:1], lam[:, 0:1], -LAMBDA_INIT, None, ALU.add))
                elif st.kind in ("proj", "up"):
                    if st.kind == "proj" and st.acc == "h_ready" and st.last:
                        bank_filled(dve, st.bank)
                        if st.h_needed:
                            dve.wait_ge(sem["h_ready"], st.h_needed)
                        cols = slice(st.group * 512, (st.group + 1) * 512)
                        V.tensor_tensor(h[:, st.t, cols], psum[st.bank[0]][:, :], h[:, st.t, cols], ALU.add)\
                            .then_inc(sem["h_ready"], 1)
                elif st.kind == "split":
                    next_split(st.slab)
                elif st.kind == "rope":
                    if st.what == "kcmp":
                        dve.wait_ge(sem["kcn_made"], 1)
                    else:
                        dve.wait_ge(sem["evac_made"], st.evac)
                    if st.what == "kcmp":
                        rope(kcn[:, :, 0:16].unsqueeze(1), cc8[0:NG * NC, 2:3, :], sn8[0:NG * NC, 2:3, :], 16, st.n)
                    elif st.what == "nat":
                        v = nat[:, st.buf].rearrange("p t (h d) -> p t h d", d=HD)
                        rope(v[:, :, :, 0:16], cc8[:, 0:NT, :], sn8[:, 0:NT, :], 16, st.n)
                    elif st.what in ("kslc", "kwin"):
                        w = 0 if st.what == "kslc" else 1
                        v = nat2[:, :, w].rearrange("p t g u d -> p t (g u) d")
                        rope(v[:, :, :, 0:16], cc8[:, 0:NT, :], sn8[:, 0:NT, :], 16, st.n)
                    elif st.what == "kpe":
                        rope(kpe[:, :, :].unsqueeze(2), cc16[:, 0:NT, :], sn16[:, 0:NT, :], RO, st.n)
                        dve.wait_ge(sem["roped"], st.n)
                        dve.wait_ge(sem["t_made"], st.t_needed)
                        for t in range(NT):
                            last = V.tensor_copy(km[:, t, :, NOPE:], kpe[:, t].unsqueeze(1).broadcast_to([P, NH, RO]))
                        last.then_inc(sem["kpe_spread"], 1)
                    else:
                        rope(qm[:, :, :, NOPE:], cc16[:, 0:NT, :], sn16[:, 0:NT, :], RO, st.n)
                elif st.kind == "scores":
                    m, b = st.m, psum[st.bank[0]]
                    bank_filled(dve, st.bank)
                    if m >= 2:
                        dve.wait_ge(sem["exped"], 2 * (m - 1))
                    scale = score_operands(st.group, st.unit, st.part)[2]
                    for t, cols in ((0, slice(0, P)), (1, slice(P, 3 * P))):
                        V.tensor_tensor_reduce(masked[:, m % 2, cols], b[:, cols], tri[:, cols], -scale, 3e38, ALU.add,
                                               ALU.min, nmax[:, 2 * m + t:2 * m + t + 1]).then_inc(sem["masked"], 1)
                elif st.kind == "combine":
                        m0, m1 = st.maps
                        dve.wait_ge(sem["exped"], 2 * (m1 + 1))
                        c = slice(2 * m0, 2 * m0 + 4)
                        link(V.tensor_scalar(rinv[:, c], sums[:, c], 1e-30, None, ALU.max))
                        link(V.reciprocal(rinv[:, c], rinv[:, c]))
                        link(V.tensor_scalar(rinv[:, 2 * m1:2 * m1 + 2], rinv[:, 2 * m1:2 * m1 + 2], lam[:, 0:1], None,
                                             ALU.mult))
                        if st.unit >= 2:
                            wait(dve, comb_free[st.unit - 2])
                        for t, cols in ((0, slice(0, P)), (1, slice(P, 3 * P))):
                            ins = V.tensor_scalar(comb[:, st.unit % 2, cols], prob[:, m0 % 4, cols],
                                                  rinv[:, 2 * m0 + t:2 * m0 + t + 1], None, ALU.mult)
                        link(ins)
                        for t, cols in ((0, slice(0, P)), (1, slice(P, 3 * P))):
                            ins = V.scalar_tensor_tensor(comb[:, st.unit % 2, cols], prob[:, m1 % 4, cols],
                                                         rinv[:, 2 * m1 + t:2 * m1 + t + 1],
                                                         comb[:, st.unit % 2, cols], ALU.mult, ALU.add)
                        ins.then_inc(sem["combined"], 1)
                elif st.kind == "turn":
                    if not st.diff:
                        bank_filled(dve, st.bank)
                        wait(dve, st.pv_before)
                        V.tensor_copy(pt[:, st.uid % 2, :], psum[st.bank[0]][:, 0:SCORE_COLS])\
                            .then_inc(sem[f"pt_made{st.uid % 2}"], 1)
                elif st.kind == "out":
                    bank_filled(dve, st.banks[0])
                    bank_filled(dve, st.banks[1])
                    if st.group == "diff":
                        ob = o[:, :, 512:1024]
                        for t in range(NT):
                            last = V.tensor_copy(ob[:, t, :], psum[st.banks[t][0]][:, :])
                            last.then_inc(sem["o_banks_read"], 1)
                        dve.wait_ge(sem["o_banks_read"], st.read)
                        junk = [comb[:, 0, :], comb[:, 1, :], otmp[:, :]]
                        for j in range(NT * NDH):
                            v = ob[:, j // NDH, (j % NDH) * P:(j % NDH + 1) * P]
                            last = V.tensor_tensor_reduce(junk[j // 3][:, (j % 3) * P:(j % 3 + 1) * P], v, v, 1.0, 0.0,
                                                          ALU.mult, ALU.add, ssq[:, j:j + 1])
                        link(last)
                        root(ssq, [(0, NT * NDH, 1.0 / (2 * HD))], st.n)
                        for t in range(NT):
                            v = ob[:, t, :].rearrange("p (a d) -> p a d", d=2 * HD)
                            r = rstd[:, 4 * t:4 * t + 4].unsqueeze(2).broadcast_to([P, NDH, 2 * HD])
                            last = V.tensor_tensor(v, v, r, ALU.mult)
                        link(last)
                        for t in range(NT):
                            v = ob[:, t, :].rearrange("p (a d) -> p a d", d=2 * HD)
                            g = subln[:, :].unsqueeze(1).broadcast_to([P, NDH, 2 * HD])
                            last = V.tensor_tensor(v, v, g, ALU.mult)
                        last.then_inc(sem["o_ready"], 1)
                        continue
                    if st.group == "cmp":
                        src = csum[:, :].rearrange("p (t h) -> p t h", t=NT)
                    else:
                        dve.wait_ge(sem["exped"], 2 * (st.maps[-1] + 1))
                        c = slice(2 * st.maps[0], 2 * st.maps[-1] + 2)
                        src = sums[:, c].rearrange("p (h t) -> p t h", t=NT)
                    link(V.tensor_scalar(coef[:, :, :], src, 1e-30, None, ALU.max))
                    link(V.reciprocal(coef[:, :, :], coef[:, :, :]))
                    branch = {"cmp": 0, "slc": 1, "win": 2}.get(st.group)
                    if branch is not None:
                        dve.wait_ge(sem["gates_made"], 1)
                        gv = gate[:, :, :].rearrange("p t (h b) -> p t h b", b=3)[:, :, :, branch]
                        link(V.tensor_tensor(coef[:, :, :], coef[:, :, :], gv, ALU.mult))
                    lo = 512 if st.group == "mla" else 0
                    for t in range(NT):
                        v = psum[st.banks[t][0]][:, :].rearrange("p (h d) -> p h d", d=HD)
                        c = coef[:, t].unsqueeze(2).broadcast_to([P, NH, HD])
                        if st.group in ("slc", "cmp"):
                            V.tensor_tensor(otmp[:, :].rearrange("p (h d) -> p h d", d=HD), v, c, ALU.mult)\
                                .then_inc(sem["o_banks_read"], 1)
                            dve.wait_ge(sem["o_banks_read"], st.read - NT + t + 1)
                            add = V.tensor_tensor(o[:, t, 0:512], o[:, t, 0:512], otmp[:, :], ALU.add)
                            if st.group == "cmp" and t == NT - 1:
                                add.then_inc(sem["o_ready"], 1)
                            else:
                                link(add)
                        else:
                            V.tensor_tensor(o[:, t, lo:lo + 512].rearrange("p (h d) -> p h d", d=HD), v, c, ALU.mult)\
                                .then_inc(sem["o_banks_read"], 1)
                    dve.wait_ge(sem["o_banks_read"], st.read)
                elif st.kind == "blocks":
                    b = psum[st.bank[0]]
                    bank_filled(dve, st.bank)
                    if st.kv == 0:
                        dve.wait_ge(sem["gains_made"], 1)
                        dve.wait_ge(sem["pe_made"], 1)
                    else:
                        dve.wait_ge(sem["xch_made"], 1)
                        dve.wait_ge(sem["xc_lo_made"], 1)
                    v = b[:, :].rearrange("p (g n s) -> p s g n", g=NG, s=16)
                    for par in range(2):
                        rows = slice(64 * par, 64 * par + 64)
                        for late in range(2):
                            pe_cols = pet[rows, st.kv, 16 * late + par:16 * late + 16:2]
                            last = V.tensor_tensor(
                                xc[rows, 8 * late:8 * late + 8, :, 0:NCMP], v[rows, par:16:2, :, late:late + NCMP],
                                pe_cols.unsqueeze(2).unsqueeze(3).broadcast_to([64, 8, NG, NCMP]), ALU.add)
                    last.then_inc(sem["xc_made"], 1)
                    dve.wait_ge(sem["xch_made"], st.kv + 1)
                    dve.wait_ge(sem["xc_made"], st.kv + 1)
                    at = 64 * st.kv
                    V.tensor_tensor(xcs[:, :, at + 32:at + 64], xc[:, :, :, :].rearrange("p j g n -> p j (g n)"),
                                    xcs[:, :, at:at + 32].bitcast(F32), ALU.subtract)\
                        .then_inc(sem["xc_lo_made"], 1)
                elif st.kind == "gelu":
                    dve.wait_ge(sem["hid_read"], st.hid)
                    link(V.tensor_tensor(hid2[:, :, :], hid[:, :, :], hid[:, :, :], ALU.mult))
                    link(V.tensor_scalar(hid2[:, :, :], hid2[:, :, :], 0.044715, 1.0, ALU.mult, ALU.add))
                    V.tensor_tensor(hid2[:, :, :], hid2[:, :, :], hid[:, :, :], ALU.mult).then_inc(sem["gelu_in"], 1)
                    dve.wait_ge(sem["gelu_th"], st.kv + 1)
                    link(V.scalar_tensor_tensor(hid3[:, :, :], hid3[:, :, :], 1.0, hid[:, :, :], ALU.add, ALU.mult))
                    if st.kv == 0:
                        V.tensor_scalar(hk[:, :, :], hid3[:, :, :], 0.5, None, ALU.mult).then_inc(sem["gelu_out"], 1)
                    else:
                        v = hid3[:, :, :].rearrange("p c (g n) -> p (c g) n", g=NG).unsqueeze(2)
                        V.tensor_scalar(hv[:, :, :, :].rearrange("p c (g r) n -> p (c g) r n", g=NG),
                                        v.broadcast_to([P, 2 * NG, NH // NG, NC]), 0.5, None, ALU.mult)\
                            .then_inc(sem["gelu_out"], 1)
                elif st.kind == "second":
                    if st.kv:
                        bank_filled(dve, st.bank)
                        src = psum[st.bank[0]][:, 0:HD].unsqueeze(1).broadcast_to([P, NH, HD])
                        V.tensor_tensor(vbd[:, :, :], src, bdm[:, :].unsqueeze(2).broadcast_to([P, NH, HD]), ALU.mult)\
                            .then_inc(sem["vbd_made"], 1)
                elif st.kind == "cscores":
                    bank_filled(dve, st.bank)
                    v = psum[st.bank[0]][:, 0:NT * NH * NC].rearrange("p (t h n) -> p t h n", t=NT, n=NC)
                    V.tensor_tensor(cs[:, :, :, :], v, cmask[:, :, :].unsqueeze(2).broadcast_to([P, NT, NH, NC]),
                                    ALU.add).then_inc(sem["c_masked"], 1)
                    dve.wait_ge(sem["c_masked"], 1)
                    rows = cs[:, :, :, :].rearrange("p t h n -> p (t h) n")
                    link(V.tensor_reduce(cmx[:, :], rows, AX.X, ALU.max))
                    V.tensor_tensor(rows, rows, cmx[:, :].unsqueeze(2).broadcast_to([P, NT * NH, NC]), ALU.subtract)\
                        .then_inc(sem["c_centred"], 1)
                    dve.wait_ge(sem["c_exped"], 1)
                    link(V.tensor_tensor(cs[:, :, :, :], cs[:, :, :, :],
                                         cvalid[:, :, :].unsqueeze(2).broadcast_to([P, NT, NH, NC]), ALU.mult))
                    V.tensor_reduce(csum[:, :], rows, AX.X, ALU.add).then_inc(sem["c_ready"], 1)
                elif st.kind == "gates":
                    dve.wait_ge(sem["evac_made"], st.evac)
                    V.tensor_tensor(gate[:, :, :], gate[:, :, :],
                                    gateb[:, :].unsqueeze(1).broadcast_to([P, NT, NH * 3]), ALU.add)\
                        .then_inc(sem["gate_in"], 1)
                    dve.wait_ge(sem["gate_th"], 1)
                    V.tensor_scalar(gate[:, :, :], gate[:, :, :], 1.0, 0.5, ALU.add, ALU.mult)\
                        .then_inc(sem["gates_made"], 1)
                elif st.kind == "latent_norm":
                    dve.wait_ge(sem["evac_made"], st.evac)
                    for j, (lo, hi) in enumerate(((0, LQ), (LQ, LQ + LKV))):
                        for t in range(NT):
                            last = V.tensor_tensor_reduce(lats[:, t, lo:hi], lat[:, t, lo:hi], lat[:, t, lo:hi],
                                                          1.0, 0.0, ALU.mult, ALU.add,
                                                          ssq[:, 2 * j + t:2 * j + t + 1])
                    link(last)
                    root(ssq, [(0, NT, 1.0 / LQ), (NT, 2 * NT, 1.0 / LKV)], st.n)
                    for j, (lo, hi) in enumerate(((0, LQ), (LQ, LQ + LKV))):
                        for t in range(NT):
                            last = V.tensor_scalar(lats[:, t, lo:hi], lat[:, t, lo:hi],
                                                   rstd[:, 2 * j + t:2 * j + t + 1], None, ALU.mult)
                    last.then_inc(sem["lat_made"], 1)
                elif st.kind == "ffn":
                    s0, u0, base = st.s0, st.u0, st.base

                    def gated(i):
                        dve.wait_ge(sem["tanh_made"], i + (base + 1))
                        V.scalar_tensor_tensor(ga[:, :], th[:, :], 1.0, psum[0][:, :], ALU.add, ALU.mult)\
                            .then_inc(sem["gated"], 1)

                    def hidden(i):
                        dve.wait_ge(filled[1], i + (u0 + 1))
                        dve.wait_ge(sem["gated"], i + (base + 1))
                        V.scalar_tensor_tensor(hf[:, :], ga[:, :], 0.5, psum[1][:, :], ALU.mult, ALU.mult)\
                            .then_inc(sem["h_made"], 1)

                    def hidden_lo(i):
                        dve.wait_ge(sem["hhi_made"], i + (base + 1))
                        V.tensor_tensor(hlo[:, :], hf[:, :], hhi[:, :].bitcast(F32), ALU.subtract)\
                            .then_inc(sem["hlo_made"], 1)

                    def body(i, more=True):
                        r = i * RING
                        gated(i)
                        if more or s0 - 1 + 3 * i + RING < n_slabs:
                            split_lo(dve, (s0 + 2) % RING, r + (s0 - 1 + RING + 1), SLAB)
                        hidden(i)
                        if more or s0 + 3 * i + RING < n_slabs:
                            split_lo(dve, (s0 + 3) % RING, r + (s0 + RING + 1), SLAB)
                        hidden_lo(i)
                        if more or s0 + 1 + 3 * i + RING < n_slabs:
                            split_lo(dve, (s0 + 4) % RING, r + (s0 + 1 + RING + 1), SLAB)

                    gated(0)
                    split_lo(dve, s0 % RING, s0 + 4, SLAB)
                    hidden(0)
                    split_lo(dve, (s0 + 1) % RING, s0 + 5, SLAB)
                    hidden_lo(0)
                    body(1)
                    with dve.Fori(2, NI - 1) as i:
                        body(i)
                    body(NI - 1, more=False)
                    for t in range(NT):
                        for n in range(2):
                            use = st.out[2 * t + n]
                            bank_filled(dve, use)
                            cols = slice(n * 512, (n + 1) * 512)
                            V.tensor_tensor(h[:, t, cols], psum[use[0]][:, :], h[:, t, cols], ALU.add)\
                                .then_inc(sem["h_ready"], 1)


_INS = ["x", "positions", "attn_norm", "ffn_norm", "final_norm", "ffn_w_gate", "ffn_w_up", "ffn_w_down", "ev_w_in",
        "ev_w_out", "diff_lambda_q1", "diff_lambda_k1", "diff_lambda_q2", "diff_lambda_k2", "diff_subln", "od_w_in",
        "od_w_out", "nsa_gate_b", "nsa_pe_k", "nsa_pe_v", "nsa_k_w1", "nsa_k_w2", "nsa_v_w1", "nsa_v_w2",
        "mla_q_norm", "mla_w_uq", "mla_kv_norm", "mla_w_ukv"]


def kernel(**inputs):
    import concourse.bacc as bacc
    from concourse.bass_utils import run_bass_kernel_spmd

    nc = bacc.Bacc("TRN2", target_bir_lowering=False, num_devices=1)
    arrays, aps = {}, {}
    for name in _INS:
        a = np.ascontiguousarray(inputs[name])
        arrays[f"in_{name}"] = a
        aps[name] = nc.dram_tensor(f"in_{name}", a.shape, mybir.dt.from_np(a.dtype), kind="ExternalInput").ap()
    out = nc.dram_tensor("out", (1, SEQ, D), F32, kind="ExternalOutput").ap()
    build(nc, aps, out)
    r = run_bass_kernel_spmd(nc, [arrays], core_ids=[0])
    return r.results[0]["out"]
```

```python
from contextlib import ExitStack

import numpy as np
import concourse.bass as bass
from concourse import mybir

F32 = mybir.dt.float32
F32R = mybir.dt.float32r
I32 = mybir.dt.int32
ALU = mybir.AluOpType
ACT = mybir.ActivationFunctionType
AX = mybir.AxisListType

P = 128
SEQ = 256
NT = SEQ // P
D = 1024
KT = D // P
FF = 2816
NI = FF // 256
HD = 64
NH = 8
NDH = 4
NG = 2
NCMP = SEQ // 16 - 1
NC = NCMP + 1
LQ, LKV, RO, NOPE = 256, 128, 32, 64
MD = NOPE + RO
EPS = 1e-5
THETA = 500000.0
LAMBDA_INIT = 0.8 - 0.6 * float(np.exp(-0.3 * 0))
NEG = -1e30
RING = 3
SLAB = 2048
SCORE_COLS = 3 * P
OD_W = [512, 512, 512, 184]
MLA_ROOM = 6
PI = float(np.float32(np.pi))
TWO_PI_PARTS = (6.28125, 1.93500518798828125e-3, 3.01991598196e-7)
ROUND = 1.5 * 2.0 ** 23


SPLIT_LAGS = {"ev_in": (2, 1), "ev_out": (2, 1), "od_in": (2, 0), "uq": (4, 4),
              "ukv": (2, 1), "w1": (2, 2), "od_out": (2, 1), "down": (1, 0)}
TURN_LAG = 3
LAYER_NORMS, LATENT_NORMS = 8, 10
TILE_ORDER = [(t, n) for t in range(NT) for n in range(2)]


class Step:

    def __init__(self, kind,
                 acc=None, bank=None, banks=None, base=None, buf=None, chunks=None, combined=None,
                 diff=None, down_base=None, dst=None, end=None, evac=None,
                 first=None, g0=None, gain=None, gate_wait=None, group=None, h_needed=None,
                 half=None, head=None, hid=None, k=None, k0=None, kts=None, kv=None, last=None,
                 layer=None, m=None, maps=None, n=None, needs=None, out=None, part=None, pt=None,
                 pv_before=None, read=None, ready=None, released=None, free=None, roped=None, s0=None,
                 slab=None, src=None, t=None, t_needed=None, u0=None, uid=None, unit=None,
                 up_wait=None, what=None, where=None, which=None, width=None,
                 x_needed=None):
        self.kind = kind
        self.acc = acc
        self.bank = bank
        self.banks = banks
        self.base = base
        self.buf = buf
        self.chunks = chunks
        self.combined = combined
        self.diff = diff
        self.down_base = down_base
        self.dst = dst
        self.end = end
        self.evac = evac
        self.first = first
        self.free = free
        self.g0 = g0
        self.gain = gain
        self.gate_wait = gate_wait
        self.group = group
        self.h_needed = h_needed
        self.half = half
        self.head = head
        self.hid = hid
        self.k = k
        self.k0 = k0
        self.kts = kts
        self.kv = kv
        self.last = last
        self.layer = layer
        self.m = m
        self.maps = maps
        self.n = n
        self.needs = needs
        self.out = out
        self.part = part
        self.pt = pt
        self.pv_before = pv_before
        self.read = read
        self.ready = ready
        self.released = released
        self.roped = roped
        self.s0 = s0
        self.slab = slab
        self.src = src
        self.t = t
        self.t_needed = t_needed
        self.u0 = u0
        self.uid = uid
        self.unit = unit
        self.up_wait = up_wait
        self.what = what
        self.where = where
        self.which = which
        self.width = width
        self.x_needed = x_needed


class Plan:

    def __init__(self):
        self.steps, self.slabs = [], []
        self.count = {}
        self.bank_free = [None] * 8
        self.bank_fills = [0] * 8
        for b in range(2):
            self.take(b, (("gains_made", "pe_made")[b], 1))
        self.tbank = 0
        self.maps = self.units = 0

    def tick(self, name, n=1):
        self.count[name] = self.count.get(name, 0) + n
        return self.count[name]

    def add(self, kind, **fields):
        s = Step(kind, **fields)
        self.steps.append(s)
        return s

    def take(self, b, release):
        wait, self.bank_free[b] = self.bank_free[b], release
        self.bank_fills[b] += 1
        return (b, wait, self.bank_fills[b])

    def turn(self, release):
        b = 2 + self.tbank % 2
        self.tbank += 1
        return self.take(b, release)

    def slab(self, what, n, *where):
        self.slabs.append(Step("slab", what=what, n=n, where=where, released=None))
        return len(self.slabs) - 1

    def norm(self, k, order):
        self.add("norm", k=k, h_needed=self.count.get("h_ready", 0), chunks=order, n=self.tick("rstd_made"),
                 m=self.tick("msq_made"))

    def x_transposed(self, src, ready, chunks, gain):
        n = self.tick("xlo_made")
        self.tick("xhi_made")
        release = ("xlo_made", n)
        bank = self.take(4 + chunks[0] // 2, release) if src in ("x", "h") and chunks[0] >= 4 else self.turn(release)
        self.add("xt", src=src, ready=ready, chunks=chunks, gain=gain, n=n, bank=bank)
        return n

    def projection(self, what, group, width, slabs, banks, x_needed, kts, x0=0, acc="evac_made",
                   x_base=None, root=None):
        uses = []
        for t in range(NT):
            uses.append(self.take(banks[t], (acc, self.tick(acc))))
        at = x0
        for i, s in enumerate(slabs):
            last = i == len(slabs) - 1
            for t in range(NT):
                end = t == NT - 1
                if end:
                    self.slabs[s].released = ("filled", uses[t][0], uses[t][2]) if last else \
                        ("slab_used", self.tick("slab_used"))
                self.add("proj", what=what, group=group, width=width, slab=s, t=t, bank=uses[t], kts=kts[i],
                         k0=at, first=i == 0, last=last, end=end, x_needed=x_needed[i], acc=acc, base=x_base,
                         ready=root)
            at += kts[i]
        return uses

    def transposed(self, kind, **fields):
        n = self.tick("t_made")
        self.add(kind, n=n, bank=self.turn(("t_made", n)), **fields)
        return n

    def ffn(self, layer):
        s0 = len(self.slabs)
        order = [("gate", 0), ("up", 0)]
        for i in range(1, NI):
            order += [("gate", i), ("up", i), ("down", i - 1)]
        order.append(("down", NI - 1))
        st = self.add("ffn", layer=layer, s0=s0, base=NI * layer, down_base=(NI - 1) * layer,
                      g0=self.bank_fills[0], u0=self.bank_fills[1],
                      gate_wait=self.bank_free[0], up_wait=self.bank_free[1])
        for what, i in order:
            s = self.slab(what, SLAB, layer, i)
            rel = {"gate": ("filled", 0, st.g0 + i + 1), "up": ("filled", 1, st.u0 + i + 1),
                   "down": ("down_done", st.down_base + i + 1)}[what]
            self.slabs[s].released = rel
        st.n = self.tick("row_made")
        st.bank = self.turn(("row_made", st.n))
        self.bank_fills[0] += NI
        self.bank_fills[1] += NI
        self.bank_free[0] = ("gate_scaled", st.base + NI)
        self.bank_free[1] = ("h_made", st.base + NI)
        st.x_needed = self.count["xlo_made"]
        st.out = [self.take(4 + b, ("h_ready", self.tick("h_ready"))) for b in range(4)]
        self.slabs[-1].released = ("filled", 7, st.out[3][2])
        st.end, st.slab = True, len(self.slabs) - 1


def interleave(*lists):
    keyed = []
    for n, steps in enumerate(lists):
        work = [{"proj": 5, "up": 4}[s.kind] if isinstance(s, Step) else 1 for s in steps]
        done = 0
        for w, s in zip(work, steps):
            keyed.append(((done + w / 2) / sum(work), n, s))
            done += w
    return [s for _, _, s in sorted(keyed, key=lambda k: k[:2])]


def attention_rounds(*groups):
    units = [(name, u, per) for name, n, per in groups for u in range(n)]
    n_units = {name: n for name, n, _ in groups}
    rounds = []
    for r in range(len(units) + TURN_LAG + 1):
        turn, value, out, scores, combine = [], [], [], [], []
        if TURN_LAG <= r < len(units) + TURN_LAG:
            name, u, _ = units[r - TURN_LAG]
            turn.append((name, "turn", u, 0))
        if r > TURN_LAG:
            name, u, _ = units[r - TURN_LAG - 1]
            value.append((name, "value", u, 0))
            if u == n_units[name] - 1:
                out.append((name, "out", 0, 0))
        if r < len(units):
            name, u, per = units[r]
            scores += [(name, "scores", u, i) for i in range(per)]
        if 1 <= r < len(units) + 1:
            name, u, per = units[r - 1]
            if per == 2:
                combine.append((name, "combine", u, 0))
        rounds.append(turn + value + out + scores + combine)
    return rounds


def later_splits(steps, slabs):
    out, due = [], []
    for i, s in enumerate(steps):
        if s.kind == "ffn":
            out += [Step(kind, slab=k) for _, kind, k in due]
            due = []
        out.append(s)
        if s.kind == "xt":
            continue
        following = steps[i + 1].kind if i + 1 < len(steps) else None
        while due and due[0][0] <= i and following not in ("norm", "xt"):
            _, kind, k = due.pop(0)
            out.append(Step(kind, slab=k))
        if s.end:
            dense = following == "proj"
            hi_lag, lo_lag = (1, 0) if dense else SPLIT_LAGS[slabs[s.slab].what]
            due.append((i + hi_lag, "split_hi", s.slab))
            due.append((i + hi_lag + lo_lag, "split_lo", s.slab))
            due.sort(key=lambda d: (d[0], d[2]))
    return out


def make_plan():
    p = Plan()

    def read_out(name, banks, maps):
        for b, _, fill in banks:
            assert p.bank_fills[b] == fill
            p.bank_free[b] = ("o_banks_read", p.tick("o_banks_read"))
        read[name] = p.count["o_banks_read"]
        p.add("out", group=name, banks=banks, maps=maps, read=read[name],
              n=p.tick("rstd_made") if name == "diff" else None)
        if name == "cmp":
            p.tick("o_ready")

    read = {}

    def emit(tokens, groups):
        for tok in tokens:
            if isinstance(tok, Step):
                p.steps.append(tok)
                continue
            if callable(tok):
                tok()
                continue
            name, what, u, i = tok
            g = groups[name]
            if what == "scores":
                m = p.maps
                p.maps += 1
                g["maps"].append(m)
                b = m % 2
                p.add("scores", group=name, unit=u, part=i, m=m, bank=p.take(b, ("masked", 2 * (m + 1))),
                      needs=g["needs"])
            elif what == "combine":
                p.add("combine", group=name, unit=u, maps=g["maps"][2 * u:2 * u + 2], n=p.tick("combined"))
            elif what == "turn":
                n_maps = g["per"]
                uid = p.units
                p.units += 1
                g["uids"].append(uid)
                n = p.tick(f"pt_made{uid % 2}")
                p.add("turn", group=name, unit=u, uid=uid, maps=g["maps"][u * n_maps:(u + 1) * n_maps], n=n,
                      bank=p.turn((f"pt_made{uid % 2}", n)), diff=n_maps == 2, pv_before=g_pv.get(uid - 2),
                      combined=u + 1)
            elif what == "value":
                last = u == g["n"] - 1
                if u == 0:
                    g["banks"] = [p.take(4 + t, None) for t in range(NT)]
                uid = g["uids"][u]
                rel = ("filled", 5, g["banks"][1][2]) if last else ("pv_done", p.tick("pv_done"))
                g_pv[uid] = rel
                pt = next(s for s in p.steps if s.kind == "turn" and s.uid == uid)
                p.add("value", group=name, unit=u, uid=uid, pt=pt.n, banks=g["banks"], first=u == 0, last=last,
                      needs=g["v_needs"])
            else:
                read_out(name, g["banks"], g["maps"])

    g_pv = {}

    def group(n, per):
        return {"n": n, "per": per, "maps": [], "uids": [], "needs": None, "v_needs": None}

    evac = {}

    def cut(start):
        made = p.steps[start:]
        del p.steps[start:]
        return made

    def project(key, what, group, width, slabs, banks, x_needed, x_base=None):
        start = len(p.steps)
        p.projection(what, group, width, slabs, banks, x_needed, [4] * len(slabs), x_base=x_base,
                     root=p.count["rstd_made"])
        evac[key] = p.count["evac_made"]
        return cut(start)

    def rope_step(what, key, w=16, buf=None):
        def step():
            roped[key] = p.tick("roped")
            p.add("rope", what=what, buf=buf, evac=evac[key], n=roped[key], t_needed=p.count.get("t_made", 0))
        return step

    def qk_turn(g, key, buf, half):
        return lambda: p.transposed("qkt", dst=(g, half), buf=buf, roped=roped[key])

    def now(g):
        def step():
            groups[g]["needs"] = p.count["t_made"]
        return step

    roped = {}
    groups = {"moba": group(NH, 1), "diff": group(NDH, 2), "slc": group(NH, 1), "win": group(NH, 1),
              "mla": group(NH, 1)}

    p.add("start")
    for j in range(KT // 2):
        p.x_transposed("x", None, (2 * j, 2 * j + 1), 0)
    p.add("first_splits")
    p.norm(0, TILE_ORDER)
    ev = {}
    for i, g in enumerate((3, 4, 5, 0, 1, 2)):
        slabs = [p.slab("ev_in", SLAB, g, h) for h in range(2)]
        ev[g] = project(g, "ev_in", g, 512, slabs, (4, 5) if i in (0, 2) else (6, 7), [4, 4], 0 if i == 0 else None)
    groups["diff"]["v_needs"] = evac[5]
    groups["moba"]["v_needs"] = evac[2]
    rounds = attention_rounds(("diff", NDH, 2), ("moba", NH, 1))

    def over(first, last, fill):
        emit(interleave([tok for r in rounds[first:last] for tok in r], fill), groups)

    emit(ev[3][:1] + [lambda: p.add("tables")] + ev[3][1:] + ev[4][:2] + [rope_step("nat", 3, buf=0)] + ev[4][2:]
         + ev[5][:1] + [qk_turn(3, 3, 0, 0), rope_step("nat", 4, buf=1)] + ev[5][1:2] + [qk_turn(3, 3, 0, 1)]
         + ev[5][2:3] + [qk_turn(4, 4, 1, 0)] + ev[5][3:] + [qk_turn(4, 4, 1, 1), now("diff")], groups)
    over(0, 4, ev[0] + ev[1][:1] + [rope_step("nat", 0, buf=0)] + ev[1][1:3] + [qk_turn(0, 0, 0, 0)] + ev[1][3:]
         + [qk_turn(0, 0, 0, 1), rope_step("nat", 1, buf=1)] + ev[2][:1])
    emit([qk_turn(1, 1, 1, 0)] + ev[2][1:2] + [qk_turn(1, 1, 1, 1), now("moba")], groups)
    over(4, 6, ev[2][2:])
    over(6, 6 + TURN_LAG, [])

    def head_norm():
        p.add("head_norm", n=p.count["rstd_made"])
        p.tick("o_ready")

    emit([head_norm], groups)
    over(6 + TURN_LAG, 7 + TURN_LAG, [])

    def out_half(what, half, ready):
        base = p.count["xlo_made"]
        before = p.count.get("h_ready", 0)
        turns = [lambda j=j: p.x_transposed("o", ready, (2 * j, 2 * j + 1), None) for j in (2 * half, 2 * half + 1)]
        start = len(p.steps)
        for g in range(2):
            slab = p.slab(what, SLAB, g, half)
            p.projection(what, g, 512, [slab], (6, 7), [base + 2], [4], x0=4 * half, acc="h_ready")
            for s in p.steps[-NT:]:
                s.h_needed = before
        return turns + cut(start)

    def both_halves(first, what, half, ready, last_group, n_ready):
        a = out_half(what, half, ready)
        over(first, len(rounds), a[:-2])
        b = out_half(what, 1 - half, (read[last_group], n_ready))
        emit(a[-2:-1] + b[:1] + a[-1:] + b[1:], groups)

    both_halves(7 + TURN_LAG, "ev_out", 1, (read["diff"], 1), "moba", 1)

    def norm_and_ffn(layer):
        for j in range(KT // 2):
            p.x_transposed("h", p.count["h_ready"] - (2 if j < 2 else 0), (2 * j, 2 * j + 1), 16 + 8 * layer)
        p.norm(2 * layer + 1, [(t, n) for n, t in TILE_ORDER])
        p.ffn(layer)

    norm_and_ffn(0)

    base = p.count["xlo_made"]
    for j in range(KT // 2):
        p.x_transposed("h", p.count["h_ready"] - (1 if j < 2 else 0), (2 * j, 2 * j + 1), 8)
    p.norm(2, TILE_ORDER)
    od = {}
    for i, g in enumerate((2, 0, 3, 1)):
        slabs = [p.slab("od_in", 4 * OD_W[g], g, h) for h in range(2)]
        od[g] = project("o%d" % g, "od_in", g, OD_W[g], slabs, (4, 5) if i == 0 else (6, 7),
                        [base + 4, base + 4], base if i == 0 else None)

    def k_turn(which, key):
        return lambda: p.transposed("kdt", which=which, roped=roped[key + "k"], evac=evac[key])

    def k_rope(what, key):
        def step():
            roped[key + "k"] = p.tick("roped")
            p.add("rope", what=what, evac=evac[key], n=roped[key + "k"])
        return step

    def blocks(kv):
        def step():
            n = p.tick("xc_lo_made")
            p.tick("xc_made")
            p.add("blocks", kv=kv, n=n, evac=evac["o1"], bank=p.turn(("xc_made", n)))
        return step

    emit(od[2] + od[0][:1] + [k_rope("kwin", "o2")] + od[0][1:2] + [k_turn(1, "o2")] + od[0][2:]
         + od[3][:1] + [rope_step("nat", "o0", buf=0)] + od[3][1:2] + [qk_turn(6, "o0", 0, 0)] + od[3][2:3]
         + [qk_turn(6, "o0", 0, 1), now("win")] + od[3][3:], groups)
    groups["win"]["v_needs"] = evac["o2"]
    groups["slc"]["v_needs"] = evac["o1"]

    latent_root = []

    def latent_norm():
        latent_root.append(p.tick("rstd_made"))
        p.add("latent_norm", evac=evac["o3"], n=latent_root[0], m=p.tick("msq_made"))

    def latents():
        xb = p.count["xlo_made"]
        turns = [lambda: p.x_transposed("latent", evac["o3"], (0, 1), 32),
                 lambda: p.x_transposed("latent", evac["o3"], (2,), 32)]
        start = len(p.steps)
        uq = p.slab("uq", 2 * 768, 0)
        ukv = p.slab("ukv", 1024, 0)
        for what, s, k0, kts, need in (("uq", uq, 0, 2, xb + 1), ("ukv", ukv, 2, 1, xb + 2)):
            for half in range(2):
                uses = [p.take(6 + t, ("evac_made", p.tick("evac_made"))) for t in range(NT)]
                for t in range(NT):
                    if half and t:
                        p.slabs[s].released = ("filled", 7, uses[t][2])
                    p.add("up", ready=latent_root[0], what=what, half=half, slab=s, t=t, bank=uses[t], kts=kts,
                          k0=k0, x_needed=need,
                          end=bool(half and t), acc="evac_made",
                          width=768 if what == "uq" else 1024)
        evac["mla"] = p.count["evac_made"]
        return turns + cut(start)

    rounds = attention_rounds(("win", NH, 1), ("slc", NH, 1), ("mla", NH, 1))
    over(0, 5, [lambda: p.add("gates", evac=evac["o2"])] + od[1][:1]
         + [latent_norm]
         + od[1][1:])
    ups = latents()
    over(5, 8, [k_rope("kslc", "o1"), ups[0], blocks(0), ups[1], blocks(1), k_turn(0, "o1"), now("slc"), ups[2],
                rope_step("kpe", "o3"), ups[3]])

    def compress(kv):
        def half(h):
            def step():
                if h == 0:
                    c["slabs"] = [p.slab("w1", SLAB, kv, i) for i in range(2)]
                    c["bank"] = p.take(6 + kv, ("he_made", kv + 1))
                p.slabs[c["slabs"][h]].released = ("filled", 6 + kv, c["bank"][2]) if h else \
                    ("slab_used", p.tick("slab_used"))
                p.add("compress", kv=kv, half=h, slab=c["slabs"][h], bank=c["bank"], x_needed=kv + 1, end=True)
            return step

        def turned():
            p.add("hid_turn", kv=kv, bank=p.turn(("hid_read", kv + 1)))
        c = {}
        return [half(0), half(1), turned]

    def gelu(kv):
        return lambda: p.add("gelu", kv=kv, hid=kv + 1)

    def second(kv):
        def step():
            if kv == 0:
                c["n"] = p.tick("kcn_made")
                p.add("second", kv=kv, bank=p.turn(("kcn_made", 1)))
            else:
                p.add("second", kv=kv, bank=p.turn(("vbd_made", 1)))
        c = {}
        return step

    def c_rope():
        roped["kc"] = p.tick("roped")
        p.add("rope", what="kcmp", n=roped["kc"])

    def c_turn():
        n2 = p.tick("t_made")
        p.add("kcmp", roped=roped["kc"], n=n2, bank=p.turn(("t_made", n2)))

    def c_scores():
        p.add("cscores", t_needed=p.count["t_made"], bank=p.take(6, ("c_masked", 1)))

    def c_probs():
        p.add("cturn", bank=p.turn(("pct_made", 1)))

    def c_values():
        b4 = [p.take(6 + t, None) for t in range(NT)]
        p.add("cvalue", banks=b4)
        read_out("cmp", b4, [])

    def mla_turn(h, bank):
        def step():
            free = None
            if h >= MLA_ROOM:
                s = next(s for s in p.steps if s.kind == "scores" and s.group == "mla" and s.unit == h - MLA_ROOM)
                free = ("filled", s.bank[0], s.bank[2])
            n = p.tick("t_made")
            p.add("mqkt", head=h, roped=roped["mla"], free=free, n=n, bank=p.take(bank, ("t_made", n)))
            groups["mla"]["needs"] = p.count["t_made"]
        return step

    groups["mla"]["v_needs"] = evac["mla"]
    k_layer, v_layer = compress(0), compress(1)
    over(8, 11, ups[4:])
    over(11, 12, [rope_step("qpe", "mla")] + k_layer[:2] + [mla_turn(0, 7)] + k_layer[2:])
    over(12, 14, v_layer[:1] + [gelu(0), mla_turn(1, 6)] + v_layer[1:2] + [second(0)])
    over(14, 16, v_layer[2:] + [c_rope, mla_turn(2, 6), gelu(1), c_turn, mla_turn(3, 7)])
    over(16, 19, [second(1), mla_turn(4, 6), c_scores, mla_turn(5, 7)])
    done = 17 + TURN_LAG
    over(19, done, [c_probs, mla_turn(6, 6), mla_turn(7, 7)])
    over(done, done + 2, [])
    emit([c_values], groups)
    both_halves(done + 2, "od_out", 0, (read["cmp"], 2), "mla", 2)
    norm_and_ffn(1)
    p.norm(4, TILE_ORDER)
    p.steps = later_splits(p.steps, p.slabs)
    return p


def build(nc, t_in, out):
    plan = make_plan()
    steps, slabs = plan.steps, plan.slabs
    n_slabs = len(slabs)
    with ExitStack() as ctx:
        def sb(name, shape, dt=F32):
            return ctx.enter_context(nc.sbuf_tensor(name, shape, dt))

        raw = [sb(f"raw{i}", [P, SLAB]) for i in range(RING)]
        whi = [sb(f"whi{i}", [P, SLAB], F32R) for i in range(RING)]
        wlo = [sb(f"wlo{i}", [P, SLAB], F32R) for i in range(RING)]
        h = sb("h", [P, NT, D])
        o = sb("o", [P, NT, D])
        xhi = sb("xhi", [P, KT, SEQ], F32R)
        xlo = sb("xlo", [P, KT, SEQ], F32R)
        nat = sb("nat", [P, 2, NT, 512])
        qk = sb("qk", [P, 4, 4, SEQ])
        vals = sb("vals", [P, 2, NT, 512])
        vnsa = sb("vnsa", [P, 2, NT, P])
        nat2 = sb("nat2", [P, NT, 4, NG, 2, HD])
        kd = sb("kd", [P, 2, NG, SEQ])
        masked = sb("masked", [P, 2, SCORE_COLS])
        prob = sb("prob", [P, 4, SCORE_COLS])
        comb = sb("comb", [P, 2, SCORE_COLS])
        pt = sb("pt", [P, 2, SCORE_COLS])
        n_maps = plan.maps
        nmax = sb("nmax", [P, 2 * n_maps])
        sums = sb("sums", [P, 2 * n_maps])
        rinv = sb("rinv", [P, 2 * n_maps])
        coef = sb("coef", [P, NT, NH])
        rope_a = sb("rope_a", [P, NT, NH, RO])
        rope_b = sb("rope_b", [P, NT, NH, RO])
        otmp = sb("otmp", [P, 512])
        xc = sb("xc", [P, 16, NG, NC])
        xcs = sb("xcs", [P, 16, 4 * NG * NC], F32R)
        fold = sb("fold", [P, NG * NC])
        hid = sb("hid", [P, 2, NG * NC])
        hid2 = sb("hid2", [P, 2, NG * NC])
        hid3 = sb("hid3", [P, 2, NG * NC])
        hk = sb("hk", [P, 2, NG * NC])
        hv = sb("hv", [P, 2, NH, NC])
        kcn = sb("kcn", [NG * NC, 2, HD])
        kct = sb("kct", [P, NG, 2, NC])
        vbd = sb("vbd", [P, NH, HD])
        cs = sb("cs", [P, NT, NH, NC])
        cmx = sb("cmx", [P, NT * NH])
        csum = sb("csum", [P, NT * NH])
        pct = sb("pct", [P, NT, P])
        gate = sb("gate", [P, NT, NH * 3])
        lat = sb("lat", [P, NT, LQ + LKV])
        lat_squares = comb[:, :, :].rearrange("p a n -> p (a n)").rearrange("p (t n) -> p t n", t=NT)
        kpe = sb("kpe", [P, NT, RO])
        def room(flat, d):
            return flat[:, 0:NT * NH * d].rearrange("p (t h d) -> p t h d", t=NT, h=NH)

        qm = room(nat[:, :, :, :].rearrange("p b t n -> p (b t n)"), MD)
        km = room(nat2[:, :, :, :, :, :].rearrange("p t w g u d -> p (t w g u d)"), MD)
        vm = room(vals[:, 0].rearrange("p t n -> p (t n)"), HD)
        free = masked[:, :, :].rearrange("p a n -> p (a n)"), prob[:, :, :].rearrange("p a n -> p (a n)")
        dg = free[0][:, 0:NT * P].rearrange("p (t n) -> p t n", t=NT)
        th = free[0][:, 0:512]
        ga, hf, gr = (free[1][:, 512 * i:512 * (i + 1)] for i in range(3))
        rrow = pt[:, 0, 0:SEQ]
        flat = xcs[:, :, :].rearrange("p j n -> p (j n)")
        hhi, hlo = flat[:, 0:512], flat[:, 512:1024]
        he = vals[:, 1, 0, 0:256]
        ident = sb("ident", [P, P])
        ones = sb("ones", [P, P])
        tri = sb("tri", [P, SCORE_COLS])
        cmask = sb("cmask", [P, NT, NC])
        cvalid = sb("cvalid", [P, NT, NC])
        bdm = sb("bdm", [P, NH])
        invf = sb("invf", [P, 16])
        mhalf = sb("mhalf", [P, 8])
        posi = sb("posi", [P, 3], I32)
        posf = sb("posf", [P, 3])
        ang = sb("ang", [P, 3, 16])
        turns = sb("turns", [P, 3, 16])
        red = sb("red", [P, 2, 3, 16])
        trig = sb("trig", [P, 2, 3, 16])
        cc8 = sb("cc8", [P, 3, 16])
        sn8 = sb("sn8", [P, 3, 16])
        cc16 = sb("cc16", [P, 3, 32])
        sn16 = sb("sn16", [P, 3, 32])
        grow = sb("grow", [35, P])
        gains = sb("gains", [P, 35])
        perow = sb("perow", [32, 2, 2, HD])
        pet = sb("pet", [P, 2, 32])
        w2 = sb("w2", [P, 2, 2, HD])
        gfin = sb("gfin", [P, D])
        subln = sb("subln", [P, 2 * HD])
        gateb = sb("gateb", [P, NH * 3])
        lqk = sb("lqk", [P, 4, HD])
        lam = sb("lam", [P, 4])
        ssq = sb("ssq", [P, 8])
        msq = sb("msq", [P, 8])
        rstd = sb("rstd", [P, 14])

        def mla_slot(head):
            return 4 + 2 * (head % MLA_ROOM)

        def mla_qk(head, which):
            slot = mla_slot(head) + which
            return qk[0:MD, slot // 4, slot % 4, :]

        psum = [ctx.enter_context(nc.psum_tensor(f"bank{b}", [P, 512], F32)) for b in range(8)]

        sem = {n: ctx.enter_context(nc.semaphore(n)) for n in (
            "x0_landed", "x1_landed", "small_landed", "hi_made", "slab_used", "ssq_made", "rstd_made",
            "msq_made", "diag_made", "gains_landed", "gains_made", "ident_made", "pe_made", "xhi_made",
            "xlo_made", "evac_made", "roped", "t_made", "masked", "exped", "pt_made0", "pt_made1", "pv_done",
            "o_banks_read", "o_ready", "combined", "tanh_made", "gate_scaled", "row_made", "gated", "h_made",
            "hhi_made", "hlo_made", "down_done", "h_ready", "dve_step", "pool_step", "posi_cleared",
            "consts_made", "angles_made", "sin_made", "lam_dots", "lam_exp", "xc_made", "xch_made",
            "xc_lo_made", "he_made", "head_squares", "kcn_made", "vbd_made", "gelu_in", "gelu_th", "gelu_out",
            "hid_read", "c_masked", "c_centred", "c_exped", "c_ready", "pct_made", "gate_in", "gate_th",
            "gates_made", "half_landed", "half_hi_made", "half_lo_made", "kpe_spread", "h_gained", "fin0_made",
            "fin1_made", "stored")}
        filled = [ctx.enter_context(nc.semaphore(f"filled{b}")) for b in range(8)]
        lo_made = [ctx.enter_context(nc.semaphore(f"lo_made{i}")) for i in range(RING)]
        landed = [ctx.enter_context(nc.semaphore(f"landed{i}")) for i in range(RING)]
        block = ctx.enter_context(nc.Block())

        def wait(eng, what):
            if what is None:
                return
            if what[0] == "filled":
                eng.wait_ge(filled[what[1]], what[2])
            else:
                eng.wait_ge(sem[what[0]], what[1])

        prob_free, comb_free = {}, {}
        for st in steps:
            if st.kind == "turn":
                turned = ("filled", st.bank[0], st.bank[2])
                for m in st.maps:
                    prob_free[m] = ("combined", st.combined) if st.diff else turned
                if st.diff:
                    comb_free[st.unit] = turned

        def bank_filled(eng, bank):
            eng.wait_ge(filled[bank[0]], bank[2])

        def tiles(ap):
            return ap.rearrange("(k p) n -> p k n", p=P)

        ev_in, ev_out = tiles(t_in["ev_w_in"][0]), tiles(t_in["ev_w_out"][0])
        od_in, od_out = tiles(t_in["od_w_in"][0]), tiles(t_in["od_w_out"][0])
        w_gate = [tiles(t_in["ffn_w_gate"][l]) for l in range(2)]
        w_up = [tiles(t_in["ffn_w_up"][l]) for l in range(2)]
        w_down = [tiles(t_in["ffn_w_down"][l]) for l in range(2)]
        w1 = [tiles(t_in[n][0]) for n in ("nsa_k_w1", "nsa_v_w1")]

        def slab_source(s):
            what, w = s.what, s.where
            if what in ("ev_in", "ev_out", "od_out"):
                v = {"ev_in": ev_in, "ev_out": ev_out, "od_out": od_out}[what]
                return v[:, 4 * w[1]:4 * w[1] + 4, 512 * w[0]:512 * (w[0] + 1)]
            if what == "od_in":
                return od_in[:, 4 * w[1]:4 * w[1] + 4, 512 * w[0]:512 * w[0] + OD_W[w[0]]]
            if what == "w1":
                return w1[w[0]][:, 8 * w[1]:8 * w[1] + 8, :]
            if what == "uq":
                return tiles(t_in["mla_w_uq"][0])
            if what == "ukv":
                return tiles(t_in["mla_w_ukv"][0])
            return ffn_source(what, *w)

        def ffn_source(what, layer, i):
            if what == "gate":
                return w_gate[layer][:, :, bass.ds(256 * i, 256)]
            if what == "up":
                return w_up[layer][:, :, bass.ds(256 * i, 256)]
            return w_down[layer][:, bass.ds(2 * i, 2), :]

        def parts(tile, k, n):
            return tile[:, 0:k * n].rearrange("p (k n) -> p k n", k=k)

        n_gains, n_small = 4, 17

        def pool_splits(k):
            if k < RING or k >= n_slabs or slabs[k - RING].what == "down":
                return False
            return slabs[k].what in ("ev_in", "od_in", "uq") or slabs[k].what == "w1" and slabs[k].where[1] == 0

        @block.sync
        def _(sp):
            x = t_in["x"][0].rearrange("(t p) d -> p t d", p=P)
            for t in range(NT):
                sp.dma_start(h[:, t, :], x[:, t, :]).then_inc(sem[f"x{t}_landed"], 16)

            def load(slot, source, n, k, split):
                if split is not None:
                    sp.wait_ge(lo_made[slot], split)
                sp.dma_start(parts(raw[slot], k, n // k), source).then_inc(landed[slot], 16)

            def small_loads():
                loads = [
                    (gfin[:, :], t_in["final_norm"].partition_broadcast(P)),
                    (subln[:, :], t_in["diff_subln"][0].partition_broadcast(P)),
                    (gateb[:, :], t_in["nsa_gate_b"][0].partition_broadcast(P)),
                ]
                for j, n in enumerate(("diff_lambda_q1", "diff_lambda_k1", "diff_lambda_q2", "diff_lambda_k2")):
                    loads.append((lqk[:, j, :], t_in[n][0].partition_broadcast(P)))
                for kv, n in enumerate(("nsa_pe_k", "nsa_pe_v")):
                    for dup in range(2):
                        loads.append((perow[:, kv, dup, :], t_in[n][0]))
                for kv, n in enumerate(("nsa_k_w2", "nsa_v_w2")):
                    loads.append((w2[:, kv, :, :], tiles(t_in[n][0])))
                for dst, src in loads:
                    sp.dma_start(dst, src).then_inc(sem["small_landed"], 16)
                pos = t_in["positions"]
                sp.wait_ge(sem["posi_cleared"], 1)
                for t in range(NT):
                    sp.dma_start(posi[:, t:t + 1], pos[0, t * P:(t + 1) * P].unsqueeze(1),
                                   allow_slow_non_contiguous=True).then_inc(sem["small_landed"], 16)
                ends = pos[0, 16:SEQ].rearrange("(n s) -> n s", s=16)[:, 15:16]
                for g in range(NG):
                    sp.dma_start(posi[g * NC:g * NC + NCMP, 2:3], ends,
                                   allow_slow_non_contiguous=True).then_inc(sem["small_landed"], 16)
                assert len(loads) + 2 * NT == n_small

            ffn_at = {s.s0: s for s in steps if s.kind == "ffn"}
            sp.wait_ge(sem["gains_landed"], 16 * n_gains)
            s = 0
            while s < n_slabs:
                sl = slabs[s]
                if s in ffn_at:
                    st = ffn_at[s]
                    lyr, s0 = st.layer, st.s0

                    def ffn_slab(k, what, i, split):
                        load((s0 + k) % RING, ffn_source(what, lyr, i), SLAB, 2 if what == "down" else KT, split)

                    for k, (what, i) in enumerate((("gate", 0), ("up", 0), ("gate", 1), ("up", 1), ("down", 0))):
                        ffn_slab(k, what, i, (s0 + k) // RING)
                    with sp.Fori(2, NI) as i:
                        for j, (what, back) in enumerate((("gate", 0), ("up", 0), ("down", 1))):
                            ffn_slab(2 + j, what, i - back, i + (s0 - 1 + j) // RING)
                    ffn_slab(3 * NI - 1, "down", NI - 1, (s0 + 3 * NI - 1) // RING)
                    s += 3 * NI
                    continue
                if s == RING:
                    small_loads()
                if s == 0:
                    for half, landing in ((0, sem["half_landed"]), (1, landed[0])):
                        sp.dma_start(parts(raw[0], 4, 512)[:, 2 * half:2 * half + 2, :],
                                     slab_source(sl)[:, 2 * half:2 * half + 2, :]).then_inc(landing, 16)
                    s += 1
                    continue
                k = slab_source(sl).shape[1]
                load(s % RING, slab_source(sl), sl.n, k, s // RING if s >= RING else None)
                s += 1
            for t in (0, 1):
                sp.wait_ge(sem[f"fin{t}_made"], 1)
                sp.dma_start(out[0, t * P:(t + 1) * P, :], h[:, t, :]).then_inc(sem["stored"], 16)
            sp.wait_ge(sem["stored"], 32)

        @block.gpsimd
        def _(pool):
            step = [0]

            def made(ins):
                step[0] += 1
                ins.then_inc(sem["pool_step"], 1)

            made(pool.memset(ident[:, :], 0.0))
            pool.wait_ge(sem["pool_step"], step[0])
            pool.affine_select(out=ident[:, :], in_=ident[:, :], compare_op=ALU.not_equal, fill=1.0, base=0,
                               pattern=[[-1, P]], channel_multiplier=1).then_inc(sem["ident_made"], 1)
            pool.memset(posi[:, :], 0).then_inc(sem["posi_cleared"], 1)
            made(pool.memset(mhalf[:, :], -0.5))
            pool.wait_ge(sem["pool_step"], step[0])

            def root(st, n, col=0):
                if st.kind != "out":
                    pool.wait_ge(sem["msq_made"], st.m)
                pool.tensor_tensor(rstd[:, col:col + n], msq[:, 0:n], mhalf[:, 0:n], ALU.pow)\
                    .then_inc(sem["rstd_made"], 1)

            norms = [s for s in steps if s.kind == "norm"]
            root(norms[0], NT, LAYER_NORMS)
            made(pool.memset(tri[:, :], 0.0))
            made(pool.memset(cmask[:, :, :], 0.0))
            made(pool.memset(cvalid[:, :, :], 1.0))
            made(pool.memset(bdm[:, :], 1.0))
            made(pool.memset(ones[:, :], 1.0))
            made(pool.memset(kct[:, :, :, :], 0.0))
            for i in range(16):
                pool.memset(invf[:, i:i + 1], float(np.float32(1.0 / THETA ** (i / 16))))
            pool.memset(xc[:, :, :, :], 0.0)
            pool.wait_ge(sem["pool_step"], step[0])
            for c in (0, 2 * P):
                made(pool.affine_select(out=tri[:, c:c + P], in_=tri[:, c:c + P], compare_op=ALU.is_ge, fill=NEG,
                                        base=0, pattern=[[-1, P]], channel_multiplier=1))
            for m, fill in ((cmask, NEG), (cvalid, 0.0)):
                made(pool.affine_select(out=m[:, :, :], in_=m[:, :, :], compare_op=ALU.is_ge, fill=fill, base=-31,
                                        pattern=[[P, NT], [-16, NC]], channel_multiplier=1))
            made(pool.affine_select(out=bdm[:, :], in_=bdm[:, :], compare_op=ALU.is_ge, fill=0.0, base=0,
                                    pattern=[[-NC, NH]], channel_multiplier=1))
            pool.wait_ge(sem["pool_step"], step[0])
            pool.affine_select(out=bdm[:, :], in_=bdm[:, :], compare_op=ALU.is_ge, fill=0.0, base=NC - 1,
                               pattern=[[NC, NH]], channel_multiplier=-1).then_inc(sem["consts_made"], 1)

            for st in steps:
                if st.kind == "norm" and st.k > 0:
                    root(st, NT, LAYER_NORMS if st.k == 2 else 0)
                elif st.kind == "out" and st.group == "diff":
                    pool.wait_ge(sem["head_squares"], 1)
                    made(pool.tensor_scalar(msq[:, 0:NT * NDH], ssq[:, 0:NT * NDH], 1.0 / (2 * HD), EPS, ALU.mult,
                                            ALU.add))
                    pool.wait_ge(sem["pool_step"], step[0])
                    root(st, NT * NDH)
                elif st.kind == "latent_norm":
                    root(st, 2 * NT, LATENT_NORMS)
                elif st.kind == "split_lo" and pool_splits(st.slab + RING):
                    k = st.slab + RING
                    pool.wait_ge(sem["hi_made"], k + 1)
                    n = slabs[k].n
                    pool.tensor_tensor(wlo[k % RING][:, 0:n], raw[k % RING][:, 0:n],
                                       whi[k % RING][:, 0:n].bitcast(F32), ALU.subtract).then_inc(lo_made[k % RING], 1)

        def evac_copies(what, group, t, bank, half=0):
            b = psum[bank]
            if what == "ev_in":
                if group in (2, 5):
                    return [(vals[:, group // 3, t, :], b[:, :])]
                return [(nat[:, group % 3 % 2, t, :], b[:, :])]
            if what == "uq":
                return [(qm[:, t, 4 * half:4 * half + 4, :], b[:, 0:4 * MD].rearrange("p (h d) -> p h d", h=4))]
            if what == "ukv":
                v = b[:, :].rearrange("p (h d) -> p h d", h=4)
                return [(km[:, t, 4 * half:4 * half + 4, 0:NOPE], v[:, :, 0:NOPE]),
                        (vm[:, t, 4 * half:4 * half + 4, :], v[:, :, NOPE:])]

            def twice(c):
                v = b[:, c:c + P].rearrange("p (g d) -> p g d", g=NG).unsqueeze(2)
                return v.broadcast_to([P, NG, 2, HD])

            if group == 0:
                return [(nat[:, 0, t, :], b[:, :])]
            if group == 1:
                return [(nat2[:, t, 2], twice(0)), (nat2[:, t, 3], twice(128)), (nat2[:, t, 0], twice(256)),
                        (vnsa[:, 0, t, :], b[:, 384:512])]
            if group == 2:
                return [(nat2[:, t, 1], twice(0)), (vnsa[:, 1, t, :], b[:, 128:256]),
                        (gate[:, t, :], b[:, 256:280]), (lat[:, t, 0:232], b[:, 280:512])]
            return [(lat[:, t, 232:384], b[:, 0:152]), (kpe[:, t, :], b[:, 152:184])]

        def score_operands(group, unit, part):
            if group == "mla":
                return mla_qk(unit, 0), mla_qk(unit, 1), MD ** -0.5
            if group == "diff":
                lo = 64 * part
                return qk[lo:lo + HD, 2, unit, :], qk[lo:lo + HD, 3, unit, :], HD ** -0.5
            lo = 64 * (unit % 2)
            q = qk[lo:lo + HD, 0, unit // 2, :]
            if group == "moba":
                return q, qk[lo:lo + HD, 1, unit // 2, :], HD ** -0.5
            return q, kd[lo:lo + HD, 0 if group == "slc" else 1, unit // 4, :], HD ** -0.5

        def value_operand(group, unit, kt):
            if group == "mla":
                return vm[:, kt, unit, :]
            if group == "diff":
                return vals[:, 1, kt, unit * P:(unit + 1) * P]
            if group == "moba":
                return vals[:, 0, kt, unit * HD:(unit + 1) * HD]
            g = unit // 4
            return vnsa[:, 0 if group == "slc" else 1, kt, g * HD:(g + 1) * HD]

        def source(name):
            return {"x": h, "h": h, "o": o, "latent": lat}[name]

        def t_dst(st):
            if st.kind == "qkt":
                g, half = st.dst
                row = {0: 0, 1: 1, 3: 2, 4: 3, 6: 0}[g]
                return qk[:, row, 2 * half:2 * half + 2, :]
            return kd[:, st.which]

        def split_hi(act, slot, rounds_wait, n):
            act.wait_ge(landed[slot], rounds_wait)
            nc.scalar.activation(whi[slot][:, 0:n], raw[slot][:, 0:n], ACT.Copy).then_inc(sem["hi_made"], 1)

        def split_lo(dve, slot, count, n):
            dve.wait_ge(sem["hi_made"], count)
            nc.vector.tensor_tensor(wlo[slot][:, 0:n], raw[slot][:, 0:n], whi[slot][:, 0:n].bitcast(F32),
                                    ALU.subtract).then_inc(lo_made[slot], 1)

        @block.tensor
        def _(pe):
            def turn(dst, src, rows=P):
                return nc.tensor.transpose(dst, src, ident[0:rows, 0:rows])

            def three(dst, a, b, first, last):
                nc.tensor.matmul(dst, a[0], b[0], start=first, stop=False)
                nc.tensor.matmul(dst, a[1], b[0], start=False, stop=False)
                return nc.tensor.matmul(dst, a[0], b[1], start=False, stop=last)

            pe.wait_ge(sem["ident_made"], 1)
            pe.wait_ge(sem["gains_landed"], 16 * n_gains)
            turn(psum[0][:, 0:35], grow[:, :], 35).then_inc(filled[0], 1)

            def gate_or_up(which, slot, split, bank_sem, bank_value, x_base=None):
                pe.wait_ge(lo_made[slot], split)
                if bank_sem is not None:
                    pe.wait_ge(bank_sem, bank_value)
                hi, lo = parts(whi[slot], KT, 256), parts(wlo[slot], KT, 256)
                for c in range(2):
                    cols = slice(c * P, (c + 1) * P)
                    for k in range(KT):
                        if x_base is not None and c == 0 and k % 2 == 0:
                            pe.wait_ge(sem["xlo_made"], x_base + k // 2 + 1)
                        last = three(psum[which][:, c * SEQ:(c + 1) * SEQ], (hi[:, k, cols], lo[:, k, cols]),
                                     (xhi[:, k, :], xlo[:, k, :]), k == 0, k == KT - 1)
                last.then_inc(filled[which], 1)

            def down(slot, split, hid_count, first, final):
                pe.wait_ge(lo_made[slot], split)
                pe.wait_ge(sem["hlo_made"], hid_count)
                hi, lo = parts(whi[slot], 2, D), parts(wlo[slot], 2, D)
                for t in range(NT):
                    for n in range(2):
                        for c in range(2):
                            rows = slice(c * SEQ + t * P, c * SEQ + (t + 1) * P)
                            cols = slice(n * 512, (n + 1) * 512)
                            last = three(psum[4 + 2 * t + n][:, :], (hhi[:, rows], hlo[:, rows]),
                                         (hi[:, c, cols], lo[:, c, cols]), first and c == 0, final and c == 1)
                        if final:
                            last.then_inc(filled[4 + 2 * t + n], 1)
                if not final:
                    last.then_inc(sem["down_done"], 1)

            for st in steps:
                if st.kind == "tables":
                    pe.wait_ge(sem["small_landed"], 16 * n_small)
                    for kv in range(2):
                        last = turn(psum[1][:, 32 * kv:32 * kv + 32], perow[:, kv].rearrange("t u d -> t (u d)"), 32)
                    last.then_inc(filled[1], 1)
                elif st.kind == "xt":
                    if st.src == "h":
                        pe.wait_ge(sem["h_ready"], st.ready)
                    elif st.src == "x":
                        pe.wait_ge(sem["x0_landed"], 16)
                        pe.wait_ge(sem["x1_landed"], 16)
                    elif st.src == "o":
                        pe.wait_ge(sem["o_banks_read"], st.ready[0])
                        pe.wait_ge(sem["o_ready"], st.ready[1])
                    else:
                        pe.wait_ge(sem["evac_made"], st.ready)
                    b, w, _ = st.bank
                    wait(pe, w)
                    for i, c in enumerate(st.chunks):
                        for t in range(NT):
                            dst = psum[b][:, i * SEQ + t * P:i * SEQ + (t + 1) * P]
                            src = source(st.src)[:, t, c * P:(c + 1) * P]
                            last = turn(dst, src)
                    last.then_inc(filled[b], 1)
                elif st.kind == "proj":
                    slot = st.slab % RING
                    b, w, _ = st.bank
                    if st.slab or st.t:
                        pe.wait_ge(lo_made[slot], st.slab // RING + 1)
                    if st.base is None:
                        pe.wait_ge(sem["xlo_made"], st.x_needed)
                    if st.first:
                        wait(pe, w)
                    hi, lo = parts(whi[slot], st.kts, st.width), parts(wlo[slot], st.kts, st.width)
                    rows = slice(st.t * P, (st.t + 1) * P)
                    for k in range(st.kts):
                        if st.base is not None and st.t == 0 and k % 2 == 0:
                            pe.wait_ge(sem["xlo_made"], st.base + (st.k0 + k) // 2 + 1)
                            if st.slab == 0:
                                if k == 0:
                                    pe.wait_ge(sem["half_lo_made"], 1)
                                else:
                                    pe.wait_ge(lo_made[0], 1)
                        last = three(psum[b][:, 0:st.width], (xhi[:, st.k0 + k, rows], xlo[:, st.k0 + k, rows]),
                                     (hi[:, k, :], lo[:, k, :]), st.first and k == 0, st.last and k == st.kts - 1)
                    if st.last:
                        last.then_inc(filled[b], 1)
                    elif st.end:
                        last.then_inc(sem["slab_used"], 1)
                elif st.kind == "up":
                    slot = st.slab % RING
                    b, w, _ = st.bank
                    pe.wait_ge(lo_made[slot], st.slab // RING + 1)
                    pe.wait_ge(sem["xlo_made"], st.x_needed)
                    wait(pe, w)
                    hi, lo = parts(whi[slot], st.kts, st.width), parts(wlo[slot], st.kts, st.width)
                    rows = slice(st.t * P, (st.t + 1) * P)
                    n = st.width // 2
                    cols = slice(st.half * n, (st.half + 1) * n)
                    for k in range(st.kts):
                        last = three(psum[b][:, 0:n], (xhi[:, st.k0 + k, rows], xlo[:, st.k0 + k, rows]),
                                     (hi[:, k, cols], lo[:, k, cols]), k == 0, k == st.kts - 1)
                    last.then_inc(filled[b], 1)
                elif st.kind == "qkt":
                    b, w, _ = st.bank
                    pe.wait_ge(sem["roped"], st.roped)
                    wait(pe, w)
                    for i in range(2):
                        c = 2 * st.dst[1] + i
                        for t in range(NT):
                            last = turn(psum[b][:, i * SEQ + t * P:i * SEQ + (t + 1) * P],
                                        nat[:, st.buf, t, c * P:(c + 1) * P])
                    last.then_inc(filled[b], 1)
                elif st.kind in ("kdt", "blocks"):
                    b, w, _ = st.bank
                    pe.wait_ge(sem["evac_made"], st.evac)
                    if st.kind == "kdt":
                        pe.wait_ge(sem["roped"], st.roped)
                    which = st.which if st.kind == "kdt" else 2 + st.kv
                    wait(pe, w)
                    for g in range(NG):
                        for t in range(NT):
                            last = turn(psum[b][:, g * SEQ + t * P:g * SEQ + (t + 1) * P],
                                        nat2[:, t, which, g].rearrange("p u d -> p (u d)"))
                    last.then_inc(filled[b], 1)
                elif st.kind == "mqkt":
                    b, w, _ = st.bank
                    pe.wait_ge(sem["roped"], st.roped)
                    pe.wait_ge(sem["kpe_spread"], 1)
                    wait(pe, w)
                    for i, src in enumerate((qm, km)):
                        for t in range(NT):
                            last = turn(psum[b][0:MD, i * SEQ + t * P:i * SEQ + (t + 1) * P], src[:, t, st.head, :])
                    last.then_inc(filled[b], 1)
                elif st.kind == "scores":
                    b, w, _ = st.bank
                    q, k, _ = score_operands(st.group, st.unit, st.part)
                    pe.wait_ge(sem["t_made"], st.needs)
                    wait(pe, w)
                    nc.tensor.matmul(psum[b][:, 0:P], q[:, 0:P], k[:, 0:P], start=True, stop=True)
                    nc.tensor.matmul(psum[b][:, P:3 * P], q[:, P:2 * P], k, start=True, stop=True)\
                        .then_inc(filled[b], 1)
                elif st.kind == "turn":
                    b, w, _ = st.bank
                    if st.diff:
                        pe.wait_ge(sem["combined"], st.combined)
                        src = comb[:, st.unit % 2, :]
                    else:
                        pe.wait_ge(sem["exped"], 2 * (st.maps[0] + 1))
                        src = prob[:, st.maps[0] % 4, :]
                    wait(pe, w)
                    for i in range(3):
                        last = turn(psum[b][:, i * P:(i + 1) * P], src[:, i * P:(i + 1) * P])
                    last.then_inc(filled[b], 1)
                elif st.kind == "value":
                    pe.wait_ge(sem[f"pt_made{st.uid % 2}"], st.pt)
                    pe.wait_ge(sem["evac_made"], st.needs)
                    if st.first:
                        wait(pe, st.banks[0][1])
                        wait(pe, st.banks[1][1])
                    v0, v1 = value_operand(st.group, st.unit, 0), value_operand(st.group, st.unit, 1)
                    n = v0.shape[-1]
                    cols = slice(st.unit * n, (st.unit + 1) * n)
                    w = pt[:, st.uid % 2, :]
                    m0 = nc.tensor.matmul(psum[4][:, cols], w[:, 0:P], v0, start=True, stop=True)
                    nc.tensor.matmul(psum[5][:, cols], w[:, P:2 * P], v0, start=True, stop=False)
                    m1 = nc.tensor.matmul(psum[5][:, cols], w[:, 2 * P:3 * P], v1, start=False, stop=True)
                    if st.last:
                        m0.then_inc(filled[4], 1)
                        m1.then_inc(filled[5], 1)
                    else:
                        m1.then_inc(sem["pv_done"], 1)
                elif st.kind == "compress":
                    slot = st.slab % RING
                    b, w, _ = st.bank
                    pe.wait_ge(lo_made[slot], st.slab // RING + 1)
                    pe.wait_ge(sem["xc_lo_made"], NG)
                    if st.half == 0:
                        wait(pe, w)
                    hi, lo = parts(whi[slot], 8, 256), parts(wlo[slot], 8, 256)
                    for j in range(8):
                        jj = 8 * st.half + j
                        nc.tensor.matmul(psum[b][:, 0:256], xcs[:, jj, :], hi[:, j, :], start=jj == 0, stop=False)
                        last = nc.tensor.matmul(psum[b][:, 0:256], xcs[:, jj, :], lo[:, j, :], start=False,
                                                stop=jj == 15)
                    if st.half:
                        last.then_inc(filled[b], 1)
                    else:
                        last.then_inc(sem["slab_used"], 1)
                elif st.kind == "hid_turn":
                    b, w, _ = st.bank
                    pe.wait_ge(sem["he_made"], st.kv + 1)
                    wait(pe, w)
                    rows = slice(64 * st.kv, 64 * st.kv + 64)
                    for c in range(2):
                        last = nc.tensor.matmul(psum[b][:, c * NG * NC:(c + 1) * NG * NC],
                                                he[rows, c * P:(c + 1) * P], fold[rows, :], start=True, stop=True)
                    last.then_inc(filled[b], 1)
                elif st.kind == "second":
                    b, w, _ = st.bank
                    pe.wait_ge(sem["gelu_out"], st.kv + 1)
                    wait(pe, w)
                    for c in range(2):
                        lhs = hk[:, c, :] if st.kv == 0 else hv[:, c].rearrange("p h n -> p (h n)")
                        m = lhs.shape[-1]
                        last = nc.tensor.matmul(psum[b][0:m, 0:HD], lhs, w2[:, st.kv, c, :],
                                                start=c == 0, stop=c == 1)
                    last.then_inc(filled[b], 1)
                elif st.kind == "kcmp":
                    b, w, _ = st.bank
                    pe.wait_ge(sem["roped"], st.roped)
                    wait(pe, w)
                    turn(psum[b][:, 0:NG * NC], kcn[:, :, :].rearrange("p u d -> p (u d)"), NG * NC)\
                        .then_inc(filled[b], 1)
                elif st.kind == "cscores":
                    pe.wait_ge(sem["t_made"], st.t_needed)
                    b, w, _ = st.bank
                    wait(pe, w)
                    for t in range(NT):
                        for j in range(NH // 2):
                            at = (t * NH + 2 * j) * NC
                            last = nc.tensor.matmul(psum[b][:, at:at + 2 * NC], qk[:, 0, j, t * P:(t + 1) * P],
                                                    kct[:, 2 * j // (NH // NG)].rearrange("p u n -> p (u n)"),
                                                    start=True, stop=True)
                    last.then_inc(filled[b], 1)
                elif st.kind == "cturn":
                    b, w, _ = st.bank
                    pe.wait_ge(sem["c_ready"], 1)
                    wait(pe, w)
                    for t in range(NT):
                        last = turn(psum[b][:, t * P:(t + 1) * P], cs[:, t].rearrange("p h n -> p (h n)"))
                    last.then_inc(filled[b], 1)
                elif st.kind == "cvalue":
                    pe.wait_ge(sem["pct_made"], 1)
                    pe.wait_ge(sem["vbd_made"], 1)
                    for t in range(NT):
                        b, w, _ = st.banks[t]
                        wait(pe, w)
                        nc.tensor.matmul(psum[b][:, :], pct[:, t, :], vbd[:, :, :].rearrange("p h d -> p (h d)"),
                                         start=True, stop=True).then_inc(filled[b], 1)
                elif st.kind == "ffn":
                    s0, g0, u0, base = st.s0, st.g0, st.u0, st.base
                    wait(pe, st.gate_wait)
                    gate_or_up(0, s0 % RING, s0 // RING + 1, None, None, st.x_needed - KT // 2)
                    pe.wait_ge(sem["diag_made"], st.n)
                    wait(pe, st.bank[1])
                    nc.tensor.matmul(psum[st.bank[0]][:, 0:SEQ], ones[:, :], dg.rearrange("p t n -> p (t n)"),
                                     start=True, stop=True).then_inc(filled[st.bank[0]], 1)
                    wait(pe, st.up_wait)
                    gate_or_up(1, (s0 + 1) % RING, (s0 + 1) // RING + 1, None, None)

                    def body(i, first):
                        gate_or_up(0, (s0 + 2) % RING, i + (s0 - 1) // RING + 1, sem["gate_scaled"], i + base)
                        gate_or_up(1, s0 % RING, i + s0 // RING + 1, sem["h_made"], i + base)
                        down((s0 + 1) % RING, i + (s0 + 1) // RING + 1, i + base, first, False)

                    for o_use in st.out:
                        wait(pe, o_use[1])
                    body(1, True)
                    with pe.Fori(2, NI) as i:
                        body(i, False)
                    down((s0 + 3 * NI - 1) % RING, (s0 + 3 * NI - 1) // RING + 1, base + NI, False, True)

        @block.scalar
        def _(act):
            A = nc.scalar.activation
            gain_loads = [
                (grow[0:16, :], t_in["attn_norm"].rearrange("l (k p) -> (l k) p", p=P)),
                (grow[16:32, :], t_in["ffn_norm"].rearrange("l (k p) -> (l k) p", p=P)),
                (grow[32:34, :], t_in["mla_q_norm"].rearrange("l (k p) -> (l k) p", p=P)),
                (grow[34:35, :], t_in["mla_kv_norm"]),
            ]
            for dst, src in gain_loads:
                act.dma_start(dst, src).then_inc(sem["gains_landed"], 16)

            def next_split(k):
                s = k + RING
                if s < n_slabs:
                    wait(act, slabs[k].released)
                    split_hi(act, s % RING, 16 * (s // RING + 1), slabs[s].n)

            for st in steps:
                if st.kind == "norm":
                    for j, (t, n) in enumerate(st.chunks):
                        if st.k == 0:
                            act.wait_ge(sem[f"x{t}_landed"], 16)
                        else:
                            act.wait_ge(sem["h_ready"], st.h_needed - 3 + j)
                        cols = slice(512 * n, 512 * (n + 1))
                        A(o[:, t, cols], h[:, t, cols], ACT.Square, accum_out=ssq[:, 2 * t + n:2 * t + n + 1])\
                            .then_inc(sem["ssq_made"], 1)
                    if st.k == 4:
                        act.wait_ge(sem["h_gained"], 2)
                        act.wait_ge(sem["rstd_made"], st.n)
                        A(h[:, 0, :], h[:, 0, :], ACT.Copy, scale=rstd[:, 0:1]).then_inc(sem["fin0_made"], 1)
                elif st.kind == "start":
                    act.wait_ge(filled[0], 1)
                    A(gains[:, :], psum[0][:, 0:35], ACT.Copy).then_inc(sem["gains_made"], 1)
                elif st.kind == "xt":
                    b = st.bank[0]
                    if st.n == 1:
                        act.wait_ge(sem["gains_made"], 1)
                    bank_filled(act, st.bank)
                    if st.gain is None:
                        A(xhi[:, st.chunks[0]:st.chunks[0] + 2, :].rearrange("p k n -> p (k n)"), psum[b][:, :],
                          ACT.Copy).then_inc(sem["xhi_made"], 1)
                    else:
                        for i, c in enumerate(st.chunks):
                            last = A(xhi[:, c, :], psum[b][:, i * SEQ:(i + 1) * SEQ], ACT.Copy,
                                     scale=gains[:, st.gain + c:st.gain + c + 1])
                        last.then_inc(sem["xhi_made"], 1)
                elif st.kind in ("proj", "up"):
                    if st.acc == "evac_made" and (st.kind == "up" or st.last):
                        if st.kind == "proj" and st.what == "ev_in" and st.group in (0, 1):
                            act.wait_ge(sem["t_made"], 2 * (st.group + 1))
                        bank_filled(act, st.bank)
                        act.wait_ge(sem["rstd_made"], st.ready)
                        col = {"uq": LATENT_NORMS, "ukv": LATENT_NORMS + NT}.get(st.what, LAYER_NORMS) + st.t
                        for dst, src in evac_copies(st.what, st.group if st.kind == "proj" else 0, st.t, st.bank[0],
                                                    0 if st.kind == "proj" else st.half):
                            last = A(dst, src, ACT.Copy, scale=rstd[:, col:col + 1])
                        last.then_inc(sem["evac_made"], 1)
                elif st.kind == "split_hi":
                    next_split(st.slab)
                elif st.kind in ("qkt", "kdt"):
                    bank_filled(act, st.bank)
                    A(t_dst(st), psum[st.bank[0]][:, :].rearrange("p (a n) -> p a n", a=2), ACT.Copy)\
                        .then_inc(sem["t_made"], 1)
                elif st.kind == "mqkt":
                    bank_filled(act, st.bank)
                    wait(act, st.free)
                    slot = mla_slot(st.head)
                    A(qk[0:MD, slot // 4, slot % 4:slot % 4 + 2, :],
                      psum[st.bank[0]][0:MD, :].rearrange("p (a n) -> p a n", a=2), ACT.Copy)\
                        .then_inc(sem["t_made"], 1)
                elif st.kind == "first_splits":
                    act.wait_ge(sem["half_landed"], 16)
                    A(whi[0][:, 0:SLAB // 2], raw[0][:, 0:SLAB // 2], ACT.Copy).then_inc(sem["half_hi_made"], 1)
                    act.wait_ge(landed[0], 16)
                    A(whi[0][:, SLAB // 2:], raw[0][:, SLAB // 2:], ACT.Copy).then_inc(sem["hi_made"], 1)
                    for s in range(1, RING):
                        split_hi(act, s, 16, slabs[s].n)
                elif st.kind == "tables":
                    act.wait_ge(filled[1], 1)
                    A(pet[:, :, :].rearrange("p a b -> p (a b)"), psum[1][:, 0:64], ACT.Copy)\
                        .then_inc(sem["pe_made"], 1)
                    act.wait_ge(sem["angles_made"], 1)
                    A(trig[:, :, :, :].rearrange("p a b c -> p (a b c)"),
                      red[:, :, :, :].rearrange("p a b c -> p (a b c)"), ACT.Sin).then_inc(sem["sin_made"], 1)
                    act.wait_ge(sem["lam_dots"], 1)
                    A(lam[:, 2:4], lam[:, 0:2], ACT.Exp).then_inc(sem["lam_exp"], 1)
                elif st.kind == "scores":
                    m = st.m
                    if m >= 4:
                        wait(act, prob_free[m - 4])
                    for t, cols in ((0, slice(0, P)), (1, slice(P, 3 * P))):
                        act.wait_ge(sem["masked"], 2 * m + t + 1)
                        A(prob[:, m % 4, cols], masked[:, m % 2, cols], ACT.Exp, bias=nmax[:, 2 * m + t:2 * m + t + 1],
                          scale=-1.0, accum_out=sums[:, 2 * m + t:2 * m + t + 1]).then_inc(sem["exped"], 1)
                elif st.kind == "turn" and st.diff:
                    bank_filled(act, st.bank)
                    wait(act, st.pv_before)
                    A(pt[:, st.uid % 2, :], psum[st.bank[0]][:, 0:SCORE_COLS], ACT.Copy)\
                        .then_inc(sem[f"pt_made{st.uid % 2}"], 1)
                elif st.kind == "blocks":
                    act.wait_ge(sem["xc_made"], st.kv + 1)
                    at = 64 * st.kv
                    A(xcs[:, :, at:at + NG * NC], xc[:, :, :, :].rearrange("p j g n -> p j (g n)"),
                      ACT.Copy).then_inc(sem["xch_made"], 1)
                elif st.kind == "compress":
                    if st.half:
                        bank_filled(act, st.bank)
                        rows = slice(64 * st.kv, 64 * st.kv + 64)
                        A(he[rows, :], psum[st.bank[0]][rows, 0:256], ACT.Copy).then_inc(sem["he_made"], 1)
                elif st.kind == "hid_turn":
                    bank_filled(act, st.bank)
                    if st.kv:
                        act.wait_ge(sem["gelu_out"], st.kv)
                    A(hid[:, :, :].rearrange("p c n -> p (c n)"), psum[st.bank[0]][:, 0:2 * NG * NC], ACT.Copy)\
                        .then_inc(sem["hid_read"], 1)
                elif st.kind == "gelu":
                    act.wait_ge(sem["gelu_in"], st.kv + 1)
                    A(hid3[:, :, :], hid2[:, :, :], ACT.Tanh, scale=float(np.sqrt(2 / np.pi)))\
                        .then_inc(sem["gelu_th"], 1)
                elif st.kind == "second":
                    if st.kv == 0:
                        bank_filled(act, st.bank)
                        src = psum[st.bank[0]][0:NG * NC, 0:HD].unsqueeze(1).broadcast_to([NG * NC, 2, HD])
                        A(kcn[:, :, :], src, ACT.Copy).then_inc(sem["kcn_made"], 1)
                elif st.kind == "kcmp":
                    bank_filled(act, st.bank)
                    act.wait_ge(sem["consts_made"], 1)
                    for u in range(2):
                        rows = slice(64 * u, 64 * u + 64)
                        last = A(kct[rows, :, u, :],
                                 psum[st.bank[0]][rows, 0:NG * NC].rearrange("p (g n) -> p g n", g=NG), ACT.Copy)
                    last.then_inc(sem["t_made"], 1)
                elif st.kind == "cscores":
                    act.wait_ge(sem["c_centred"], 1)
                    flat_cs = cs[:, :, :, :].rearrange("p t h n -> p (t h n)")
                    A(flat_cs, flat_cs,
                      ACT.Exp, scale=HD ** -0.5).then_inc(sem["c_exped"], 1)
                elif st.kind == "cturn":
                    bank_filled(act, st.bank)
                    A(pct[:, :, :].rearrange("p t n -> p (t n)"), psum[st.bank[0]][:, 0:NT * P], ACT.Copy)\
                        .then_inc(sem["pct_made"], 1)
                elif st.kind == "gates":
                    act.wait_ge(sem["gate_in"], 1)
                    A(gate[:, :, :], gate[:, :, :], ACT.Tanh, scale=0.5).then_inc(sem["gate_th"], 1)
                elif st.kind == "out" and st.group == "diff":
                    act.wait_ge(sem["o_banks_read"], st.read)
                    junk = [comb[:, 0, :], comb[:, 1, :], otmp[:, :]]
                    for j in range(NT * NDH):
                        v = o[:, j // NDH, 512 + (j % NDH) * P:512 + (j % NDH + 1) * P]
                        last = A(junk[j // 3][:, (j % 3) * P:(j % 3 + 1) * P], v, ACT.Square,
                                 accum_out=ssq[:, j:j + 1])
                    last.then_inc(sem["head_squares"], 1)
                elif st.kind == "ffn":
                    s0, g0, u0, base = st.s0, st.g0, st.u0, st.base

                    bank_filled(act, st.bank)
                    A(rrow, psum[st.bank[0]][:, 0:SEQ], ACT.Copy).then_inc(sem["row_made"], 1)

                    def tanh(i):
                        act.wait_ge(sem["gate_scaled"], i + (base + 1))
                        if not isinstance(i, int) or base + i > 0:
                            act.wait_ge(sem["gated"], i + base)
                        A(th[:, :], gr[:, :], ACT.Tanh, scale=0.5).then_inc(sem["tanh_made"], 1)

                    def hidden(i):
                        act.wait_ge(sem["h_made"], i + (base + 1))
                        A(hhi[:, :], hf[:, :], ACT.Copy).then_inc(sem["hhi_made"], 1)

                    def body(i, more=True):
                        r = i * 16
                        q = [(s0 - 1 + RING + j) for j in range(3)]
                        tanh(i)
                        if more or s0 - 1 + 3 * i + RING < n_slabs:
                            split_hi(act, q[0] % RING, r + 16 * (q[0] // RING + 1), SLAB)
                        if more or s0 + 3 * i + RING < n_slabs:
                            act.wait_ge(filled[1], i + (u0 + 1))
                            split_hi(act, q[1] % RING, r + 16 * (q[1] // RING + 1), SLAB)
                        act.wait_ge(sem["down_done"], down_at + i)
                        hidden(i)
                        if more or s0 + 1 + 3 * i + RING < n_slabs:
                            split_hi(act, q[2] % RING, r + 16 * (q[2] // RING + 1), SLAB)

                    down_at = st.down_base
                    tanh(0)
                    split_hi(act, (s0 + 3) % RING, 16 * ((s0 + 3) // RING + 1), SLAB)
                    act.wait_ge(filled[1], u0 + 1)
                    split_hi(act, (s0 + 4) % RING, 16 * ((s0 + 4) // RING + 1), SLAB)
                    hidden(0)
                    body(1)
                    with act.Fori(2, NI - 1) as i:
                        body(i)
                    body(NI - 1, more=False)

        @block.vector
        def _(dve):
            V = nc.vector
            step = [0]

            def link(ins):
                step[0] += 1
                ins.then_inc(sem["dve_step"], 1)
                dve.wait_ge(sem["dve_step"], step[0])

            def next_split(k):
                s = k + RING
                if s < n_slabs and not pool_splits(s):
                    split_lo(dve, s % RING, s + 1, slabs[s].n)

            def to_root(src, scales):
                for c0, c1, scale in scales:
                    last = V.tensor_scalar(msq[:, c0:c1], src[:, c0:c1], scale, EPS, ALU.mult, ALU.add)
                last.then_inc(sem["msq_made"], 1)

            def rope(x, cos, sin, w, n):
                if n > 1:
                    dve.wait_ge(sem["roped"], n - 1)
                r = w // 2
                shape = list(x.shape)
                a = rope_a[0:shape[0], 0:shape[1], 0:shape[2], 0:w]
                b = rope_b[0:shape[0], 0:shape[1], 0:shape[2], 0:w]

                def per_head(t):
                    return t.unsqueeze(2).broadcast_to(shape[:3] + [t.shape[-1]])

                V.tensor_tensor(a, x, per_head(cos), ALU.mult)
                V.tensor_tensor(b[:, :, :, 0:r], x[:, :, :, r:w], per_head(sin[:, :, 0:r]), ALU.mult)
                link(V.tensor_tensor(b[:, :, :, r:w], x[:, :, :, 0:r], per_head(sin[:, :, r:w]), ALU.mult))
                V.tensor_tensor(x, a, b, ALU.add).then_inc(sem["roped"], 1)

            for st in steps:
                if st.kind == "norm":
                    if st.k == 4:
                        for n in range(2):
                            cols = slice(512 * n, 512 * (n + 1))
                            dve.wait_ge(sem["ssq_made"], 4 * st.k + n + 1)
                            V.tensor_tensor(h[:, 0, cols], h[:, 0, cols], gfin[:, cols], ALU.mult)\
                                .then_inc(sem["h_gained"], 1)
                    dve.wait_ge(sem["ssq_made"], 4 * (st.k + 1))
                    v = ssq[:, 0:4].rearrange("p (t n) -> p t n", n=2)
                    link(V.tensor_tensor(msq[:, 0:2], v[:, :, 0], v[:, :, 1], ALU.add))
                    to_root(msq, [(0, NT, 1.0 / D)])
                    if st.k % 2 or st.k == 4:
                        dve.wait_ge(sem["rstd_made"], st.n)
                    if st.k % 2:
                        for t in range(NT):
                            last = V.tensor_scalar(dg[:, t, :], ident[:, :], rstd[:, t:t + 1], None, ALU.mult)
                        last.then_inc(sem["diag_made"], 1)
                    elif st.k == 4:
                        V.scalar_tensor_tensor(h[:, 1, :], h[:, 1, :], rstd[:, 1:2], gfin[:, :], ALU.mult, ALU.mult)\
                            .then_inc(sem["fin1_made"], 1)
                elif st.kind == "xt":
                    b = st.bank[0]
                    dve.wait_ge(sem["xhi_made"], st.n)
                    if st.gain is None:
                        c = st.chunks[0]
                        V.tensor_tensor(xlo[:, c:c + 2, :].rearrange("p k n -> p (k n)"), psum[b][:, :],
                                        xhi[:, c:c + 2, :].rearrange("p k n -> p (k n)").bitcast(F32),
                                        ALU.subtract).then_inc(sem["xlo_made"], 1)
                    else:
                        for i, c in enumerate(st.chunks):
                            last = V.scalar_tensor_tensor(
                                xlo[:, c, :], psum[b][:, i * SEQ:(i + 1) * SEQ],
                                gains[:, st.gain + c:st.gain + c + 1], xhi[:, c, :].bitcast(F32), ALU.mult,
                                ALU.subtract)
                        last.then_inc(sem["xlo_made"], 1)
                elif st.kind == "first_splits":
                    for cols, made, signal in ((slice(0, SLAB // 2), "half_hi_made", sem["half_lo_made"]),
                                               (slice(SLAB // 2, SLAB), "hi_made", lo_made[0])):
                        dve.wait_ge(sem[made], 1)
                        V.tensor_tensor(wlo[0][:, cols], raw[0][:, cols], whi[0][:, cols].bitcast(F32),
                                        ALU.subtract).then_inc(signal, 1)
                    for s in range(1, RING):
                        split_lo(dve, s, s + 1, slabs[s].n)
                elif st.kind == "tables":
                    dve.wait_ge(sem["small_landed"], 16 * n_small)
                    dve.wait_ge(sem["consts_made"], 1)
                    V.tensor_reduce(fold[:, :], ident[:, :].rearrange("p (k n) -> p n k", n=NG * NC), AX.X, ALU.add)
                    link(V.tensor_copy(posf[:, :], posi[:, :]))
                    link(V.tensor_tensor(ang[:, :, :], posf[:, :].unsqueeze(2).broadcast_to([P, 3, 16]),
                                         invf[:, :].unsqueeze(1).broadcast_to([P, 3, 16]), ALU.mult))
                    link(V.tensor_scalar(turns[:, :, :], ang[:, :, :], 1.0 / (2 * np.pi), ROUND, ALU.mult, ALU.add))
                    link(V.tensor_scalar(turns[:, :, :], turns[:, :, :], ROUND, None, ALU.subtract))
                    for part in TWO_PI_PARTS:
                        link(V.scalar_tensor_tensor(ang[:, :, :], turns[:, :, :], -part, ang[:, :, :], ALU.mult,
                                                    ALU.add))
                    link(V.tensor_scalar(red[:, 0], ang[:, :, :], 3.1415925, -3.1415925, ALU.min, ALU.max))
                    link(V.scalar_tensor_tensor(ang[:, :, :], red[:, 0], -1.0, red[:, 0], ALU.mult, ALU.max))
                    V.tensor_scalar(red[:, 1], ang[:, :, :], -1.0, PI / 2, ALU.mult, ALU.add)\
                        .then_inc(sem["angles_made"], 1)
                    for j in range(2):
                        last = V.tensor_tensor_reduce(otmp[:, j * HD:(j + 1) * HD], lqk[:, 2 * j], lqk[:, 2 * j + 1],
                                                      1.0, 0.0, ALU.mult, ALU.add, lam[:, j:j + 1])
                    last.then_inc(sem["lam_dots"], 1)
                    V.tensor_scalar(subln[:, :], subln[:, :], 1.0 - LAMBDA_INIT, None, ALU.mult)
                    dve.wait_ge(sem["sin_made"], 1)
                    for cc, sn, w, every in ((cc8, sn8, 16, 2), (cc16, sn16, 32, 1)):
                        r = w // 2
                        s_, c_ = trig[:, 0, :, 0:16:every], trig[:, 1, :, 0:16:every]
                        V.tensor_copy(cc[:, :, 0:r], c_)
                        V.tensor_copy(cc[:, :, r:w], c_)
                        V.tensor_scalar(sn[:, :, 0:r], s_, -1.0, None, ALU.mult)
                        link(V.tensor_copy(sn[:, :, r:w], s_))
                    dve.wait_ge(sem["lam_exp"], 1)
                    link(V.scalar_tensor_tensor(lam[:, 0:1], lam[:, 2:3], -1.0, lam[:, 3:4], ALU.mult, ALU.add))
                    link(V.tensor_scalar(lam[:, 0:1], lam[:, 0:1], -LAMBDA_INIT, None, ALU.add))
                elif st.kind in ("proj", "up"):
                    if st.kind == "proj" and st.acc == "h_ready" and st.last:
                        bank_filled(dve, st.bank)
                        if st.h_needed:
                            dve.wait_ge(sem["h_ready"], st.h_needed)
                        cols = slice(st.group * 512, (st.group + 1) * 512)
                        V.tensor_tensor(h[:, st.t, cols], psum[st.bank[0]][:, :], h[:, st.t, cols], ALU.add)\
                            .then_inc(sem["h_ready"], 1)
                elif st.kind == "split_lo":
                    next_split(st.slab)
                elif st.kind == "rope":
                    if st.what == "kcmp":
                        dve.wait_ge(sem["kcn_made"], 1)
                    else:
                        dve.wait_ge(sem["evac_made"], st.evac)
                    if st.what == "kcmp":
                        rope(kcn[:, :, 0:16].unsqueeze(1), cc8[0:NG * NC, 2:3, :], sn8[0:NG * NC, 2:3, :], 16, st.n)
                    elif st.what == "nat":
                        v = nat[:, st.buf].rearrange("p t (h d) -> p t h d", d=HD)
                        rope(v[:, :, :, 0:16], cc8[:, 0:NT, :], sn8[:, 0:NT, :], 16, st.n)
                    elif st.what in ("kslc", "kwin"):
                        w = 0 if st.what == "kslc" else 1
                        v = nat2[:, :, w].rearrange("p t g u d -> p t (g u) d")
                        rope(v[:, :, :, 0:16], cc8[:, 0:NT, :], sn8[:, 0:NT, :], 16, st.n)
                    elif st.what == "kpe":
                        rope(kpe[:, :, :].unsqueeze(2), cc16[:, 0:NT, :], sn16[:, 0:NT, :], RO, st.n)
                        dve.wait_ge(sem["roped"], st.n)
                        dve.wait_ge(sem["t_made"], st.t_needed)
                        for t in range(NT):
                            last = V.tensor_copy(km[:, t, :, NOPE:], kpe[:, t].unsqueeze(1).broadcast_to([P, NH, RO]))
                        last.then_inc(sem["kpe_spread"], 1)
                    else:
                        rope(qm[:, :, :, NOPE:], cc16[:, 0:NT, :], sn16[:, 0:NT, :], RO, st.n)
                elif st.kind == "scores":
                    m, b = st.m, psum[st.bank[0]]
                    bank_filled(dve, st.bank)
                    if m >= 2:
                        dve.wait_ge(sem["exped"], 2 * (m - 1))
                    scale = score_operands(st.group, st.unit, st.part)[2]
                    for t, cols in ((0, slice(0, P)), (1, slice(P, 3 * P))):
                        V.tensor_tensor_reduce(masked[:, m % 2, cols], b[:, cols], tri[:, cols], -scale, 3e38, ALU.add,
                                               ALU.min, nmax[:, 2 * m + t:2 * m + t + 1]).then_inc(sem["masked"], 1)
                elif st.kind == "combine":
                    m0, m1 = st.maps
                    dve.wait_ge(sem["exped"], 2 * (m1 + 1))
                    c = slice(2 * m0, 2 * m0 + 4)
                    link(V.tensor_scalar(rinv[:, c], sums[:, c], 1e-30, None, ALU.max))
                    link(V.reciprocal(rinv[:, c], rinv[:, c]))
                    link(V.tensor_scalar(rinv[:, 2 * m1:2 * m1 + 2], rinv[:, 2 * m1:2 * m1 + 2], lam[:, 0:1], None,
                                         ALU.mult))
                    if st.unit >= 2:
                        wait(dve, comb_free[st.unit - 2])
                    for t, cols in ((0, slice(0, P)), (1, slice(P, 3 * P))):
                        ins = V.tensor_scalar(comb[:, st.unit % 2, cols], prob[:, m0 % 4, cols],
                                              rinv[:, 2 * m0 + t:2 * m0 + t + 1], None, ALU.mult)
                    link(ins)
                    for t, cols in ((0, slice(0, P)), (1, slice(P, 3 * P))):
                        ins = V.scalar_tensor_tensor(comb[:, st.unit % 2, cols], prob[:, m1 % 4, cols],
                                                     rinv[:, 2 * m1 + t:2 * m1 + t + 1],
                                                     comb[:, st.unit % 2, cols], ALU.mult, ALU.add)
                    ins.then_inc(sem["combined"], 1)
                elif st.kind == "turn":
                    if not st.diff:
                        bank_filled(dve, st.bank)
                        wait(dve, st.pv_before)
                        V.tensor_copy(pt[:, st.uid % 2, :], psum[st.bank[0]][:, 0:SCORE_COLS])\
                            .then_inc(sem[f"pt_made{st.uid % 2}"], 1)
                elif st.kind == "out":
                    bank_filled(dve, st.banks[0])
                    bank_filled(dve, st.banks[1])
                    if st.group == "diff":
                        ob = o[:, :, 512:1024]
                        for t in range(NT):
                            last = V.tensor_copy(ob[:, t, :], psum[st.banks[t][0]][:, :])
                            last.then_inc(sem["o_banks_read"], 1)
                        continue
                    if st.group == "cmp":
                        src = csum[:, :].rearrange("p (t h) -> p t h", t=NT)
                    else:
                        dve.wait_ge(sem["exped"], 2 * (st.maps[-1] + 1))
                        c = slice(2 * st.maps[0], 2 * st.maps[-1] + 2)
                        src = sums[:, c].rearrange("p (h t) -> p t h", t=NT)
                    link(V.tensor_scalar(coef[:, :, :], src, 1e-30, None, ALU.max))
                    link(V.reciprocal(coef[:, :, :], coef[:, :, :]))
                    branch = {"cmp": 0, "slc": 1, "win": 2}.get(st.group)
                    if branch is not None:
                        dve.wait_ge(sem["gates_made"], 1)
                        gv = gate[:, :, :].rearrange("p t (h b) -> p t h b", b=3)[:, :, :, branch]
                        link(V.tensor_tensor(coef[:, :, :], coef[:, :, :], gv, ALU.mult))
                    lo = 512 if st.group == "mla" else 0
                    for t in range(NT):
                        v = psum[st.banks[t][0]][:, :].rearrange("p (h d) -> p h d", d=HD)
                        c = coef[:, t].unsqueeze(2).broadcast_to([P, NH, HD])
                        if st.group in ("slc", "cmp"):
                            V.tensor_tensor(otmp[:, :].rearrange("p (h d) -> p h d", d=HD), v, c, ALU.mult)\
                                .then_inc(sem["o_banks_read"], 1)
                            dve.wait_ge(sem["o_banks_read"], st.read - NT + t + 1)
                            add = V.tensor_tensor(o[:, t, 0:512], o[:, t, 0:512], otmp[:, :], ALU.add)
                            if st.group == "cmp" and t == NT - 1:
                                add.then_inc(sem["o_ready"], 1)
                            else:
                                link(add)
                        else:
                            V.tensor_tensor(o[:, t, lo:lo + 512].rearrange("p (h d) -> p h d", d=HD), v, c, ALU.mult)\
                                .then_inc(sem["o_banks_read"], 1)
                    dve.wait_ge(sem["o_banks_read"], st.read)
                elif st.kind == "head_norm":
                    dve.wait_ge(sem["rstd_made"], st.n)
                    for j in range(NT * NDH):
                        v = o[:, j // NDH, 512 + (j % NDH) * P:512 + (j % NDH + 1) * P]
                        last = V.scalar_tensor_tensor(v, v, rstd[:, j:j + 1], subln[:, :], ALU.mult, ALU.mult)
                    last.then_inc(sem["o_ready"], 1)
                elif st.kind == "blocks":
                    b = psum[st.bank[0]]
                    bank_filled(dve, st.bank)
                    if st.kv == 0:
                        dve.wait_ge(sem["gains_made"], 1)
                        dve.wait_ge(sem["pe_made"], 1)
                    else:
                        dve.wait_ge(sem["xch_made"], 1)
                        dve.wait_ge(sem["xc_lo_made"], 1)
                    v = b[:, :].rearrange("p (g n s) -> p s g n", g=NG, s=16)
                    for par in range(2):
                        rows = slice(64 * par, 64 * par + 64)
                        for late in range(2):
                            pe_cols = pet[rows, st.kv, 16 * late + par:16 * late + 16:2]
                            last = V.tensor_tensor(
                                xc[rows, 8 * late:8 * late + 8, :, 0:NCMP], v[rows, par:16:2, :, late:late + NCMP],
                                pe_cols.unsqueeze(2).unsqueeze(3).broadcast_to([64, 8, NG, NCMP]), ALU.add)
                    last.then_inc(sem["xc_made"], 1)
                    dve.wait_ge(sem["xch_made"], st.kv + 1)
                    dve.wait_ge(sem["xc_made"], st.kv + 1)
                    at = 64 * st.kv
                    V.tensor_tensor(xcs[:, :, at + 32:at + 64], xc[:, :, :, :].rearrange("p j g n -> p j (g n)"),
                                    xcs[:, :, at:at + 32].bitcast(F32), ALU.subtract)\
                        .then_inc(sem["xc_lo_made"], 1)
                elif st.kind == "gelu":
                    dve.wait_ge(sem["hid_read"], st.hid)
                    link(V.tensor_tensor(hid2[:, :, :], hid[:, :, :], hid[:, :, :], ALU.mult))
                    link(V.tensor_scalar(hid2[:, :, :], hid2[:, :, :], 0.044715, 1.0, ALU.mult, ALU.add))
                    V.tensor_tensor(hid2[:, :, :], hid2[:, :, :], hid[:, :, :], ALU.mult).then_inc(sem["gelu_in"], 1)
                    dve.wait_ge(sem["gelu_th"], st.kv + 1)
                    link(V.scalar_tensor_tensor(hid3[:, :, :], hid3[:, :, :], 1.0, hid[:, :, :], ALU.add, ALU.mult))
                    if st.kv == 0:
                        V.tensor_scalar(hk[:, :, :], hid3[:, :, :], 0.5, None, ALU.mult).then_inc(sem["gelu_out"], 1)
                    else:
                        v = hid3[:, :, :].rearrange("p c (g n) -> p (c g) n", g=NG).unsqueeze(2)
                        V.tensor_scalar(hv[:, :, :, :].rearrange("p c (g r) n -> p (c g) r n", g=NG),
                                        v.broadcast_to([P, 2 * NG, NH // NG, NC]), 0.5, None, ALU.mult)\
                            .then_inc(sem["gelu_out"], 1)
                elif st.kind == "second":
                    if st.kv:
                        bank_filled(dve, st.bank)
                        src = psum[st.bank[0]][:, 0:HD].unsqueeze(1).broadcast_to([P, NH, HD])
                        V.tensor_tensor(vbd[:, :, :], src, bdm[:, :].unsqueeze(2).broadcast_to([P, NH, HD]), ALU.mult)\
                            .then_inc(sem["vbd_made"], 1)
                elif st.kind == "cscores":
                    bank_filled(dve, st.bank)
                    v = psum[st.bank[0]][:, 0:NT * NH * NC].rearrange("p (t h n) -> p t h n", t=NT, n=NC)
                    V.tensor_tensor(cs[:, :, :, :], v, cmask[:, :, :].unsqueeze(2).broadcast_to([P, NT, NH, NC]),
                                    ALU.add).then_inc(sem["c_masked"], 1)
                    dve.wait_ge(sem["c_masked"], 1)
                    rows = cs[:, :, :, :].rearrange("p t h n -> p (t h) n")
                    link(V.tensor_reduce(cmx[:, :], rows, AX.X, ALU.max))
                    V.tensor_tensor(rows, rows, cmx[:, :].unsqueeze(2).broadcast_to([P, NT * NH, NC]), ALU.subtract)\
                        .then_inc(sem["c_centred"], 1)
                    dve.wait_ge(sem["c_exped"], 1)
                    link(V.tensor_tensor(cs[:, :, :, :], cs[:, :, :, :],
                                         cvalid[:, :, :].unsqueeze(2).broadcast_to([P, NT, NH, NC]), ALU.mult))
                    V.tensor_reduce(csum[:, :], rows, AX.X, ALU.add).then_inc(sem["c_ready"], 1)
                elif st.kind == "gates":
                    dve.wait_ge(sem["evac_made"], st.evac)
                    V.tensor_tensor(gate[:, :, :], gate[:, :, :],
                                    gateb[:, :].unsqueeze(1).broadcast_to([P, NT, NH * 3]), ALU.add)\
                        .then_inc(sem["gate_in"], 1)
                    dve.wait_ge(sem["gate_th"], 1)
                    V.tensor_scalar(gate[:, :, :], gate[:, :, :], 1.0, 0.5, ALU.add, ALU.mult)\
                        .then_inc(sem["gates_made"], 1)
                elif st.kind == "latent_norm":
                    dve.wait_ge(sem["evac_made"], st.evac)
                    for j, (lo, hi) in enumerate(((0, LQ), (LQ, LQ + LKV))):
                        for t in range(NT):
                            last = V.tensor_tensor_reduce(lat_squares[:, t, lo:hi], lat[:, t, lo:hi], lat[:, t, lo:hi],
                                                          1.0, 0.0, ALU.mult, ALU.add,
                                                          ssq[:, 2 * j + t:2 * j + t + 1])
                    link(last)
                    to_root(ssq, [(0, NT, 1.0 / LQ), (NT, 2 * NT, 1.0 / LKV)])
                elif st.kind == "ffn":
                    s0, g0, u0, base = st.s0, st.g0, st.u0, st.base

                    dve.wait_ge(sem["row_made"], st.n)
                    row = rrow.unsqueeze(1).broadcast_to([P, 2, SEQ])

                    def scaled(i):
                        dve.wait_ge(filled[0], i + (g0 + 1))
                        V.tensor_tensor(gr[:, :].rearrange("p (c n) -> p c n", c=2),
                                        psum[0][:, :].rearrange("p (c n) -> p c n", c=2), row, ALU.mult)\
                            .then_inc(sem["gate_scaled"], 1)

                    def gated(i):
                        dve.wait_ge(sem["tanh_made"], i + (base + 1))
                        V.scalar_tensor_tensor(ga[:, :], th[:, :], 1.0, gr[:, :], ALU.add, ALU.mult)\
                            .then_inc(sem["gated"], 1)

                    def hidden(i):
                        dve.wait_ge(filled[1], i + (u0 + 1))
                        dve.wait_ge(sem["gated"], i + (base + 1))
                        V.scalar_tensor_tensor(hf[:, :], ga[:, :], 0.5, psum[1][:, :], ALU.mult, ALU.mult)\
                            .then_inc(sem["h_made"], 1)

                    def hidden_lo(i):
                        dve.wait_ge(sem["hhi_made"], i + (base + 1))
                        V.tensor_tensor(hlo[:, :], hf[:, :], hhi[:, :].bitcast(F32), ALU.subtract)\
                            .then_inc(sem["hlo_made"], 1)

                    def body(i, more=True):
                        r = i * RING
                        scaled(i)
                        if more or s0 - 1 + 3 * i + RING < n_slabs:
                            split_lo(dve, (s0 + 2) % RING, r + (s0 - 1 + RING + 1), SLAB)
                        gated(i)
                        hidden(i)
                        if more or s0 + 3 * i + RING < n_slabs:
                            split_lo(dve, (s0 + 3) % RING, r + (s0 + RING + 1), SLAB)
                        hidden_lo(i)
                        if more or s0 + 1 + 3 * i + RING < n_slabs:
                            split_lo(dve, (s0 + 4) % RING, r + (s0 + 1 + RING + 1), SLAB)

                    scaled(0)
                    split_lo(dve, s0 % RING, s0 + 4, SLAB)
                    gated(0)
                    hidden(0)
                    split_lo(dve, (s0 + 1) % RING, s0 + 5, SLAB)
                    hidden_lo(0)
                    body(1)
                    with dve.Fori(2, NI - 1) as i:
                        body(i)
                    body(NI - 1, more=False)
                    for t in range(NT):
                        for n in range(2):
                            use = st.out[2 * t + n]
                            bank_filled(dve, use)
                            cols = slice(n * 512, (n + 1) * 512)
                            V.scalar_tensor_tensor(h[:, t, cols], psum[use[0]][:, :], rstd[:, t:t + 1], h[:, t, cols],
                                                   ALU.mult, ALU.add).then_inc(sem["h_ready"], 1)


_INS = ["x", "positions", "attn_norm", "ffn_norm", "final_norm", "ffn_w_gate", "ffn_w_up", "ffn_w_down", "ev_w_in",
        "ev_w_out", "diff_lambda_q1", "diff_lambda_k1", "diff_lambda_q2", "diff_lambda_k2", "diff_subln", "od_w_in",
        "od_w_out", "nsa_gate_b", "nsa_pe_k", "nsa_pe_v", "nsa_k_w1", "nsa_k_w2", "nsa_v_w1", "nsa_v_w2",
        "mla_q_norm", "mla_w_uq", "mla_kv_norm", "mla_w_ukv"]


def kernel(**inputs):
    import concourse.bacc as bacc
    from concourse.bass_utils import run_bass_kernel_spmd

    nc = bacc.Bacc("TRN2", target_bir_lowering=False, num_devices=1)
    arrays, aps = {}, {}
    for name in _INS:
        a = np.ascontiguousarray(inputs[name])
        arrays[f"in_{name}"] = a
        aps[name] = nc.dram_tensor(f"in_{name}", a.shape, mybir.dt.from_np(a.dtype), kind="ExternalInput").ap()
    out = nc.dram_tensor("out", (1, SEQ, D), F32, kind="ExternalOutput").ap()
    build(nc, aps, out)
    r = run_bass_kernel_spmd(nc, [arrays], core_ids=[0])
    return r.results[0]["out"]
```
